# Optimizing a Trainium2 kernel written in Bass

```python
import jax, jax.numpy as jnp
from jax import lax
import numpy as np

D_MODEL = 1024
BATCH = 1
SEQ = 256
DEPTH = 2
DEC_BATCH = 8
DEC_SEQ = 8
PAST_LEN = 2048
PAGE_SIZE = 128

PLE_DIM = 256
W_POOL = 512
POOL_WINDOWS = (2, 4, 8, 16)
N_POOL_GROUPS = 4
POOL_GROUP = W_POOL // N_POOL_GROUPS
POOL_BUF = max(POOL_WINDOWS) - 1
W_SCONV = 512
SCONV_K = 3
W_CCONV = 512
CCONV_K = 31
D_FF = 2816
N_BRANCH = 3
IN_COLS = W_POOL + 3 * W_SCONV + 2 * W_CCONV + N_BRANCH * D_MODEL
EPS = 1e-6

kernel_name = "hybrid_pool_shortconv_conformer_decoder_step"

def rmsnorm(x, g):
    xf = x.astype(jnp.float32)
    y = xf * lax.rsqrt(jnp.mean(xf * xf, axis=-1, keepdims=True) + EPS)
    return (y * g.astype(jnp.float32)).astype(x.dtype)

def layernorm(x, g, b):
    xf = x.astype(jnp.float32)
    mu = jnp.mean(xf, axis=-1, keepdims=True)
    xc = xf - mu
    y = xc * lax.rsqrt(jnp.mean(xc * xc, axis=-1, keepdims=True) + EPS)
    return (y * g.astype(jnp.float32) + b.astype(jnp.float32)).astype(x.dtype)

def swiglu(x, wg, wu, wd):
    return (jax.nn.silu(x @ wg) * (x @ wu)) @ wd

def causal_dwconv(buf, x, w):
    xp = jnp.concatenate([buf.astype(x.dtype), x], axis=1)
    c = x.shape[-1]
    out = lax.conv_general_dilated(xp, w[:, None, :].astype(x.dtype), window_strides=(1,), padding='VALID',
                                   dimension_numbers=('NWC', 'WIO', 'NWC'), feature_group_count=c)
    k = w.shape[0]
    return out, xp[:, xp.shape[1] - (k - 1):]

def pool_mixer(buf, a, pos0, pool_w, pool_scale):
    n, l, _ = a.shape
    ap = jnp.concatenate([buf.astype(a.dtype), a], axis=1)
    cs = jnp.pad(jnp.cumsum(ap.astype(jnp.float32), axis=1), ((0, 0), (1, 0), (0, 0)))
    pos = pos0 + jnp.arange(l)
    means = []
    for gi, w in enumerate(POOL_WINDOWS):
        sl = slice(gi * POOL_GROUP, (gi + 1) * POOL_GROUP)
        s = cs[:, POOL_BUF + 1:POOL_BUF + 1 + l, sl] - cs[:, POOL_BUF + 1 - w:POOL_BUF + 1 - w + l, sl]
        cnt = jnp.minimum(w, pos + 1).astype(jnp.float32)
        means.append(s / cnt[None, :, None])
    m = (jnp.concatenate(means, axis=-1) - a.astype(jnp.float32)).astype(a.dtype)
    m = m.reshape(n, l, N_POOL_GROUPS, POOL_GROUP)
    y = jnp.einsum('blgc,gcd->blgd', m, pool_w).reshape(n, l, W_POOL)
    return y * pool_scale, ap[:, ap.shape[1] - POOL_BUF:]

def mixer(u, bpool, bsc, bcf, pos0, P, i):
    n, l, _ = u.shape
    z = u @ P['w_in'][i]
    o = 0
    a = z[..., o:o + W_POOL]; o += W_POOL
    v = z[..., o:o + W_SCONV]; o += W_SCONV
    bg = z[..., o:o + W_SCONV]; o += W_SCONV
    cg = z[..., o:o + W_SCONV]; o += W_SCONV
    ga = z[..., o:o + W_CCONV]; o += W_CCONV
    gg = z[..., o:o + W_CCONV]; o += W_CCONV
    gates = jax.nn.sigmoid(z[..., o:].reshape(n, l, N_BRANCH, D_MODEL))
    ya, nb_pool = pool_mixer(bpool, a, pos0, P['pool_w'][i], P['pool_scale'][i])
    cv, nb_sc = causal_dwconv(bsc, cg * v, P['sc_conv'][i])
    yb = bg * cv
    glu = ga * jax.nn.sigmoid(gg)
    cc, nb_cf = causal_dwconv(bcf, glu, P['cf_conv'][i])
    yc = jax.nn.silu(layernorm(cc + P['cf_conv_b'][i], P['cf_ln_g'][i], P['cf_ln_b'][i]))
    m = (gates[:, :, 0] * (ya @ P['w_pool_out'][i])
         + gates[:, :, 1] * (yb @ P['w_sc_out'][i])
         + gates[:, :, 2] * (yc @ P['w_cf_out'][i]))
    return m @ P['w_o'][i], nb_pool, nb_sc, nb_cf

def trunk(x, p, bpool, bsc, bcf, pos0, P):
    h = x
    npool, nsc, ncf = [], [], []
    for i in range(DEPTH):
        f = swiglu(rmsnorm(h, P['g_f1_pre'][i]), P['w_f1_gate'][i], P['w_f1_up'][i], P['w_f1_down'][i])
        h = h + 0.5 * rmsnorm(f, P['g_f1_post'][i])
        mo, a1, a2, a3 = mixer(rmsnorm(h, P['g_mix_pre'][i]), bpool[i], bsc[i], bcf[i], pos0, P, i)
        h = h + rmsnorm(mo, P['g_mix_post'][i])
        f = swiglu(rmsnorm(h, P['g_f2_pre'][i]), P['w_f2_gate'][i], P['w_f2_up'][i], P['w_f2_down'][i])
        h = h + 0.5 * rmsnorm(f, P['g_f2_post'][i])
        gate = jax.nn.sigmoid(rmsnorm(h, P['g_ple_pre'][i]) @ P['w_ple_gate'][i])
        h = h + rmsnorm((p[i] @ P['w_ple_proj'][i]) * gate, P['g_ple_post'][i])
        npool.append(a1); nsc.append(a2); ncf.append(a3)
    return rmsnorm(h, P['g_final']), jnp.stack(npool), jnp.stack(nsc), jnp.stack(ncf)

def setup_inputs(seed: int = 0) -> dict:
    key = jax.random.key(seed)
    ks = iter(jax.random.split(key, 64))
    f32 = jnp.float32

    def nrm(shape, scale=1.0):
        return jax.random.normal(next(ks), shape, f32) * scale

    def gain(shape):
        return 1.0 + 0.05 * jax.random.normal(next(ks), shape, f32)

    d = {}
    d['x_prompt'] = nrm((BATCH, SEQ, D_MODEL))
    d['x_sample'] = nrm((DEC_BATCH, DEC_SEQ, D_MODEL))
    d['p_prompt'] = nrm((DEPTH, BATCH, SEQ, PLE_DIM))
    d['p_sample'] = nrm((DEPTH, DEC_BATCH, DEC_SEQ, PLE_DIM))
    d['state_pool'] = nrm((DEPTH, DEC_BATCH, POOL_BUF, W_POOL))
    d['state_sconv'] = nrm((DEPTH, DEC_BATCH, SCONV_K - 1, W_SCONV))
    d['state_cconv'] = nrm((DEPTH, DEC_BATCH, CCONV_K - 1, W_CCONV), 0.5)
    d['g_f1_pre'] = gain((DEPTH, D_MODEL))
    d['w_f1_gate'] = nrm((DEPTH, D_MODEL, D_FF), D_MODEL ** -0.5)
    d['w_f1_up'] = nrm((DEPTH, D_MODEL, D_FF), D_MODEL ** -0.5)
    d['w_f1_down'] = nrm((DEPTH, D_FF, D_MODEL), D_FF ** -0.5)
    d['g_f1_post'] = gain((DEPTH, D_MODEL))
    d['g_mix_pre'] = gain((DEPTH, D_MODEL))
    d['w_in'] = nrm((DEPTH, D_MODEL, IN_COLS), D_MODEL ** -0.5)
    d['pool_w'] = nrm((DEPTH, N_POOL_GROUPS, POOL_GROUP, POOL_GROUP), POOL_GROUP ** -0.5)
    d['pool_scale'] = gain((DEPTH, W_POOL))
    d['w_pool_out'] = nrm((DEPTH, W_POOL, D_MODEL), W_POOL ** -0.5)
    d['sc_conv'] = nrm((DEPTH, SCONV_K, W_SCONV), SCONV_K ** -0.5)
    d['w_sc_out'] = nrm((DEPTH, W_SCONV, D_MODEL), W_SCONV ** -0.5)
    d['cf_conv'] = nrm((DEPTH, CCONV_K, W_CCONV), CCONV_K ** -0.5)
    d['cf_conv_b'] = nrm((DEPTH, W_CCONV), 0.01)
    d['cf_ln_g'] = gain((DEPTH, W_CCONV))
    d['cf_ln_b'] = nrm((DEPTH, W_CCONV), 0.01)
    d['w_cf_out'] = nrm((DEPTH, W_CCONV, D_MODEL), W_CCONV ** -0.5)
    d['w_o'] = nrm((DEPTH, D_MODEL, D_MODEL), D_MODEL ** -0.5)
    d['g_mix_post'] = gain((DEPTH, D_MODEL))
    d['g_f2_pre'] = gain((DEPTH, D_MODEL))
    d['w_f2_gate'] = nrm((DEPTH, D_MODEL, D_FF), D_MODEL ** -0.5)
    d['w_f2_up'] = nrm((DEPTH, D_MODEL, D_FF), D_MODEL ** -0.5)
    d['w_f2_down'] = nrm((DEPTH, D_FF, D_MODEL), D_FF ** -0.5)
    d['g_f2_post'] = gain((DEPTH, D_MODEL))
    d['g_ple_pre'] = gain((DEPTH, D_MODEL))
    d['w_ple_gate'] = nrm((DEPTH, D_MODEL, D_MODEL), D_MODEL ** -0.5)
    d['w_ple_proj'] = nrm((DEPTH, PLE_DIM, D_MODEL), PLE_DIM ** -0.5)
    d['g_ple_post'] = gain((DEPTH, D_MODEL))
    d['g_final'] = gain((D_MODEL,))
    return d

def reference(x_prompt, x_sample, p_prompt, p_sample, state_pool, state_sconv, state_cconv,
              g_f1_pre, w_f1_gate, w_f1_up, w_f1_down, g_f1_post,
              g_mix_pre, w_in, pool_w, pool_scale, w_pool_out, sc_conv, w_sc_out,
              cf_conv, cf_conv_b, cf_ln_g, cf_ln_b, w_cf_out, w_o, g_mix_post,
              g_f2_pre, w_f2_gate, w_f2_up, w_f2_down, g_f2_post,
              g_ple_pre, w_ple_gate, w_ple_proj, g_ple_post, g_final):
    P = dict(g_f1_pre=g_f1_pre, w_f1_gate=w_f1_gate, w_f1_up=w_f1_up, w_f1_down=w_f1_down, g_f1_post=g_f1_post,
             g_mix_pre=g_mix_pre, w_in=w_in, pool_w=pool_w, pool_scale=pool_scale, w_pool_out=w_pool_out,
             sc_conv=sc_conv, w_sc_out=w_sc_out, cf_conv=cf_conv, cf_conv_b=cf_conv_b, cf_ln_g=cf_ln_g,
             cf_ln_b=cf_ln_b, w_cf_out=w_cf_out, w_o=w_o, g_mix_post=g_mix_post,
             g_f2_pre=g_f2_pre, w_f2_gate=w_f2_gate, w_f2_up=w_f2_up, w_f2_down=w_f2_down, g_f2_post=g_f2_post,
             g_ple_pre=g_ple_pre, w_ple_gate=w_ple_gate, w_ple_proj=w_ple_proj, g_ple_post=g_ple_post,
             g_final=g_final)
    dt = x_prompt.dtype
    zp = jnp.zeros((DEPTH, BATCH, POOL_BUF, W_POOL), dt)
    zs = jnp.zeros((DEPTH, BATCH, SCONV_K - 1, W_SCONV), dt)
    zc = jnp.zeros((DEPTH, BATCH, CCONV_K - 1, W_CCONV), dt)
    y_prompt, npool_p, nsc_p, ncf_p = trunk(x_prompt, p_prompt, zp, zs, zc, 0, P)
    y_sample, npool_s, nsc_s, ncf_s = trunk(x_sample, p_sample, state_pool, state_sconv, state_cconv, PAST_LEN, P)
    return (y_prompt, y_sample, npool_p, nsc_p, ncf_p, npool_s, nsc_s, ncf_s)


_drawn_inputs = setup_inputs


def setup_inputs(seed=0):
    import zlib

    import numpy as np

    out = dict(_drawn_inputs(seed))
    spreads = {}
    factors = {'cf_conv_b': 7.31,
     'cf_ln_g': 2.829,
     'cf_ln_b': 27.532,
     'g_f2_post': 3.034,
     'g_ple_pre': 4.13,
     'pool_scale': 2.955}
    for name, (base, spread) in spreads.items():
        noise = np.random.default_rng([zlib.crc32(name.encode()), seed]).standard_normal(out[name].shape)
        drawn = base * np.exp(spread * noise) if base else spread * noise
        out[name] = __import__('jax').numpy.asarray(drawn.astype(out[name].dtype))
    for name, factor in factors.items():
        out[name] = (out[name] * factor).astype(out[name].dtype)
    return out
```

```python
from contextlib import ExitStack

import concourse.bass as bass
from concourse import mybir

F32 = mybir.dt.float32
F32R = mybir.dt.float32r
ALU = mybir.AluOpType
ACT = mybir.ActivationFunctionType

P = 128
DEPTH = 2
D = 1024
DFF = 2816
W = 512
PLE = 256
SEQ, NSEQ, SLEN = 256, 8, 8
T = SEQ + NSEQ * SLEN
TPAD = 384
DT, FT, WT, PT = D // P, DFF // P, W // P, PLE // P
EPS = 1e-6
CK, SK, WMAX = 31, 3, 16
CH, SH, AH = CK - 1, SK - 1, WMAX - 1


def padded(h):
    return h + SEQ + NSEQ * (h + SLEN)


PHASES = [("f1_up", FT // 2, DT), ("f1_dn", DT // 2, FT // 2),
          ("glu", 2, DT), ("short", 2, DT), ("pool", 1, DT), ("bgate", 1, DT),
          ("gate0", 2, DT), ("out0", 1, 2 * WT), ("gate1", 2, DT), ("out1", 1, 2 * WT),
          ("gate2", 2, DT), ("out2", 1, 2 * WT), ("wo", 2, DT),
          ("f2_up", FT // 2, DT), ("f2_dn", DT // 2, FT // 2),
          ("pg", 2, DT), ("pp", 1, 2 * PT)]
PAIRS = {n: p for n, p, _ in PHASES}
HALF = {n: t * P for n, _, t in PHASES}
PAIR0 = {n: sum(p for _, p, _ in PHASES[:i]) for i, (n, _, _) in enumerate(PHASES)}
NPAIR = sum(PAIRS.values())
NHALF = 4 * NPAIR
HMAX = max(HALF.values())

_MOVED = [("f1_up", 4 * PAIRS["f1_up"]), ("glu", 8), ("short", 8), ("pool", 4), ("bgate", 4),
          ("gate0", 8), ("out0", 8), ("gate1", 4), ("poolw", 4), ("gate1b", 4), ("out1", 8),
          ("gate2", 8), ("out2", 8), ("f2_up", 4 * PAIRS["f2_up"]), ("pg", 8), ("pp", 8)]
MOVED0 = {n: sum(k for _, k in _MOVED[:i]) for i, (n, _) in enumerate(_MOVED)}
NMOVED = sum(k for _, k in _MOVED)

_SQ = [("post1", DT), ("pre1", DT), ("ln", WT), ("post2", DT), ("pre2", DT),
       ("post3", DT), ("pre3", DT), ("post4", DT), ("pre4", DT)]
SQ0 = {n: sum(k for _, k in _SQ[:i]) for i, (n, _) in enumerate(_SQ)}
NSQ = sum(k for _, k in _SQ)
STAT = {n: i for i, (n, _) in enumerate(_SQ)}
NSTAT = len(_SQ)
X0 = {"b1": 0, "m": DT, "b2": 2 * DT, "b3": 3 * DT, "b4": 4 * DT}
NX = 5 * DT
SIG0 = {"f1": 0, "glu": FT, "gate0": FT + WT, "gate1": FT + WT + DT, "gate2": FT + WT + 2 * DT,
        "f2": FT + WT + 3 * DT, "pg": 2 * FT + WT + 3 * DT}
NSIG = 2 * FT + WT + 4 * DT

TAPS = [(k, t) for k in range(CK) for t in (0, 1)]
TAPS[8:8] = [(0, 3)]
TAPS += [(k, 2) for k in range(CK)]
TAP_AT = {u: i for i, u in enumerate(TAPS)}
NTAP = 2 * len(TAPS)
RING3 = 4

_COLS = [("g_f1_post", DT), ("g_mix_pre", DT), ("g_mix_post", DT), ("g_f2_pre", DT), ("g_f2_post", DT),
         ("g_ple_pre", DT), ("g_ple_post", DT), ("g_next", DT), ("pool_scale", WT), ("cf_conv_b", WT),
         ("cf_ln_g", WT), ("cf_ln_b", WT), ("sc_conv", SK * WT), ("cf_conv", CK * WT)]
COL = {n: sum(k for _, k in _COLS[:i]) for i, (n, _) in enumerate(_COLS)}
NCOL = sum(k for _, k in _COLS)
FIRST_G = DEPTH * NCOL
COUNTS = FIRST_G + DT
NPAR = COUNTS + WT * AH

HISTORY = [WT * NSEQ * k for k in (CH, SH, AH)]
STATES = [WT * (NSEQ + 1) * k for k in (CH, SH, AH)]


def trunk(nc, x, par, side, early, streams, y, states):
    with ExitStack() as ctx:
        def sb(name, cols, dt=F32, where=ctx):
            return where.enter_context(nc.sbuf_tensor(name, [P, *cols], dt))

        def sem(name):
            return ctx.enter_context(nc.semaphore(name))

        raw = sb("raw", [4, HMAX])
        w_hi_sb = sb("w_hi_sb", [4, HMAX], F32R)
        w_lo_sb = sb("w_lo_sb", [4, HMAX], F32R)
        h = sb("h", [DT, T])
        x_hi = sb("x_hi", [DT, T], F32R)
        x_lo = sb("x_lo", [DT, T], F32R)
        f = sb("f", [DT, T])
        ga = sb("ga", [2, T])
        gb = sb("gb", [2, T])
        sg = sb("sg", [RING3, T])
        sq = sb("sq", [2, T])
        ssq = sb("ssq", [TPAD])
        rb = sb("rb", [T])
        pars = sb("pars", [NPAR])
        cur = sb("cur", [NCOL])
        ones = sb("ones", [P])
        meanw = sb("meanw", [P])
        ident = sb("ident", [P])
        eps = sb("eps", [2])
        root = sb("root", [3])
        rinv = sb("rinv", [3])
        hist = sb("hist", [sum(STATES)])
        p_raw, pw_raw = hist[:, 0:PT * T], hist[:, PT * T:PT * T + WT * P]
        p_hi = sb("p_hi", [PT * T], F32R)
        p_lo = sb("p_lo", [PT * T], F32R)
        pw_hi = sb("pw_hi", [WT * P], F32R)
        pw_lo = sb("pw_lo", [WT * P], F32R)
        with ExitStack() as ffn:
            mid_hi = sb("mid_hi", [FT, T], F32R, ffn)
            mid_lo = sb("mid_lo", [FT, T], F32R, ffn)
        cbuf = sb("cbuf", [WT, padded(CH)])
        sbuf = sb("sbuf", [WT, padded(SH)])
        abuf = sb("abuf", [WT, padded(AH)])
        bg = sb("bg", [WT, T])
        cc = sb("cc", [WT, T])
        y0_hi = sb("y0_hi", [WT, T], F32R)
        y0_lo = sb("y0_lo", [WT, T], F32R)
        y1_hi = sb("y1_hi", [WT, T], F32R)
        y1_lo = sb("y1_lo", [WT, T], F32R)
        gate = sb("gate", [DT, T])
        win = sb("win", [2, padded(AH)])
        pmf = sb("pmf", [T])

        ps = ctx.enter_context(nc.psum_tensor("ps", [P, 8, 512], F32))
        STATB = 7
        bc = ps[:, STATB, 64:64 + T]
        FIRST_BANKS = (4, 5, 6, 3)

        loaded = sem("loaded")
        raw_in = [sem("raw_in0"), sem("raw_in1")]
        early_in = sem("early_in")
        side_in = sem("side_in")
        const_ready = sem("const_ready")
        w_hi = sem("w_hi")
        w_lo = sem("w_lo")
        halves_done = sem("halves_done")
        moved = sem("moved")
        squared = sem("squared")
        summed = sem("summed")
        stat_full = sem("stat_full")
        root_ready = sem("root_ready")
        rinv_ready = sem("rinv_ready")
        bc_full = sem("bc_full")
        rb_ready = sem("rb_ready")
        par_ready = sem("par_ready")
        step_t = sem("step_t")
        h_ready = sem("h_ready")
        xhi_ready = sem("xhi_ready")
        x_ready = sem("x_ready")
        sig = sem("sig")
        swi = sem("swi")
        mid_ready = sem("mid_ready")
        glu_ready = sem("glu_ready")
        cv_ready = sem("cv_ready")
        tap = sem("tap")
        prod3 = sem("prod3")
        tap3 = sem("tap3")
        c3 = sem("c3")
        pstep = sem("pstep")
        pm_ready = sem("pm_ready")
        pw_split = sem("pw_split")
        pw_hi_ready = sem("pw_hi_ready")
        poolw_done = sem("poolw_done")
        ya_hi = sem("ya_hi")
        yb_ready = sem("yb_ready")
        yb_step = sem("yb_step")
        yc_ready = sem("yc_ready")
        added = sem("added")
        ln_sum = sem("ln_sum")
        ln_mean = sem("ln_mean")
        ln_step = sem("ln_step")
        ln_sig = sem("ln_sig")
        ln_y = sem("ln_y")
        yc_step = sem("yc_step")
        hist_in = sem("hist_in")
        staged = sem("staged")
        stored = sem("stored")
        y_ready = sem("y_ready")
        tick = sem("tick")

        block = ctx.enter_context(nc.Block())

        def v_half(L, ph, pair, j):
            return L * NHALF + 4 * (PAIR0[ph] + pair) + j + 1

        def v_moved(L, ph, n):
            return L * NMOVED + MOVED0[ph] + n + 5

        def v_sq(L, name, m):
            return DT + L * NSQ + SQ0[name] + m + 1

        def v_stat(L, name):
            return L * NSTAT + STAT[name] + 2

        def v_x(L, b, m):
            return DT + L * NX + X0[b] + m + 1

        def v_sig(L, name, m):
            return L * NSIG + SIG0[name] + m + 1

        def prompt(t):
            return t[:, 0:SEQ]

        def sample(t):
            return t[:, SEQ:T].rearrange("p (s t) -> p s t", t=SLEN)

        def pad_prompt(t, hist_rows, at):
            return t[:, at:at + SEQ]

        def pad_sample(t, hist_rows, at, n=SLEN):
            return t[:, hist_rows + SEQ:].rearrange("p (s w) -> p s w", w=hist_rows + SLEN)[:, :, at:at + n]

        def part(i, buf, hist_rows, tile, at):
            row = buf[:, tile, :]
            return pad_sample(row, hist_rows, at) if i else pad_prompt(row, hist_rows, at)

        def tok(i, row):
            return sample(row) if i else prompt(row)

        @block.sync
        def _(sp):
            sp.dma_start(pars[:, :], par).then_inc(loaded, 16)
            sp.dma_start(h[:, :, :], x.rearrange("p (k t) -> p k t", t=T)).then_inc(loaded, 16)

            def load_pair(L, ph, pair):
                src = streams[ph]
                for s in range(2):
                    sp.wait_ge(w_lo, L * NHALF + 4 * (PAIR0[ph] + pair) + 2 * s + 2)
                    row = (L * PAIRS[ph] + pair) * 2 + s
                    sp.dma_start(raw[:, 2 * s:2 * s + 2, 0:HALF[ph]],
                                 src[bass.ds(row, 1), :, :].rearrange("a p (h n) -> (a p) h n", h=2)
                                 ).then_inc(raw_in[s], 16)

            with sp.Fori(0, DEPTH) as L:
                sp.wait_ge(stored, L * 16 + 16)
                sp.sem_inc(tick, 1)
                sp.wait_ge(pw_split, L * 2 + 2)
                sp.dma_start(hist[:, 0:PT * T + WT * P], early[bass.ds(L, 1), :, :].rearrange("a p n -> (a p) n")).then_inc(early_in, 16)
                for ph, n, _ in PHASES:
                    if ph == "f1_dn":
                        sp.wait_ge(pw_split, L * 2 + 4)
                        sp.dma_start(hist[:, 0:sum(HISTORY)],
                                     side[bass.ds(L, 1), :, :].rearrange("a p n -> (a p) n")).then_inc(side_in, 16)
                    if n > 2:
                        with sp.Fori(0, n) as i:
                            load_pair(L, ph, i)
                    else:
                        for i in range(n):
                            load_pair(L, ph, i)

        @block.tensor
        def _(pe):
            def products(out, w, n, rhs_hi, rhs_lo, start, stop):
                whi, wlo = w_hi_sb[:, w, n:n + P], w_lo_sb[:, w, n:n + P]
                pe.matmul(out, whi, rhs_hi, start=start, stop=False, skip_group_check=True)
                pe.matmul(out, whi, rhs_lo, start=False, stop=False, skip_group_check=True)
                return pe.matmul(out, wlo, rhs_hi, start=False, stop=stop, skip_group_check=True)

            def wait_half(L, ph, pair, j):
                pe.wait_ge(w_lo, v_half(L, ph, pair, j) + 4)

            def pair_of_x(L, ph, pair, moved0, between={}, stat=None):
                for j in range(4):
                    wait_half(L, ph, pair, j)
                    if moved0 is not None:
                        pe.wait_ge(moved, moved0 + j - 4)
                    for k in range(DT):
                        mm = products(ps[:, j, 0:T], j, k * P, x_hi[:, k, :], x_lo[:, k, :], k == 0, k == DT - 1)
                    mm.then_inc(halves_done, 1)
                    if j in between:
                        between[j](L, stat)

            def first_pair(L, ph, xname, xl, moved0, stat=None):
                half = DT // 2
                for j in range(4):
                    wait_half(L, ph, 0, j)
                if moved0 is not None:
                    pe.wait_ge(moved, moved0 - 1)
                for k in range(half):
                    pe.wait_ge(x_ready, xl + k + 1)
                    for j in range(4):
                        products(ps[:, FIRST_BANKS[j], 0:T], j, k * P, x_hi[:, k, :], x_lo[:, k, :], k == 0, False)
                for j in range(4):
                    for k in range(half, DT):
                        if j == 0:
                            pe.wait_ge(x_ready, xl + k + 1)
                        mm = products(ps[:, FIRST_BANKS[j], 0:T], j, k * P, x_hi[:, k, :], x_lo[:, k, :], False, k == DT - 1)
                    mm.then_inc(halves_done, 1)
                    if j == 1 and stat is not None:
                        sums(*stat)
                    if j == 2 and stat is not None:
                        spread(*stat)

            def sums(L, name):
                if name is None:
                    pe.wait_ge(summed, DT)
                    v = 1
                else:
                    n = WT if name == "ln" else DT
                    pe.wait_ge(summed, v_sq(L, name, n - 1))
                for t in range(3):
                    mm = pe.matmul(ps[:, STATB, t:t + 1], ssq[:, t * P:(t + 1) * P], ones[:, 0:1], start=True, stop=True)
                mm.then_inc(stat_full, 1)

            def spread(L, name):
                pe.wait_ge(rinv_ready, 1 if name is None else v_stat(L, name))
                for t in range(3):
                    n = min(P, T - t * P)
                    mm = pe.matmul(ps[:, STATB, 64 + t * P:64 + t * P + n], rinv[:, t:t + 1].broadcast_to([P, P]),
                                   ident[:, 0:n], start=True, stop=True)
                mm.then_inc(bc_full, 1)

            def down(L, ph, which, moved_all, sq):
                with pe.Fori(0, PAIRS[ph]) as i:
                    pe.wait_ge(moved, moved_all)
                    for g in range(2):
                        pe.wait_ge(squared, v_sq(L, sq, 2 * i + g - 2))
                        for c in range(2):
                            j = 2 * g + c
                            wait_half(L, ph, i, j)
                            pe.wait_ge(mid_ready, L * 2 * FT + which * FT + 2 + (c + 1) * (FT // 2))
                            for k in range(FT // 2):
                                m = c * (FT // 2) + k
                                mm = products(ps[:, g, 0:T], j, k * P, mid_hi[:, m, :], mid_lo[:, m, :], m == 0, m == FT - 1)
                            mm.then_inc(halves_done, 1)

            def narrow(L, ph, kt, rhs_hi, rhs_lo):
                for j in range(4):
                    wait_half(L, ph, 0, j)
                    for c in range(2):
                        q = 2 * j + c
                        pe.wait_ge(moved, v_moved(L, ph, q) - 4)
                        for k in range(kt):
                            mm = products(ps[:, q % 4, 0:T], j, k * 2 * P + c * P, rhs_hi[:, k, :], rhs_lo[:, k, :],
                                          k == 0, k == kt - 1)
                    mm.then_inc(halves_done, 1)

            pe.wait_ge(const_ready, 6)
            sums(0, None)
            spread(0, None)
            with pe.Fori(0, DEPTH) as L:
                first_pair(L, "f1_up", "b4", L * NX, v_moved(L, "f1_up", 0))
                with pe.Fori(1, PAIRS["f1_up"]) as i:
                    pair_of_x(L, "f1_up", i, v_moved(L, "f1_up", 4 * i))
                down(L, "f1_dn", 0, v_moved(L, "f1_up", 4 * PAIRS["f1_up"] - 1), "post1")
                sums(L, "post1")
                spread(L, "post1")
                first_pair(L, "glu", "b1", v_x(L, "b1", -1), None, (L, "pre1"))
                pair_of_x(L, "glu", 1, v_moved(L, "glu", 4))
                for ph in ("short", "pool", "bgate", "gate0"):
                    for i in range(PAIRS[ph]):
                        pair_of_x(L, ph, i, v_moved(L, ph, 4 * i))
                pe.wait_ge(yb_ready, L * WT + WT)
                narrow(L, "out0", WT, y0_hi, y0_lo)
                pair_of_x(L, "gate1", 0, v_moved(L, "gate1", 0))
                pe.wait_ge(pw_split, L * 2 + 4)
                for g in range(WT):
                    pe.wait_ge(pm_ready, L * WT + g + 1)
                    pe.wait_ge(moved, v_moved(L, "poolw", g) - 4)
                    whi, wlo = pw_hi[:, g * P:(g + 1) * P], pw_lo[:, g * P:(g + 1) * P]
                    pe.matmul(ps[:, g, 0:T], whi, y1_hi[:, g, :], start=True, stop=False)
                    pe.matmul(ps[:, g, 0:T], whi, y1_lo[:, g, :], start=False, stop=False)
                    pe.matmul(ps[:, g, 0:T], wlo, y1_hi[:, g, :], start=False, stop=True).then_inc(poolw_done, 1)
                pair_of_x(L, "gate1", 1, v_moved(L, "gate1b", 0))
                pe.wait_ge(moved, v_moved(L, "poolw", WT - 1))
                narrow(L, "out1", WT, y0_hi, y0_lo)
                pe.wait_ge(ln_sum, L * (WT - 1) + WT - 1)
                pe.matmul(bc, meanw[:, :], pmf[:, :], start=True, stop=True).then_inc(ln_mean, 1)
                pair_of_x(L, "gate2", 0, v_moved(L, "gate2", 0))
                pair_of_x(L, "gate2", 1, v_moved(L, "gate2", 4), {0: sums, 1: spread}, "ln")
                pe.wait_ge(yc_ready, L * WT + WT)
                narrow(L, "out2", WT, y1_hi, y1_lo)
                first_pair(L, "wo", "m", v_x(L, "m", -1), v_moved(L, "out2", 8))
                for j in range(4):
                    wait_half(L, "wo", 1, j)
                    if j == 3:
                        pe.wait_ge(squared, v_sq(L, "post2", 3))
                    for k in range(DT):
                        mm = products(ps[:, j, 0:T], j, k * P, x_hi[:, k, :], x_lo[:, k, :], k == 0, k == DT - 1)
                    mm.then_inc(halves_done, 1)
                sums(L, "post2")
                spread(L, "post2")
                first_pair(L, "f2_up", "b2", v_x(L, "b2", -1), None, (L, "pre2"))
                with pe.Fori(1, PAIRS["f2_up"]) as i:
                    pair_of_x(L, "f2_up", i, v_moved(L, "f2_up", 4 * i))
                down(L, "f2_dn", 1, v_moved(L, "f2_up", 4 * PAIRS["f2_up"] - 1), "post3")
                sums(L, "post3")
                spread(L, "post3")
                first_pair(L, "pg", "b3", v_x(L, "b3", -1), None, (L, "pre3"))
                pair_of_x(L, "pg", 1, v_moved(L, "pg", 4))
                narrow(L, "pp", PT, p_hi[:, :].rearrange("p (k t) -> p k t", t=T),
                       p_lo[:, :].rearrange("p (k t) -> p k t", t=T))
                sums(L, "post4")
                spread(L, "post4")
                sums(L, "pre4")
                spread(L, "pre4")

        @block.scalar
        def _(act):
            def split(L, ph, pair, j):
                if j % 2 == 0:
                    act.wait_ge(raw_in[j // 2], (L * NPAIR + PAIR0[ph] + pair + 1) * 16)
                act.wait_ge(halves_done, v_half(L, ph, pair, j))
                n = HALF[ph]
                act.activation(w_hi_sb[:, j, 0:n], raw[:, j, 0:n], ACT.Copy).then_inc(w_hi, 1)

            def square(src, L, name, m, par):
                act.wait_ge(summed, v_sq(L, name, m - 2) if name else m - 1)
                act.activation(sq[:, par, :], src, ACT.Square).then_inc(squared, 1)

            def finish_root(L, name):
                act.wait_ge(stat_full, 1 if name is None else v_stat(L, name))
                twice = 4.0 if name in ("post1", "post3") else 1.0
                width = W if name == "ln" else D
                e = eps[:, 1:2] if twice == 4.0 else eps[:, 0:1]
                act.activation(root[:, :], ps[:, STATB, 0:3], ACT.Sqrt, bias=e, scale=twice / width).then_inc(root_ready, 1)

            def keep_rb(L, name):
                act.wait_ge(bc_full, 1 if name is None else v_stat(L, name))
                act.activation(rb[:, :], bc, ACT.Copy).then_inc(rb_ready, 1)

            def out_of_psum(src, L, name, m, par, gain):
                act.activation(f[:, bass.ds(m, 1), :] if not isinstance(m, int) else f[:, m, :], src, ACT.Copy,
                               scale=cur[:, bass.ds(COL[gain] + m, 1)] if not isinstance(m, int)
                               else cur[:, COL[gain] + m:COL[gain] + m + 1])
                square(src, L, name, m, par)

            def chase(L, b, gain, name, n):
                for m in range(DT):
                    act.wait_ge(h_ready, L * 4 * DT + n * DT + m + 1)
                    act.activation(x_hi[:, m, :], h[:, m, :], ACT.Copy,
                                   scale=cur[:, COL[gain] + m:COL[gain] + m + 1]).then_inc(xhi_ready, 1)
                    square(h[:, m, :], L, name, m, m % 2)

            def boundary(L, n, post, pre, gain):
                finish_root(L, post)
                chase(L, None, gain, pre, n)
                finish_root(L, pre)
                act.preload_act_table(ACT.Sigmoid)
                keep_rb(L, pre)

            def sigmoid(out, src, L, ph, n):
                act.wait_ge(moved, v_moved(L, ph, n))
                act.activation(out, src, ACT.Sigmoid).then_inc(sig, 1)

            def up_step(L, ph, nxt, pair, prev_pair):
                for j in range(4):
                    split(L, nxt, pair, j)
                    if j % 2 == 1:
                        sigmoid(sg[:, j // 2, :], ga[:, j // 2, :], L, ph, 4 * prev_pair + j - 1)

            def down_step(L, ph, nxt, pair, prev_pair, name, gain):
                for j in range(4):
                    split(L, nxt, pair, j)
                    if j % 2 == 1:
                        act.wait_ge(halves_done, v_half(L, ph, prev_pair, j) + 4)
                        out_of_psum(ps[:, j // 2, 0:T], L, name, 2 * prev_pair + j // 2, j // 2, gain)

            def ffn(L, up, dn, after, name, gain):
                with act.Fori(1, PAIRS[up]) as i:
                    up_step(L, up, up, i, i - 1)
                up_step(L, up, dn, 0, PAIRS[up] - 1)
                act.preload_act_table(ACT.Sqrt)
                with act.Fori(1, PAIRS[dn]) as i:
                    down_step(L, dn, dn, i, i - 1, name, gain)
                down_step(L, dn, after, 0, PAIRS[dn] - 1, name, gain)

            tap_of_3 = iter(range(1, CK))

            def product3(L):
                k = next(tap_of_3, None)
                if k is None:
                    return
                if k == 1:
                    act.wait_ge(hist_in, L * 6 + 2)
                    act.wait_ge(glu_ready, L * WT + WT)
                if k > RING3:
                    act.wait_ge(tap3, L * (CK - 1) + k - RING3)
                c = COL["cf_conv"] + k * WT + 3
                for i in range(2):
                    op = act.activation(tok(i, sg[:, k % RING3, :]), part(i, cbuf, CH, 3, k), ACT.Copy, scale=cur[:, c:c + 1])
                op.then_inc(prod3, 1)

            def gates(L, ph, group, name, m0, nxt, pair):
                for j in range(4):
                    split(L, nxt, pair, j)
                    sigmoid(gate[:, m0 + j, :], ga[:, j % 2, :], L, group, j)
                    if ph != "pg":
                        product3(L)

            act.wait_ge(loaded, 32)
            act.wait_ge(const_ready, 6)
            act.preload_act_table(ACT.Sqrt)
            for m in range(DT):
                act.activation(x_hi[:, m, :], h[:, m, :], ACT.Copy,
                               scale=pars[:, FIRST_G + m:FIRST_G + m + 1]).then_inc(xhi_ready, 1)
                if m >= 2:
                    act.wait_ge(summed, m - 1)
                act.activation(sq[:, m % 2, :], h[:, m, :], ACT.Square).then_inc(squared, 1)
            finish_root(0, None)
            keep_rb(0, None)
            act.preload_act_table(ACT.Sigmoid)
            with act.Fori(0, DEPTH) as L:
                for j in range(4):
                    split(L, "f1_up", 0, j)
                act.wait_ge(early_in, L * 16 + 16)
                act.activation(p_hi[:, :], p_raw, ACT.Copy).then_inc(pw_hi_ready, 1)
                act.activation(pw_hi[:, :], pw_raw, ACT.Copy).then_inc(pw_hi_ready, 1)
                act.wait_ge(par_ready, L + 1)
                ffn(L, "f1_up", "f1_dn", "glu", "post1", "g_f1_post")
                boundary(L, 0, "post1", "pre1", "g_mix_pre")
                for pair in range(2):
                    nxt = [("glu", 1), ("short", 0)][pair]
                    for j in range(4):
                        split(L, nxt[0], nxt[1], j)
                        if j % 2 == 1:
                            act.wait_ge(moved, v_moved(L, "glu", 4 * pair + j))
                            act.activation(sg[:, j // 2, :], gb[:, j // 2, :], ACT.Sigmoid).then_inc(sig, 1)
                for nxt in (("short", 1), ("pool", 0), ("bgate", 0), ("gate0", 0)):
                    for j in range(4):
                        split(L, *nxt, j)
                        product3(L)
                gates(L, "gate0", "gate0", "gate0", 0, "gate0", 1)
                for j in range(4):
                    split(L, "out0", 0, j)
                    sigmoid(gate[:, 4 + j, :], ga[:, j % 2, :], L, "gate0", 4 + j)
                    product3(L)
                for j in range(4):
                    split(L, "gate1", 0, j)
                    product3(L)
                for j in range(4):
                    split(L, "gate1", 1, j)
                    sigmoid(gate[:, j, :], ga[:, j % 2, :], L, "gate1", j)
                    product3(L)
                for g in range(WT):
                    act.wait_ge(poolw_done, L * WT + g + 1)
                    act.activation(y0_hi[:, g, :], ps[:, g, 0:T], ACT.Copy,
                                   scale=cur[:, COL["pool_scale"] + g:COL["pool_scale"] + g + 1]).then_inc(ya_hi, 1)
                for j in range(4):
                    split(L, "out1", 0, j)
                    sigmoid(gate[:, 4 + j, :], ga[:, j % 2, :], L, "gate1b", j)
                for j in range(4):
                    split(L, "gate2", 0, j)
                for j in range(4):
                    split(L, "gate2", 1, j)
                    act.wait_ge(ln_step, L * 3 * WT + j + 1)
                    square(cc[:, j, :], L, "ln", j, j % 2)
                    sigmoid(gate[:, j, :], ga[:, j % 2, :], L, "gate2", j)
                act.preload_act_table(ACT.Sqrt)
                finish_root(L, "ln")
                act.preload_act_table(ACT.Sigmoid)
                for j in range(4):
                    split(L, "out2", 0, j)
                    act.wait_ge(ln_step, L * 3 * WT + WT + j + 1)
                    if j >= 2:
                        act.wait_ge(yc_ready, L * WT + j - 1)
                    act.activation(sg[:, j % 2, :], cc[:, j, :], ACT.Sigmoid,
                                   scale=cur[:, COL["cf_ln_g"] + j:COL["cf_ln_g"] + j + 1],
                                   bias=cur[:, COL["cf_ln_b"] + j:COL["cf_ln_b"] + j + 1]).then_inc(ln_sig, 1)
                    sigmoid(gate[:, 4 + j, :], ga[:, j % 2, :], L, "gate2", 4 + j)
                for j in range(4):
                    split(L, "wo", 0, j)
                    for m in (2 * j, 2 * j + 1):
                        act.wait_ge(added, L * 2 * DT + DT + m + 1)
                        act.activation(x_hi[:, m, :], f[:, m, :], ACT.Copy).then_inc(xhi_ready, 1)
                act.preload_act_table(ACT.Sqrt)
                for j in range(4):
                    split(L, "wo", 1, j)
                    act.wait_ge(halves_done, v_half(L, "wo", 0, j) + 4)
                    out_of_psum(ps[:, FIRST_BANKS[j], 0:T], L, "post2", j, j % 2, "g_mix_post")
                for j in range(4):
                    split(L, "f2_up", 0, j)
                    act.wait_ge(halves_done, v_half(L, "wo", 1, j) + 4)
                    out_of_psum(ps[:, j, 0:T], L, "post2", 4 + j, j % 2, "g_mix_post")
                boundary(L, 1, "post2", "pre2", "g_f2_pre")
                act.wait_ge(staged, L * 6 + 6)
                act.dma_start(states[bass.ds(L, 1), :, :].rearrange("a p n -> (a p) n"), hist[:, :]).then_inc(stored, 16)
                ffn(L, "f2_up", "f2_dn", "pg", "post3", "g_f2_post")
                boundary(L, 2, "post3", "pre3", "g_ple_pre")
                gates(L, "pg", "pg", "pg", 0, "pg", 1)
                for j in range(4):
                    split(L, "pp", 0, j)
                    sigmoid(gate[:, 4 + j, :], ga[:, j % 2, :], L, "pg", 4 + j)
                act.preload_act_table(ACT.Sqrt)
                for m in range(DT):
                    act.wait_ge(moved, v_moved(L, "pp", m))
                    out_of_psum(gate[:, m, :], L, "post4", m, m % 2, "g_ple_post")
                boundary(L, 3, "post4", "pre4", "g_next")
            act.wait_ge(y_ready, DT)
            act.dma_start(y, f[:, :, :].rearrange("p k t -> p (k t)")).then_inc(stored, 16)
            act.wait_ge(stored, 16 * DEPTH + 32)

        @block.vector
        def _(dve):
            def split(L, ph, pair, j):
                dve.wait_ge(w_hi, v_half(L, ph, pair, j))
                n = HALF[ph]
                dve.tensor_tensor(w_lo_sb[:, j, 0:n], raw[:, j, 0:n], w_hi_sb[:, j, 0:n].bitcast(F32),
                                  ALU.subtract).then_inc(w_lo, 1)

            def add_square(L, name, m, par):
                dve.wait_ge(squared, v_sq(L, name, m) if name else m + 1)
                first = isinstance(m, int) and m == 0
                if first:
                    dve.tensor_copy(ssq[:, 0:T], sq[:, par, :]).then_inc(summed, 1)
                else:
                    dve.wait_ge(summed, v_sq(L, name, m - 1) if name else m)
                    dve.tensor_tensor(ssq[:, 0:T], ssq[:, 0:T], sq[:, par, :], ALU.add).then_inc(summed, 1)

            def invert(L, name):
                dve.wait_ge(root_ready, 1 if name is None else v_stat(L, name))
                dve.reciprocal(rinv[:, :], root[:, :]).then_inc(rinv_ready, 1)

            def boundary(L, n, b, post, pre, gain):
                invert(L, post)
                dve.wait_ge(bc_full, v_stat(L, post))
                for i in range(DT + 2):
                    if i < DT:
                        if i >= 2:
                            dve.wait_ge(h_ready, L * 4 * DT + n * DT + i - 1)
                        dve.tensor_tensor(ga[:, i % 2, :], f[:, i, :], bc, ALU.mult).then_inc(step_t, 1)
                    if i >= 2:
                        m = i - 2
                        dve.wait_ge(xhi_ready, v_x(L, b, m))
                        dve.scalar_tensor_tensor(x_lo[:, m, :], h[:, m, :], cur[:, COL[gain] + m:COL[gain] + m + 1],
                                                 x_hi[:, m, :].bitcast(F32), ALU.mult, ALU.subtract).then_inc(x_ready, 1)
                        add_square(L, pre, m, m % 2)
                invert(L, pre)
                dve.wait_ge(rb_ready, L * 4 + n + 2)

            def move(out, bank):
                dve.tensor_tensor(out, ps[:, bank, 0:T], rb[:, :], ALU.mult).then_inc(moved, 1)

            def up_step(L, ph, which, nxt, pair, prev_pair, banks):
                for j in range(4):
                    split(L, nxt, pair, j)
                    g = j // 2
                    dve.wait_ge(halves_done, v_half(L, ph, prev_pair, j) + 4)
                    if j % 2 == 0:
                        dve.wait_ge(mid_ready, L * 2 * FT + which * FT + 2 * prev_pair + g + 1)
                    move((ga, gb)[j % 2][:, g, :], banks[j])

            def down_step(L, nxt, pair, prev_pair, name, peel=False):
                for j in range(4):
                    split(L, nxt, pair, j)
                    if j % 2 == 1:
                        add_square(L, name, 2 * prev_pair + j // 2, j // 2)

            def ffn(L, up, dn, after, which, name):
                up_step(L, up, which, up, 1, 0, FIRST_BANKS)
                with dve.Fori(2, PAIRS[up]) as i:
                    up_step(L, up, which, up, i, i - 1, range(4))
                up_step(L, up, which, dn, 0, PAIRS[up] - 1, range(4))
                down_step(L, dn, 1, 0, name)
                with dve.Fori(2, PAIRS[dn]) as i:
                    down_step(L, dn, i, i - 1, name)
                down_step(L, after, 0, PAIRS[dn] - 1, name)

            def gate_step(L, ph, group, pair, nxt, sname, m0, banks=range(4), taps=(), short=False):
                for j in range(4):
                    split(L, *nxt, j)
                    dve.wait_ge(halves_done, v_half(L, ph, pair, j) + 4)
                    dve.wait_ge(sig, v_sig(L, sname, m0 + j - 2))
                    move(ga[:, j % 2, :], banks[j])
                    if short:
                        short_gate(L, j)
                    if j < len(taps):
                        long_taps(L, taps[j])

            todo = iter(TAPS)

            def long_taps(L, n):
                for _ in range(n):
                    k, t = next(todo)
                    c = COL["cf_conv"] + k * WT + t
                    if k == 0:
                        dve.wait_ge(glu_ready, L * WT + t + 1)
                    for i in range(2):
                        src, dst = part(i, cbuf, CH, t, k), tok(i, cc[:, t, :])
                        if k == 0:
                            b = COL["cf_conv_b"] + t
                            dve.tensor_scalar(dst, src, cur[:, c:c + 1], cur[:, b:b + 1], ALU.mult, ALU.add).then_inc(tap, 1)
                        else:
                            dve.wait_ge(tap, L * NTAP + 2 * TAP_AT[k - 1, t] + i + 1)
                            dve.scalar_tensor_tensor(dst, src, cur[:, c:c + 1], dst, ALU.mult, ALU.add).then_inc(tap, 1)

            NC3 = (2 * SK + 1) * WT

            def short_conv(L, t):
                dve.wait_ge(cv_ready, L * WT + t + 1)
                for k in range(SK):
                    c = COL["sc_conv"] + k * WT + t
                    for i in range(2):
                        src, dst = part(i, sbuf, SH, t, k), tok(i, f[:, t, :])
                        if k == 0:
                            dve.tensor_scalar(dst, src, cur[:, c:c + 1], None, ALU.mult).then_inc(c3, 1)
                        else:
                            dve.wait_ge(c3, L * NC3 + 2 * SK * t + 2 * (k - 1) + i + 1)
                            dve.scalar_tensor_tensor(dst, src, cur[:, c:c + 1], dst, ALU.mult, ALU.add).then_inc(c3, 1)

            def short_gate(L, t):
                dve.wait_ge(c3, L * NC3 + 2 * SK * (t + 1))
                dve.wait_ge(moved, v_moved(L, "bgate", t))
                dve.tensor_tensor(f[:, t, :], f[:, t, :], bg[:, t, :], ALU.mult).then_inc(c3, 1)

            dve.memset(ssq[:, T:TPAD], 0.0).then_inc(w_lo, 4)
            dve.memset(ones[:, :], 1.0).then_inc(moved, 4)
            dve.memset(meanw[:, :], 1.0 / W).then_inc(const_ready, 1)
            dve.memset(eps[:, 0:1], EPS).then_inc(const_ready, 1)
            dve.memset(eps[:, 1:2], 4 * EPS).then_inc(const_ready, 1)
            dve.wait_ge(loaded, 32)
            for m in range(DT):
                dve.wait_ge(xhi_ready, m + 1)
                dve.scalar_tensor_tensor(x_lo[:, m, :], h[:, m, :], pars[:, FIRST_G + m:FIRST_G + m + 1],
                                         x_hi[:, m, :].bitcast(F32), ALU.mult, ALU.subtract).then_inc(x_ready, 1)
                add_square(0, None, m, m % 2)
            invert(0, None)
            with dve.Fori(0, DEPTH) as L:
                dve.tensor_copy(cur[:, :], pars[:, bass.ds(L * NCOL, NCOL)]).then_inc(par_ready, 1)
                dve.wait_ge(rb_ready, L * 4 + 1)
                for j in range(4):
                    split(L, "f1_up", 0, j)
                dve.wait_ge(pw_hi_ready, L * 2 + 2)
                dve.tensor_tensor(p_lo[:, :], p_raw, p_hi[:, :].bitcast(F32), ALU.subtract).then_inc(pw_split, 1)
                dve.tensor_tensor(pw_lo[:, :], pw_raw, pw_hi[:, :].bitcast(F32), ALU.subtract).then_inc(pw_split, 1)
                dve.wait_ge(par_ready, L + 1)
                ffn(L, "f1_up", "f1_dn", "glu", 0, "post1")
                boundary(L, 0, "b1", "post1", "pre1", "g_mix_pre")
                for n, (ph, pair, nxt) in enumerate([("glu", 0, ("glu", 1)), ("glu", 1, ("short", 0)),
                                                     ("short", 0, ("short", 1)), ("short", 1, ("pool", 0))]):
                    for j in range(4):
                        split(L, *nxt, j)
                        dve.wait_ge(halves_done, v_half(L, ph, pair, j) + 4)
                        if j % 2 == 0 and n > 0:
                            dve.wait_ge(glu_ready if n < 3 else cv_ready, L * WT + (2 * n - 2 if n < 3 else 0) + j // 2 + 1)
                        move((ga, gb)[j % 2][:, j // 2, :], FIRST_BANKS[j] if n == 0 else j)
                        if n >= 1:
                            long_taps(L, 3 if n > 1 else (0, 2, 2, 4)[j])
                dve.wait_ge(hist_in, L * 6 + 6)
                for j in range(4):
                    split(L, "bgate", 0, j)
                    dve.wait_ge(halves_done, v_half(L, "pool", 0, j) + 4)
                    dve.tensor_tensor(part(0, abuf, AH, j, AH), prompt(ps[:, j, 0:T]), prompt(rb), ALU.mult)
                    dve.tensor_tensor(part(1, abuf, AH, j, AH), sample(ps[:, j, 0:T]), sample(rb), ALU.mult).then_inc(moved, 1)
                    long_taps(L, 3)
                for j in range(4):
                    split(L, "gate0", 0, j)
                    dve.wait_ge(halves_done, v_half(L, "bgate", 0, j) + 4)
                    move(bg[:, j, :], j)
                    short_conv(L, j)
                    long_taps(L, 1)
                gate_step(L, "gate0", "gate0", 0, ("gate0", 1), "gate0", 0, taps=(2, 2, 2, 2), short=True)
                gate_step(L, "gate0", "gate0", 1, ("out0", 0), "gate0", 4, taps=(3, 3, 3, 3))
                dve.wait_ge(yb_ready, L * WT + WT)
                for j in range(4):
                    split(L, "gate1", 0, j)
                    dve.wait_ge(halves_done, v_half(L, "out0", 0, j) + 4)
                    for m in (2 * j, 2 * j + 1):
                        dve.wait_ge(sig, v_sig(L, "gate0", m))
                        dve.tensor_tensor(f[:, m, :], ps[:, m % 4, 0:T], gate[:, m, :], ALU.mult).then_inc(moved, 1)
                    long_taps(L, 2)
                gate_step(L, "gate1", "gate1", 0, ("gate1", 1), "gate1", 0, taps=(3, 3, 3, 3))
                for g in range(WT):
                    dve.wait_ge(ya_hi, L * WT + g + 1)
                    dve.scalar_tensor_tensor(y0_lo[:, g, :], ps[:, g, 0:T], cur[:, COL["pool_scale"] + g:COL["pool_scale"] + g + 1],
                                             y0_hi[:, g, :].bitcast(F32), ALU.mult, ALU.subtract).then_inc(moved, 1)
                gate_step(L, "gate1", "gate1b", 1, ("out1", 0), "gate1", 4, taps=(3, 3))

                def add_branch(b, nxt, xlo):
                    for j in range(4):
                        split(L, *nxt, j)
                        dve.wait_ge(halves_done, v_half(L, f"out{b}", 0, j) + 4)
                        for m in (2 * j, 2 * j + 1):
                            dve.wait_ge(sig, v_sig(L, f"gate{b}", m))
                            n = (b - 1) * DT + m
                            if n >= 2:
                                dve.wait_ge(added, L * 2 * DT + n - 1)
                            dve.tensor_tensor(gb[:, m % 2, :], ps[:, m % 4, 0:T], gate[:, m, :], ALU.mult).then_inc(moved, 1)
                        if xlo and j:
                            x_of_sum(2 * j - 2)
                            x_of_sum(2 * j - 1)

                def x_of_sum(m):
                    dve.wait_ge(xhi_ready, v_x(L, "m", m))
                    dve.tensor_tensor(x_lo[:, m, :], f[:, m, :], x_hi[:, m, :].bitcast(F32), ALU.subtract).then_inc(x_ready, 1)

                add_branch(1, ("gate2", 0), False)
                dve.wait_ge(ln_mean, L + 1)
                for t in range(WT):
                    dve.tensor_tensor(cc[:, t, :], cc[:, t, :], bc, ALU.subtract).then_inc(ln_step, 1)
                for j in range(4):
                    split(L, "gate2", 1, j)
                    dve.wait_ge(halves_done, v_half(L, "gate2", 0, j) + 4)
                    dve.wait_ge(sig, v_sig(L, "gate2", j - 2))
                    move(ga[:, j % 2, :], j)
                    add_square(L, "ln", j, j % 2)
                invert(L, "ln")
                dve.wait_ge(bc_full, v_stat(L, "ln"))
                for t in range(WT):
                    dve.tensor_tensor(cc[:, t, :], cc[:, t, :], bc, ALU.mult).then_inc(ln_step, 1)
                for j in range(4):
                    split(L, "out2", 0, j)
                    dve.wait_ge(ln_sig, L * WT + j + 1)
                    g, b = COL["cf_ln_g"] + j, COL["cf_ln_b"] + j
                    dve.tensor_scalar(cc[:, j, :], cc[:, j, :], cur[:, g:g + 1], cur[:, b:b + 1], ALU.mult, ALU.add).then_inc(ln_step, 1)
                    dve.wait_ge(halves_done, v_half(L, "gate2", 1, j) + 4)
                    dve.wait_ge(sig, v_sig(L, "gate2", 4 + j - 2))
                    move(ga[:, j % 2, :], j)
                add_branch(2, ("wo", 0), True)
                x_of_sum(DT - 2)
                x_of_sum(DT - 1)
                for j in range(4):
                    split(L, "wo", 1, j)
                    add_square(L, "post2", j, j % 2)
                for j in range(4):
                    split(L, "f2_up", 0, j)
                    add_square(L, "post2", 4 + j, j % 2)
                boundary(L, 1, "b2", "post2", "pre2", "g_f2_pre")
                ffn(L, "f2_up", "f2_dn", "pg", 1, "post3")
                boundary(L, 2, "b3", "post3", "pre3", "g_ple_pre")
                gate_step(L, "pg", "pg", 0, ("pg", 1), "pg", 0, banks=FIRST_BANKS)
                gate_step(L, "pg", "pg", 1, ("pp", 0), "pg", 4)
                for m in range(DT):
                    if m % 2 == 0:
                        dve.wait_ge(halves_done, v_half(L, "pp", 0, m // 2) + 4)
                    dve.wait_ge(sig, v_sig(L, "pg", m))
                    dve.tensor_tensor(gate[:, m, :], ps[:, m % 4, 0:T], gate[:, m, :], ALU.mult).then_inc(moved, 1)
                    if m >= 2:
                        add_square(L, "post4", m - 2, m % 2)
                for m in (DT - 2, DT - 1):
                    add_square(L, "post4", m, m % 2)
                boundary(L, 3, "b4", "post4", "pre4", "g_next")
            for m in range(DT):
                c = COL["g_next"] + m
                dve.scalar_tensor_tensor(f[:, m, :], h[:, m, :], cur[:, c:c + 1], rb[:, :], ALU.mult, ALU.mult).then_inc(y_ready, 1)

        @block.gpsimd
        def _(pool):
            def wait_alone(s, value):
                pool.wait_ge(s, value)
                pool.sem_inc(tick, 1)

            def update_h(L, n):
                for m in range(DT):
                    pool.wait_ge(step_t, L * 4 * DT + n * DT + m + 1)
                    pool.tensor_tensor(h[:, m, :], h[:, m, :], ga[:, m % 2, :], ALU.add).then_inc(h_ready, 1)

            def hidden(L, ph, which, pair):
                for g in range(2):
                    m = 2 * pair + g
                    n = (L * 2 * FT + which * FT + m) * 3
                    pool.wait_ge(moved, v_moved(L, ph, 4 * pair + 2 * g + 1))
                    pool.tensor_tensor(gb[:, g, :], ga[:, g, :], gb[:, g, :], ALU.mult).then_inc(swi, 1)
                    pool.wait_ge(swi, n + 1)
                    pool.wait_ge(sig, v_sig(L, "f1" if which == 0 else "f2", m))
                    pool.tensor_tensor(gb[:, g, :], gb[:, g, :], sg[:, g, :], ALU.mult).then_inc(swi, 1)
                    wait_alone(swi, n + 2)
                    hi, lo = mid_hi[:, bass.ds(m, 1), :], mid_lo[:, bass.ds(m, 1), :]
                    pool.tensor_copy(hi, gb[:, g:g + 1, :]).then_inc(swi, 1)
                    pool.wait_ge(swi, n + 3)
                    pool.tensor_tensor(lo, gb[:, g:g + 1, :], hi.bitcast(F32), ALU.subtract).then_inc(mid_ready, 1)

            NPS = sum(g + 1 + 3 + 1 + 1 for g in range(WT))
            steps = [sum(k + 1 + 5 for k in range(g)) for g in range(WT)]

            tap_of_3 = iter(range(1, CK))

            def add3(L, n=1):
                for _ in range(n):
                    k = next(tap_of_3)
                    pool.wait_ge(prod3, L * (CK - 1) + k)
                    if k == 1:
                        pool.wait_ge(tap, L * NTAP + 2 * TAP_AT[0, 3] + 2)
                    else:
                        pool.wait_ge(tap3, L * (CK - 1) + k - 1)
                    pool.tensor_tensor(cc[:, 3, :], cc[:, 3, :], sg[:, k % RING3, :], ALU.add).then_inc(tap3, 1)

            def pooling(L, g):
                n = L * NPS + steps[g]
                w, wide = 2 << g, padded(AH)
                src, s = abuf[:, g, :], 0
                pool.wait_ge(moved, v_moved(L, "pool", g))
                for k in range(g + 1):
                    a, d = 2 * (1 << k) - 1, 1 << k
                    dst = win[:, k % 2, :]
                    pool.tensor_tensor(dst[:, a:wide], src[:, a:wide], src[:, a - d:wide - d], ALU.add).then_inc(pstep, 1)
                    s += 1
                    if k:
                        add3(L)
                    pool.wait_ge(pstep, n + s)
                    src = dst
                c = COUNTS + g * AH
                pool.tensor_tensor(src[:, AH:AH + w - 1], src[:, AH:AH + w - 1], pars[:, c:c + w - 1], ALU.mult).then_inc(pstep, 1)
                s += 1
                wait_alone(pstep, n + s)
                pool.tensor_scalar(src[:, AH:wide], src[:, AH:wide], 1.0 / w, None, ALU.mult).then_inc(pstep, 1)
                s += 1
                pool.wait_ge(pstep, n + s)
                a = abuf[:, g, :]
                pool.tensor_tensor(prompt(pmf), pad_prompt(src, AH, AH), pad_prompt(a, AH, AH), ALU.subtract).then_inc(pstep, 1)
                pool.tensor_tensor(sample(pmf), pad_sample(src, AH, AH), pad_sample(a, AH, AH), ALU.subtract).then_inc(pstep, 1)
                s += 2
                add3(L)
                wait_alone(pstep, n + s)
                pool.tensor_copy(y1_hi[:, g, :], pmf[:, :]).then_inc(pstep, 1)
                s += 1
                pool.wait_ge(pstep, n + s)
                pool.tensor_tensor(y1_lo[:, g, :], pmf[:, :], y1_hi[:, g, :].bitcast(F32), ALU.subtract).then_inc(pm_ready, 1)
                pool.wait_ge(pm_ready, L * WT + g + 1)

            pool.memset(ident[:, :], 0.0).then_inc(const_ready, 1)
            pool.memset(ga[:, 0, :], 0.0).then_inc(mid_ready, 2)
            pool.memset(ga[:, 1, :], 0.0).then_inc(halves_done, 4)
            pool.memset(gb[:, 1, :], 0.0).then_inc(stored, 16)
            pool.memset(sg[:, 0, :], 0.0).then_inc(pw_split, 2)
            pool.wait_ge(const_ready, 4)
            pool.affine_select(out=ident[:, :], in_=ident[:, :], compare_op=ALU.not_equal, fill=1.0, base=0,
                               pattern=[[-1, P]], channel_multiplier=1).then_inc(const_ready, 1)
            pool.wait_ge(const_ready, 5)
            pool.memset(gb[:, 0, :], 0.0).then_inc(const_ready, 1)
            with pool.Fori(0, DEPTH) as L:
                with pool.Fori(0, PAIRS["f1_up"]) as i:
                    hidden(L, "f1_up", 0, i)
                update_h(L, 0)
                wait_alone(side_in, L * 16 + 16)
                at = 0
                for buf, k in ((cbuf, CH), (sbuf, SH), (abuf, AH)):
                    pool.memset(buf[:, :, 0:k], 0.0).then_inc(hist_in, 1)
                    for t in range(WT):
                        cp = pool.tensor_copy(pad_sample(buf[:, t, :], k, 0, k),
                                              hist[:, at:at + NSEQ * k].rearrange("p (s r) -> p s r", r=k))
                        at += NSEQ * k
                    cp.then_inc(hist_in, 1)
                for t in range(WT):
                    pool.wait_ge(sig, v_sig(L, "glu", t))
                    for view in (0, 1):
                        dst = pad_sample(cbuf[:, t, :], CH, CH) if view else pad_prompt(cbuf[:, t, :], CH, CH)
                        pick = sample if view else prompt
                        op = pool.tensor_tensor(dst, pick(ga[:, t % 2, :]), pick(sg[:, t % 2, :]), ALU.mult)
                    op.then_inc(glu_ready, 1)
                for t in range(WT):
                    pool.wait_ge(moved, v_moved(L, "short", 2 * t + 1))
                    for view in (0, 1):
                        dst = pad_sample(sbuf[:, t, :], SH, SH) if view else pad_prompt(sbuf[:, t, :], SH, SH)
                        pick = sample if view else prompt
                        op = pool.tensor_tensor(dst, pick(ga[:, t % 2, :]), pick(gb[:, t % 2, :]), ALU.mult)
                    op.then_inc(cv_ready, 1)
                    add3(L, 2)
                pooling(L, 0)
                pooling(L, 1)
                pooling(L, 2)
                for t in range(WT):
                    wait_alone(c3, L * (2 * SK + 1) * WT + 2 * SK * WT + t + 1)
                    pool.tensor_copy(y0_hi[:, t, :], f[:, t, :]).then_inc(yb_step, 1)
                    pool.wait_ge(yb_step, L * WT + t + 1)
                    pool.tensor_tensor(y0_lo[:, t, :], f[:, t, :], y0_hi[:, t, :].bitcast(F32), ALU.subtract).then_inc(yb_ready, 1)
                    add3(L)
                pooling(L, 3)
                wait_alone(hist_in, L * 6 + 6)
                at = 0
                for buf, k in ((cbuf, CH), (sbuf, SH), (abuf, AH)):
                    n = WT * k
                    pool.tensor_copy(hist[:, at:at + n].rearrange("p (t r) -> p t r", r=k),
                                     buf[:, :, SEQ:SEQ + k]).then_inc(staged, 1)
                    at += n
                    for t in range(WT):
                        cp = pool.tensor_copy(hist[:, at:at + NSEQ * k].rearrange("p (s r) -> p s r", r=k),
                                              pad_sample(buf[:, t, :], k, SLEN, k))
                        at += NSEQ * k
                    cp.then_inc(staged, 1)
                    add3(L, 2)
                add3(L, 2)
                def add_branch(b):
                    for m in range(DT):
                        pool.wait_ge(moved, v_moved(L, f"out{b}", m))
                        if b == 2:
                            pool.wait_ge(added, L * 2 * DT + m + 1)
                        pool.tensor_tensor(f[:, m, :], f[:, m, :], gb[:, m % 2, :], ALU.add).then_inc(added, 1)

                for t in range(1, WT):
                    if t == 1:
                        pool.wait_ge(tap, (L + 1) * NTAP)
                        pool.wait_ge(tap3, (L + 1) * (CK - 1))
                    else:
                        pool.wait_ge(ln_sum, L * (WT - 1) + t - 1)
                    pool.tensor_tensor(pmf[:, :], cc[:, 0, :] if t == 1 else pmf[:, :], cc[:, t, :], ALU.add).then_inc(ln_sum, 1)
                add_branch(1)
                for t in range(WT):
                    n = L * WT * 2 + 2 * t
                    pool.wait_ge(ln_step, L * 3 * WT + 2 * WT + t + 1)
                    pool.tensor_tensor(pmf[:, :], cc[:, t, :], sg[:, t % 2, :], ALU.mult).then_inc(yc_step, 1)
                    wait_alone(yc_step, n + 1)
                    pool.tensor_copy(y1_hi[:, t, :], pmf[:, :]).then_inc(yc_step, 1)
                    pool.wait_ge(yc_step, n + 2)
                    pool.tensor_tensor(y1_lo[:, t, :], pmf[:, :], y1_hi[:, t, :].bitcast(F32), ALU.subtract).then_inc(yc_ready, 1)
                    pool.wait_ge(yc_ready, L * WT + t + 1)
                add_branch(2)
                update_h(L, 1)
                with pool.Fori(0, PAIRS["f2_up"]) as i:
                    hidden(L, "f2_up", 1, i)
                update_h(L, 2)
                update_h(L, 3)


def _tiles(w, rows, cols):
    w = w.reshape(*w.shape[:-2], rows, P, cols, P)
    return w.swapaxes(-3, -2)


def _slots(halves):
    import numpy as np
    d, n, t = halves.shape[:3]
    a = halves.reshape(d, n // 2, 2, t, P, P).transpose(0, 1, 4, 2, 3, 5)
    return np.ascontiguousarray(a.reshape(d * (n // 2), P, 2 * t * P))


def _layout(i):
    import numpy as np
    i = {k: np.asarray(v) for k, v in i.items()}
    st = {}
    for n in ("1", "2"):
        g = _tiles(i[f"w_f{n}_gate"], DT, FT).swapaxes(1, 2)
        u = _tiles(i[f"w_f{n}_up"], DT, FT).swapaxes(1, 2)
        st[f"f{n}_up"] = _slots(np.stack([g, u], 2).reshape(DEPTH, 2 * FT, DT, P, P))
        d = _tiles(i[f"w_f{n}_down"], FT, DT).swapaxes(1, 2)
        st[f"f{n}_dn"] = _slots(d.reshape(DEPTH, 2 * DT, FT // 2, P, P))
    z = _tiles(i["w_in"], DT, 6 * WT + 3 * DT).swapaxes(1, 2)
    blk = lambda n: z[:, n * WT:(n + 1) * WT]
    pairs = lambda a, b: np.stack([a, b], 2).reshape(DEPTH, 2 * WT, DT, P, P)
    gate = lambda n: z[:, 6 * WT + n * DT:6 * WT + (n + 1) * DT]
    st["glu"], st["short"] = _slots(pairs(blk(4), blk(5))), _slots(pairs(blk(1), blk(3)))
    st["pool"], st["bgate"] = _slots(blk(0)), _slots(blk(2))
    for n, (b, w) in enumerate(((1, "w_sc_out"), (0, "w_pool_out"), (2, "w_cf_out"))):
        st[f"gate{n}"] = _slots(gate(b))
        o = _tiles(i[w], WT, DT)
        o = o.reshape(DEPTH, WT, 4, 2, P, P).transpose(0, 2, 1, 3, 4, 5)
        st[f"out{n}"] = _slots(o.reshape(DEPTH, 4, 2 * WT, P, P))
    st["wo"] = _slots(_tiles(i["w_o"], DT, DT).swapaxes(1, 2))
    st["pg"] = _slots(_tiles(i["w_ple_gate"], DT, DT).swapaxes(1, 2))
    o = _tiles(i["w_ple_proj"], PT, DT).reshape(DEPTH, PT, 4, 2, P, P).transpose(0, 2, 1, 3, 4, 5)
    st["pp"] = _slots(o.reshape(DEPTH, 4, 2 * PT, P, P))

    def cols(a):
        return a.reshape(-1, P).T

    nxt = np.concatenate([i["g_f1_pre"][1:], i["g_final"][None]])
    blocks = []
    for l in range(DEPTH):
        src = dict({n: i[n][l] for n, _ in _COLS if n != "g_next"}, g_next=nxt[l])
        blocks += [cols(src[n]) for n, _ in _COLS]
    blocks.append(cols(i["g_f1_pre"][0]))
    table = np.zeros((WT, AH), np.float32)
    for g in range(WT):
        for t in range((2 << g) - 1):
            table[g, t] = (2 << g) / (t + 1)
    blocks.append(np.broadcast_to(table.reshape(1, -1), (P, WT * AH)))
    par = np.concatenate(blocks, 1)

    def feature_major(prompt, sample, k):
        a = np.concatenate([prompt.reshape(SEQ, -1), sample.reshape(NSEQ * SLEN, -1)])
        return a.T.reshape(k, P, T).transpose(1, 0, 2).reshape(P, k * T)

    x = feature_major(i["x_prompt"], i["x_sample"], DT)
    p = np.stack([feature_major(i["p_prompt"][l], i["p_sample"][l], PT) for l in range(DEPTH)])
    side = []
    for n in ("state_cconv", "state_sconv", "state_pool"):
        s = i[n]
        s = s.reshape(DEPTH, NSEQ, s.shape[2], WT, P).transpose(0, 4, 3, 1, 2)
        side.append(s.reshape(DEPTH, P, -1))
    side = np.concatenate(side, 2)
    pw = i["pool_w"].transpose(0, 2, 1, 3).reshape(DEPTH, P, WT * P)
    arrays = dict(x=x, par=par, side=side, early=np.concatenate([p, pw], 2), **{f"w_{k}": v for k, v in st.items()})
    return {f"in_{k}": np.ascontiguousarray(v) for k, v in arrays.items()}


def kernel(**inputs):
    import numpy as np
    import concourse.bacc as bacc
    from concourse.bass_utils import run_bass_kernel_spmd as run

    arrays = _layout(inputs)
    nc = bacc.Bacc("TRN2", target_bir_lowering=False, num_devices=1)
    a = {n: nc.dram_tensor(n, v.shape, F32, kind="ExternalInput").ap() for n, v in arrays.items()}
    y = nc.dram_tensor("out_y", (P, DT * T), F32, kind="ExternalOutput").ap()
    states = nc.dram_tensor("out_states", (DEPTH, P, sum(STATES)), F32, kind="ExternalOutput").ap()
    trunk(nc, a["in_x"], a["in_par"], a["in_side"], a["in_early"],
          {n: a[f"in_w_{n}"] for n, _, _ in PHASES}, y, states)
    r = run(nc, [arrays], core_ids=[0]).results[0]

    yt = r["out_y"].reshape(P, DT, T).transpose(2, 1, 0).reshape(T, D)
    got = [yt[:SEQ].reshape(1, SEQ, D), yt[SEQ:].reshape(NSEQ, SLEN, D)]
    s, at, new = r["out_states"], 0, {}
    for name, k in (("c", CH), ("s", SH), ("a", AH)):
        n = WT * k
        new[name, 0] = s[:, :, at:at + n].reshape(DEPTH, P, WT, k).transpose(0, 3, 2, 1).reshape(DEPTH, 1, k, W)
        at += n
        n = WT * NSEQ * k
        new[name, 1] = s[:, :, at:at + n].reshape(DEPTH, P, WT, NSEQ, k).transpose(0, 3, 4, 2, 1).reshape(DEPTH, NSEQ, k, W)
        at += n
    got += [new[n, i] for i in range(2) for n in "asc"]
    return tuple(np.ascontiguousarray(g) for g in got)
```

```python
from contextlib import ExitStack

import concourse.bass as bass
from concourse import mybir

F32 = mybir.dt.float32
F32R = mybir.dt.float32r
ALU = mybir.AluOpType
ACT = mybir.ActivationFunctionType

P = 128
DEPTH = 2
D = 1024
DFF = 2816
W = 512
PLE = 256
SEQ, NSEQ, SLEN = 256, 8, 8
T = SEQ + NSEQ * SLEN
TPAD = 384
DT, FT, WT, PT = D // P, DFF // P, W // P, PLE // P
EPS = 1e-6
CK, SK, WMAX = 31, 3, 16
CH, SH, AH = CK - 1, SK - 1, WMAX - 1


def padded(h):
    return h + SEQ + NSEQ * (h + SLEN)


PHASES = [("f1_up", FT // 2, DT), ("f1_dn", DT // 2, FT // 2),
          ("glu", 2, DT), ("short", 2, DT), ("pool", 1, DT), ("bgate", 1, DT),
          ("gate0", 2, DT), ("out0", 1, 2 * WT), ("gate1", 2, DT), ("out1", 1, 2 * WT),
          ("gate2", 2, DT), ("out2", 1, 2 * WT), ("wo", 2, DT),
          ("f2_up", FT // 2, DT), ("f2_dn", DT // 2, FT // 2),
          ("pg", 2, DT), ("pp", 1, 2 * PT)]
PAIRS = {n: p for n, p, _ in PHASES}
HALF = {n: t * P for n, _, t in PHASES}
PAIR0 = {n: sum(p for _, p, _ in PHASES[:i]) for i, (n, _, _) in enumerate(PHASES)}
NPAIR = sum(PAIRS.values())
NHALF = 4 * NPAIR
HMAX = max(HALF.values())

_MOVED = [("f1_up", 4 * PAIRS["f1_up"]), ("glu", 8), ("short", 8), ("pool", 4), ("bgate", 4),
          ("gate0", 8), ("out0", 8), ("gate1", 4), ("poolw", 4), ("gate1b", 4), ("out1", 8),
          ("gate2", 8), ("out2", 8), ("f2_up", 4 * PAIRS["f2_up"]), ("pg", 8), ("pp", 8)]
MOVED0 = {n: sum(k for _, k in _MOVED[:i]) for i, (n, _) in enumerate(_MOVED)}
NMOVED = sum(k for _, k in _MOVED)

_SQ = [("post1", DT), ("pre1", DT), ("ln", WT), ("post2", DT), ("pre2", DT),
       ("post3", DT), ("pre3", DT), ("post4", DT), ("pre4", DT)]
SQ0 = {n: sum(k for _, k in _SQ[:i]) for i, (n, _) in enumerate(_SQ)}
NSQ = sum(k for _, k in _SQ)
STAT = {n: i for i, (n, _) in enumerate(_SQ)}
NSTAT = len(_SQ)
X0 = {"b1": 0, "m": DT, "b2": 2 * DT, "b3": 3 * DT, "b4": 4 * DT}
NX = 5 * DT
SIG0 = {"f1": 0, "glu": FT, "gate0": FT + WT, "gate1": FT + WT + DT, "gate2": FT + WT + 2 * DT,
        "f2": FT + WT + 3 * DT, "pg": 2 * FT + WT + 3 * DT}
NSIG = 2 * FT + WT + 4 * DT

TAPS = [(k, t) for k in range(CK) for t in (0, 1)]
TAPS[8:8] = [(0, 3)]
TAPS += [(k, 2) for k in range(CK)]
TAP_AT = {u: i for i, u in enumerate(TAPS)}
NTAP = 2 * len(TAPS)
RING3 = 4

_COLS = [("g_f1_post", DT), ("g_mix_pre", DT), ("g_mix_post", DT), ("g_f2_pre", DT), ("g_f2_post", DT),
         ("g_ple_pre", DT), ("g_ple_post", DT), ("g_next", DT), ("pool_scale", WT), ("cf_conv_b", WT),
         ("cf_ln_g", WT), ("cf_ln_b", WT), ("sc_conv", SK * WT), ("cf_conv", CK * WT)]
COL = {n: sum(k for _, k in _COLS[:i]) for i, (n, _) in enumerate(_COLS)}
NCOL = sum(k for _, k in _COLS)
FIRST_G = DEPTH * NCOL
COUNTS = FIRST_G + DT
NPAR = COUNTS + WT * AH

HISTORY = [WT * NSEQ * k for k in (CH, SH, AH)]
STATES = [WT * (NSEQ + 1) * k for k in (CH, SH, AH)]


def trunk(nc, x, par, side, early, streams, y, states):
    with ExitStack() as ctx:
        def sb(name, cols, dt=F32, where=ctx):
            return where.enter_context(nc.sbuf_tensor(name, [P, *cols], dt))

        def sem(name):
            return ctx.enter_context(nc.semaphore(name))

        raw = sb("raw", [4, HMAX])
        w_hi_sb = sb("w_hi_sb", [4, HMAX], F32R)
        w_lo_sb = sb("w_lo_sb", [4, HMAX], F32R)
        h = sb("h", [DT, T])
        x_hi = sb("x_hi", [DT, T], F32R)
        x_lo = sb("x_lo", [DT, T], F32R)
        f = sb("f", [DT, T])
        ga = sb("ga", [2, T])
        gb = sb("gb", [2, T])
        sg = sb("sg", [RING3, T])
        sq = sb("sq", [2, T])
        ssq = sb("ssq", [TPAD])
        rb = sb("rb", [T])
        pars = sb("pars", [NPAR])
        cur = sb("cur", [NCOL])
        ones = sb("ones", [P])
        meanw = sb("meanw", [P])
        ident = sb("ident", [P])
        eps = sb("eps", [2])
        root = sb("root", [3])
        rinv = sb("rinv", [3])
        hist = sb("hist", [sum(STATES)])
        p_raw, pw_raw = hist[:, 0:PT * T], hist[:, PT * T:PT * T + WT * P]
        p_hi = sb("p_hi", [PT * T], F32R)
        p_lo = sb("p_lo", [PT * T], F32R)
        pw_hi = sb("pw_hi", [WT * P], F32R)
        pw_lo = sb("pw_lo", [WT * P], F32R)
        with ExitStack() as ffn:
            mid_hi = sb("mid_hi", [FT, T], F32R, ffn)
            mid_lo = sb("mid_lo", [FT, T], F32R, ffn)
        cbuf = sb("cbuf", [WT, padded(CH)])
        sbuf = sb("sbuf", [WT, padded(SH)])
        abuf = sb("abuf", [WT, padded(AH)])
        bg = sb("bg", [WT, T])
        cc = sb("cc", [WT, T])
        y0_hi = sb("y0_hi", [WT, T], F32R)
        y0_lo = sb("y0_lo", [WT, T], F32R)
        y1_hi = sb("y1_hi", [WT, T], F32R)
        y1_lo = sb("y1_lo", [WT, T], F32R)
        gate = sb("gate", [DT, T])
        win = sb("win", [2, padded(AH)])
        pmf = sb("pmf", [T])

        ps = ctx.enter_context(nc.psum_tensor("ps", [P, 8, 512], F32))
        STATB = 7
        bc = ps[:, STATB, 64:64 + T]
        FIRST_BANKS = (4, 5, 6, 3)

        loaded = sem("loaded")
        loaded_rest = sem("loaded_rest")
        raw_in = [sem("raw_in0"), sem("raw_in1")]
        early_in = sem("early_in")
        side_in = sem("side_in")
        const_ready = sem("const_ready")
        w_hi = sem("w_hi")
        w_lo = sem("w_lo")
        halves_done = sem("halves_done")
        moved = sem("moved")
        squared = sem("squared")
        f_out = sem("f_out")
        summed = sem("summed")
        stat_full = sem("stat_full")
        root_ready = sem("root_ready")
        rinv_ready = sem("rinv_ready")
        bc_full = sem("bc_full")
        rb_ready = sem("rb_ready")
        par_ready = sem("par_ready")
        step_t = sem("step_t")
        h_ready = sem("h_ready")
        xhi_ready = sem("xhi_ready")
        x_ready = sem("x_ready")
        sig = sem("sig")
        swi = sem("swi")
        mid_ready = sem("mid_ready")
        glu_ready = sem("glu_ready")
        cv_ready = sem("cv_ready")
        tap = sem("tap")
        prod3 = sem("prod3")
        tap3 = sem("tap3")
        c3 = sem("c3")
        pstep = sem("pstep")
        pm_ready = sem("pm_ready")
        pw_split = sem("pw_split")
        pw_hi_ready = sem("pw_hi_ready")
        poolw_done = sem("poolw_done")
        ya_hi = sem("ya_hi")
        yb_ready = sem("yb_ready")
        yb_step = sem("yb_step")
        silu_even = sem("silu_even")
        silu_odd = sem("silu_odd")
        yc_hi = sem("yc_hi")
        yc_even = sem("yc_even")
        yc_odd = sem("yc_odd")
        added = sem("added")
        ln_sum = sem("ln_sum")
        ln_mean = sem("ln_mean")
        ln_step = sem("ln_step")
        ln_sig = sem("ln_sig")
        ln_y = sem("ln_y")
        hist_in = sem("hist_in")
        staged = sem("staged")
        stored = sem("stored")
        y_ready = sem("y_ready")
        tick = sem("tick")

        block = ctx.enter_context(nc.Block())

        def v_half(L, ph, pair, j):
            return L * NHALF + 4 * (PAIR0[ph] + pair) + j + 1

        def v_moved(L, ph, n):
            return L * NMOVED + MOVED0[ph] + n + 5

        def v_sq(L, name, m):
            return L * NSQ + (m + 1 if name is None else DT + SQ0[name] + m + 1)

        def v_f(L, n, m):
            return (L * 4 + n) * DT + m + 3

        def v_stat(L, name):
            return L * NSTAT + (1 if name is None else STAT[name] + 2)

        def v_x(L, b, m):
            return DT + L * NX + X0[b] + m + 1

        def v_sig(L, name, m):
            return L * NSIG + SIG0[name] + m + 1

        def prompt(t):
            return t[:, 0:SEQ]

        def sample(t):
            return t[:, SEQ:T].rearrange("p (s t) -> p s t", t=SLEN)

        def pad_prompt(t, hist_rows, at):
            return t[:, at:at + SEQ]

        def pad_sample(t, hist_rows, at, n=SLEN):
            return t[:, hist_rows + SEQ:].rearrange("p (s w) -> p s w", w=hist_rows + SLEN)[:, :, at:at + n]

        def part(i, buf, hist_rows, tile, at):
            row = buf[:, tile, :]
            return pad_sample(row, hist_rows, at) if i else pad_prompt(row, hist_rows, at)

        def tok(i, row):
            return sample(row) if i else prompt(row)

        @block.sync
        def _(sp):
            sp.dma_start(pars[:, :], par).then_inc(loaded, 16)
            for c in range(2):
                k = slice(c * (DT // 2), (c + 1) * (DT // 2))
                sp.dma_start(h[:, k, :], x.rearrange("p (k t) -> p k t", t=T)[:, k, :]).then_inc((loaded, loaded_rest)[c], 16)

            def load_pair(L, ph, pair, layer=None):
                src = streams[ph]
                for s in range(2):
                    sp.wait_ge(w_lo, L * NHALF + 4 * (PAIR0[ph] + pair) + 2 * s + 2)
                    row = ((L if layer is None else layer) * PAIRS[ph] + pair) * 2 + s
                    sp.dma_start(raw[:, 2 * s:2 * s + 2, 0:HALF[ph]],
                                 src[bass.ds(row, 1), :, :].rearrange("a p (h n) -> (a p) h n", h=2)
                                 ).then_inc(raw_in[s], 16)

            load_pair(0, "f1_up", 0)
            with sp.Fori(0, DEPTH) as L:
                sp.wait_ge(stored, L * 16 + 16)
                sp.sem_inc(tick, 1)
                sp.wait_ge(pw_split, L * 2 + 2)
                sp.dma_start(hist[:, 0:PT * T + WT * P], early[bass.ds(L, 1), :, :].rearrange("a p n -> (a p) n")).then_inc(early_in, 16)
                for ph, n, _ in PHASES:
                    if ph == "f1_dn":
                        sp.wait_ge(pw_split, L * 2 + 4)
                        sp.dma_start(hist[:, 0:sum(HISTORY)],
                                     side[bass.ds(L, 1), :, :].rearrange("a p n -> (a p) n")).then_inc(side_in, 16)
                    if n > 2:
                        with sp.Fori(1 if ph == "f1_up" else 0, n) as i:
                            load_pair(L, ph, i)
                    else:
                        for i in range(n):
                            load_pair(L, ph, i)
                load_pair(L + 1, "f1_up", 0, layer=DEPTH - 1)

        @block.tensor
        def _(pe):
            def products(out, w, n, rhs_hi, rhs_lo, start, stop):
                whi, wlo = w_hi_sb[:, w, n:n + P], w_lo_sb[:, w, n:n + P]
                pe.matmul(out, whi, rhs_hi, start=start, stop=False, skip_group_check=True)
                pe.matmul(out, whi, rhs_lo, start=False, stop=False, skip_group_check=True)
                return pe.matmul(out, wlo, rhs_hi, start=False, stop=stop, skip_group_check=True)

            def wait_half(L, ph, pair, j):
                pe.wait_ge(w_lo, v_half(L, ph, pair, j) + 4)

            def pair_of_x(L, ph, pair, moved0, between={}, stat=None, banks_free=False, last=None, xl=None):
                for j in range(4):
                    wait_half(L, ph, pair, j)
                    if j < 3 and banks_free:
                        pass
                    elif j == 3 and last is not None:
                        pe.wait_ge(moved, last)
                    else:
                        pe.wait_ge(moved, moved0 + j - 4)
                    for k in range(DT):
                        if xl is not None and j == 0:
                            pe.wait_ge(x_ready, xl + k + 1)
                        mm = products(ps[:, j, 0:T], j, k * P, x_hi[:, k, :], x_lo[:, k, :], k == 0, k == DT - 1)
                    mm.then_inc(halves_done, 1)
                    if j in between:
                        between[j](L, stat)

            def first_pair(L, ph, xl, stat):
                half = DT // 2
                for j in range(4):
                    wait_half(L, ph, 0, j)
                for k in range(half):
                    pe.wait_ge(x_ready, xl + k + 1)
                    for j in range(4):
                        products(ps[:, FIRST_BANKS[j], 0:T], j, k * P, x_hi[:, k, :], x_lo[:, k, :], k == 0, False)
                for j in range(4):
                    for k in range(half, DT):
                        if j == 0:
                            pe.wait_ge(x_ready, xl + k + 1)
                        mm = products(ps[:, FIRST_BANKS[j], 0:T], j, k * P, x_hi[:, k, :], x_lo[:, k, :], False, k == DT - 1)
                    mm.then_inc(halves_done, 1)
                    if j == 1:
                        sums(L, stat)
                    if j == 2:
                        spread(L, stat)

            def sums(L, name):
                n = WT if name == "ln" else DT
                pe.wait_ge(summed, v_sq(L, name, n - 1))
                for t in range(3):
                    mm = pe.matmul(ps[:, STATB, t:t + 1], ssq[:, t * P:(t + 1) * P], ones[:, 0:1], start=True, stop=True)
                mm.then_inc(stat_full, 1)

            def spread(L, name):
                pe.wait_ge(rinv_ready, v_stat(L, name))
                for t in range(3):
                    n = min(P, T - t * P)
                    mm = pe.matmul(ps[:, STATB, 64 + t * P:64 + t * P + n], rinv[:, t:t + 1].broadcast_to([P, P]),
                                   ident[:, 0:n], start=True, stop=True)
                mm.then_inc(bc_full, 1)

            def down(L, ph, up, which, n):
                with pe.Fori(0, PAIRS[ph]) as i:
                    pe.wait_ge(moved, v_moved(L, up, 4 * PAIRS[up] - 3))
                    for j in range(4):
                        g, c = j % 2, j // 2
                        wait_half(L, ph, i, j)
                        if c == 0:
                            pe.wait_ge(f_out, v_f(L, n, 2 * i + g - 2))
                        pe.wait_ge(mid_ready, L * 2 * FT + which * FT + 2 + (c + 1) * (FT // 2))
                        for k in range(FT // 2):
                            m = c * (FT // 2) + k
                            mm = products(ps[:, g, 0:T], j, k * P, mid_hi[:, m, :], mid_lo[:, m, :], m == 0, m == FT - 1)
                        mm.then_inc(halves_done, 1)

            def narrow(L, ph, kt, rhs_hi, rhs_lo):
                for j in range(4):
                    wait_half(L, ph, 0, j)
                    for c in range(2):
                        q = 2 * j + c
                        pe.wait_ge(moved, v_moved(L, ph, q) - 4)
                        for k in range(kt):
                            mm = products(ps[:, q % 4, 0:T], j, k * 2 * P + c * P, rhs_hi[:, k, :], rhs_lo[:, k, :],
                                          k == 0, k == kt - 1)
                    mm.then_inc(halves_done, 1)

            pe.wait_ge(const_ready, 6)
            with pe.Fori(0, DEPTH) as L:
                first_pair(L, "f1_up", L * NX, None)
                pair_of_x(L, "f1_up", 1, v_moved(L, "f1_up", 4), banks_free=True)
                with pe.Fori(2, PAIRS["f1_up"]) as i:
                    pair_of_x(L, "f1_up", i, v_moved(L, "f1_up", 4 * i))
                down(L, "f1_dn", "f1_up", 0, 0)
                sums(L, "post1")
                spread(L, "post1")
                first_pair(L, "glu", v_x(L, "b1", -1), "pre1")
                pair_of_x(L, "glu", 1, v_moved(L, "glu", 4), banks_free=True)
                for ph in ("short", "pool", "bgate", "gate0"):
                    for i in range(PAIRS[ph]):
                        pair_of_x(L, ph, i, v_moved(L, ph, 4 * i))
                pe.wait_ge(yb_ready, L * WT + WT)
                narrow(L, "out0", WT, y0_hi, y0_lo)
                pair_of_x(L, "gate1", 0, v_moved(L, "gate1", 0))
                pe.wait_ge(pw_split, L * 2 + 4)
                for g in range(WT):
                    pe.wait_ge(pm_ready, L * WT + g + 1)
                    if g == 3:
                        pe.wait_ge(moved, v_moved(L, "gate1", 3))
                    out = ps[:, FIRST_BANKS[g], 0:T]
                    whi, wlo = pw_hi[:, g * P:(g + 1) * P], pw_lo[:, g * P:(g + 1) * P]
                    pe.matmul(out, whi, y1_hi[:, g, :], start=True, stop=False)
                    pe.matmul(out, whi, y1_lo[:, g, :], start=False, stop=False)
                    pe.matmul(out, wlo, y1_hi[:, g, :], start=False, stop=True).then_inc(poolw_done, 1)
                pair_of_x(L, "gate1", 1, v_moved(L, "gate1", 4), last=v_moved(L, "poolw", 3))
                pe.wait_ge(moved, v_moved(L, "poolw", WT - 1))
                narrow(L, "out1", WT, y0_hi, y0_lo)
                pe.wait_ge(ln_sum, L * (WT - 1) + WT - 1)
                pe.matmul(bc, meanw[:, :], pmf[:, :], start=True, stop=True).then_inc(ln_mean, 1)
                pair_of_x(L, "gate2", 0, v_moved(L, "gate2", 0), {2: sums, 3: spread}, "ln")
                pair_of_x(L, "gate2", 1, v_moved(L, "gate2", 4))
                pe.wait_ge(yc_even, L * 2 + 2)
                pe.wait_ge(yc_odd, L * 2 + 2)
                narrow(L, "out2", WT, y1_hi, y1_lo)
                pair_of_x(L, "wo", 0, v_moved(L, "out2", 8), xl=v_x(L, "m", -1))
                for j in range(4):
                    wait_half(L, "wo", 1, j)
                    pe.wait_ge(f_out, v_f(L, 1, j))
                    for k in range(DT):
                        mm = products(ps[:, j, 0:T], j, k * P, x_hi[:, k, :], x_lo[:, k, :], k == 0, k == DT - 1)
                    mm.then_inc(halves_done, 1)
                sums(L, "post2")
                spread(L, "post2")
                first_pair(L, "f2_up", v_x(L, "b2", -1), "pre2")
                pair_of_x(L, "f2_up", 1, v_moved(L, "f2_up", 4), banks_free=True)
                with pe.Fori(2, PAIRS["f2_up"]) as i:
                    pair_of_x(L, "f2_up", i, v_moved(L, "f2_up", 4 * i))
                down(L, "f2_dn", "f2_up", 1, 2)
                sums(L, "post3")
                spread(L, "post3")
                first_pair(L, "pg", v_x(L, "b3", -1), "pre3")
                pair_of_x(L, "pg", 1, v_moved(L, "pg", 4), banks_free=True)
                narrow(L, "pp", PT, p_hi[:, :].rearrange("p (k t) -> p k t", t=T),
                       p_lo[:, :].rearrange("p (k t) -> p k t", t=T))
                sums(L, "post4")
                spread(L, "post4")
            sums(DEPTH, None)
            spread(DEPTH, None)

        @block.scalar
        def _(act):
            def split(L, ph, pair, j):
                if j % 2 == 0:
                    act.wait_ge(raw_in[j // 2], (L * NPAIR + PAIR0[ph] + pair + 1) * 16)
                act.wait_ge(halves_done, v_half(L, ph, pair, j))
                n = HALF[ph]
                act.activation(w_hi_sb[:, j, 0:n], raw[:, j, 0:n], ACT.Copy).then_inc(w_hi, 1)

            def square(src, L, name, m, par):
                act.wait_ge(summed, v_sq(L, name, m - 2))
                act.activation(sq[:, par, :], src, ACT.Square).then_inc(squared, 1)

            def finish_root(L, name):
                act.wait_ge(stat_full, v_stat(L, name))
                twice = 4.0 if name in ("post1", "post3") else 1.0
                width = W if name == "ln" else D
                e = eps[:, 1:2] if twice == 4.0 else eps[:, 0:1]
                act.activation(root[:, :], ps[:, STATB, 0:3], ACT.Sqrt, bias=e, scale=twice / width).then_inc(root_ready, 1)

            def keep_rb(L, name):
                act.wait_ge(bc_full, v_stat(L, name))
                act.activation(rb[:, :], bc, ACT.Copy).then_inc(rb_ready, 1)

            def output(src, L, name, m, par, gain):
                square(src, L, name, m, par)
                act.activation(f[:, bass.ds(m, 1), :] if not isinstance(m, int) else f[:, m, :], src, ACT.Copy,
                               scale=cur[:, bass.ds(COL[gain] + m, 1)] if not isinstance(m, int)
                               else cur[:, COL[gain] + m:COL[gain] + m + 1]).then_inc(f_out, 1)

            def chase(L, b, gain, name, n):
                for m in range(DT):
                    act.wait_ge(h_ready, L * 4 * DT + n * DT + m + 1)
                    act.activation(x_hi[:, m, :], h[:, m, :], ACT.Copy,
                                   scale=cur[:, COL[gain] + m:COL[gain] + m + 1]).then_inc(xhi_ready, 1)
                    square(h[:, m, :], L, name, m, m % 2)

            def boundary(L, n, post, pre, gain):
                finish_root(L, post)
                chase(L, None, gain, pre, n)
                if n < 3:
                    finish_root(L, pre)
                    act.preload_act_table(ACT.Sigmoid)
                    keep_rb(L, pre)

            def sigmoid(out, src, L, ph, n):
                act.wait_ge(moved, v_moved(L, ph, n))
                act.activation(out, src, ACT.Sigmoid).then_inc(sig, 1)

            def up_step(L, ph, nxt, pair, prev_pair):
                for j in range(4):
                    split(L, nxt, pair, j)
                    if j % 2 == 1:
                        sigmoid(sg[:, j // 2, :], ga[:, j // 2, :], L, ph, 4 * prev_pair + j - 1)

            def down_step(L, ph, nxt, pair, prev_pair, name, gain):
                for j in range(4):
                    if j >= 2:
                        act.wait_ge(halves_done, v_half(L, ph, prev_pair, j) + 4)
                        output(ps[:, j % 2, 0:T], L, name, 2 * prev_pair + j % 2, j % 2, gain)
                    split(L, nxt, pair, j)

            def ffn(L, up, dn, after, name, gain):
                with act.Fori(1, PAIRS[up]) as i:
                    up_step(L, up, up, i, i - 1)
                up_step(L, up, dn, 0, PAIRS[up] - 1)
                act.preload_act_table(ACT.Sqrt)
                with act.Fori(1, PAIRS[dn]) as i:
                    down_step(L, dn, dn, i, i - 1, name, gain)
                down_step(L, dn, after, 0, PAIRS[dn] - 1, name, gain)

            tap_of_3 = iter(range(1, CK))

            def product3(L):
                k = next(tap_of_3, None)
                if k is None:
                    return
                if k == 1:
                    act.wait_ge(hist_in, L * 6 + 2)
                    act.wait_ge(glu_ready, L * WT + WT)
                if k > RING3:
                    act.wait_ge(tap3, L * (CK - 1) + k - RING3)
                c = COL["cf_conv"] + k * WT + 3
                for i in range(2):
                    op = act.activation(tok(i, sg[:, k % RING3, :]), part(i, cbuf, CH, 3, k), ACT.Copy, scale=cur[:, c:c + 1])
                op.then_inc(prod3, 1)

            def gates(L, ph, group, name, m0, nxt, pair):
                for j in range(4):
                    split(L, nxt, pair, j)
                    sigmoid(gate[:, m0 + j, :], ga[:, j % 2, :], L, group, j)
                    if ph != "pg":
                        product3(L)

            act.wait_ge(const_ready, 6)
            act.preload_act_table(ACT.Sqrt)
            for m in range(DT):
                if m == 0:
                    act.wait_ge(loaded, 32)
                if m == DT // 2:
                    act.wait_ge(loaded_rest, 16)
                act.activation(x_hi[:, m, :], h[:, m, :], ACT.Copy,
                               scale=pars[:, FIRST_G + m:FIRST_G + m + 1]).then_inc(xhi_ready, 1)
                if m >= 2:
                    act.wait_ge(summed, m - 1)
                act.activation(sq[:, m % 2, :], h[:, m, :], ACT.Square).then_inc(squared, 1)
            for j in range(4):
                split(0, "f1_up", 0, j)
            with act.Fori(0, DEPTH) as L:
                finish_root(L, None)
                act.preload_act_table(ACT.Sigmoid)
                keep_rb(L, None)
                act.wait_ge(early_in, L * 16 + 16)
                act.activation(p_hi[:, :], p_raw, ACT.Copy).then_inc(pw_hi_ready, 1)
                act.activation(pw_hi[:, :], pw_raw, ACT.Copy).then_inc(pw_hi_ready, 1)
                act.wait_ge(par_ready, L + 1)
                ffn(L, "f1_up", "f1_dn", "glu", "post1", "g_f1_post")
                boundary(L, 0, "post1", "pre1", "g_mix_pre")
                for pair in range(2):
                    nxt = [("glu", 1), ("short", 0)][pair]
                    for j in range(4):
                        split(L, nxt[0], nxt[1], j)
                        if j % 2 == 1:
                            act.wait_ge(moved, v_moved(L, "glu", 4 * pair + j))
                            act.activation(sg[:, j // 2, :], gb[:, j // 2, :], ACT.Sigmoid).then_inc(sig, 1)
                for nxt in (("short", 1), ("pool", 0), ("bgate", 0), ("gate0", 0)):
                    for j in range(4):
                        split(L, *nxt, j)
                        product3(L)
                gates(L, "gate0", "gate0", "gate0", 0, "gate0", 1)
                for j in range(4):
                    split(L, "out0", 0, j)
                    sigmoid(gate[:, 4 + j, :], ga[:, j % 2, :], L, "gate0", 4 + j)
                    product3(L)
                for j in range(4):
                    split(L, "gate1", 0, j)
                    product3(L)
                for j in range(4):
                    split(L, "gate1", 1, j)
                    sigmoid(gate[:, j, :], ga[:, j % 2, :], L, "gate1", j)
                    product3(L)
                for g in range(WT):
                    act.wait_ge(poolw_done, L * WT + g + 1)
                    act.activation(y0_hi[:, g, :], ps[:, FIRST_BANKS[g], 0:T], ACT.Copy,
                                   scale=cur[:, COL["pool_scale"] + g:COL["pool_scale"] + g + 1]).then_inc(ya_hi, 1)
                for j in range(4):
                    split(L, "out1", 0, j)
                    sigmoid(gate[:, 4 + j, :], ga[:, j % 2, :], L, "gate1b", j)
                for j in range(4):
                    split(L, "gate2", 0, j)
                for j in range(4):
                    split(L, "gate2", 1, j)
                    if j < 2:
                        for t in (2 * j, 2 * j + 1):
                            act.wait_ge(ln_step, L * 3 * WT + t + 1)
                            square(cc[:, t, :], L, "ln", t, t % 2)
                    sigmoid(gate[:, j, :], ga[:, j % 2, :], L, "gate2", j)
                    if j == 2:
                        act.preload_act_table(ACT.Sqrt)
                        finish_root(L, "ln")
                        act.preload_act_table(ACT.Sigmoid)
                for t in range(WT):
                    act.wait_ge(ln_step, L * 3 * WT + WT + t + 1)
                    act.activation(sg[:, t, :], cc[:, t, :], ACT.Sigmoid,
                                   scale=cur[:, COL["cf_ln_g"] + t:COL["cf_ln_g"] + t + 1],
                                   bias=cur[:, COL["cf_ln_b"] + t:COL["cf_ln_b"] + t + 1]).then_inc(ln_sig, 1)
                for j in range(4):
                    split(L, "out2", 0, j)
                    sigmoid(gate[:, 4 + j, :], ga[:, j % 2, :], L, "gate2", 4 + j)
                    if j < 2:
                        for t in (j, j + 2):
                            act.wait_ge((silu_even, silu_odd)[j], L * 2 + t // 2 + 1)
                            act.activation(y1_hi[:, t, :], cc[:, t, :], ACT.Copy).then_inc(yc_hi, 1)
                for j in range(4):
                    for m in (2 * j, 2 * j + 1):
                        if m % 2:
                            split(L, "wo", 0, j)
                        act.wait_ge(added, L * 2 * DT + DT + m + 1)
                        act.activation(x_hi[:, m, :], f[:, m, :], ACT.Copy).then_inc(xhi_ready, 1)
                act.preload_act_table(ACT.Sqrt)
                for pair, nxt in ((0, ("wo", 1)), (1, ("f2_up", 0))):
                    for j in range(4):
                        act.wait_ge(halves_done, v_half(L, "wo", pair, j) + 4)
                        output(ps[:, j, 0:T], L, "post2", 4 * pair + j, j % 2, "g_mix_post")
                        split(L, *nxt, j)
                boundary(L, 1, "post2", "pre2", "g_f2_pre")
                act.wait_ge(staged, L * 6 + 6)
                act.dma_start(states[bass.ds(L, 1), :, :].rearrange("a p n -> (a p) n"), hist[:, :]).then_inc(stored, 16)
                ffn(L, "f2_up", "f2_dn", "pg", "post3", "g_f2_post")
                boundary(L, 2, "post3", "pre3", "g_ple_pre")
                gates(L, "pg", "pg", "pg", 0, "pg", 1)
                for j in range(4):
                    split(L, "pp", 0, j)
                    sigmoid(gate[:, 4 + j, :], ga[:, j % 2, :], L, "pg", 4 + j)
                act.preload_act_table(ACT.Sqrt)
                for m in range(DT):
                    act.wait_ge(moved, v_moved(L, "pp", m))
                    output(gate[:, m, :], L, "post4", m, m % 2, "g_ple_post")
                    if m % 2:
                        split(L + 1, "f1_up", 0, m // 2)
                boundary(L, 3, "post4", "pre4", "g_next")
            finish_root(DEPTH, None)
            keep_rb(DEPTH, None)
            act.wait_ge(y_ready, DT)
            act.dma_start(y, f[:, :, :].rearrange("p k t -> p (k t)")).then_inc(stored, 16)
            act.wait_ge(stored, 16 * DEPTH + 32)

        @block.vector
        def _(dve):
            def split(L, ph, pair, j):
                dve.wait_ge(w_hi, v_half(L, ph, pair, j))
                n = HALF[ph]
                dve.tensor_tensor(w_lo_sb[:, j, 0:n], raw[:, j, 0:n], w_hi_sb[:, j, 0:n].bitcast(F32),
                                  ALU.subtract).then_inc(w_lo, 1)

            def add_square(L, name, m, par):
                dve.wait_ge(squared, v_sq(L, name, m))
                first = isinstance(m, int) and m == 0
                if first:
                    dve.tensor_copy(ssq[:, 0:T], sq[:, par, :]).then_inc(summed, 1)
                else:
                    dve.wait_ge(summed, v_sq(L, name, m - 1))
                    dve.tensor_tensor(ssq[:, 0:T], ssq[:, 0:T], sq[:, par, :], ALU.add).then_inc(summed, 1)

            def invert(L, name):
                dve.wait_ge(root_ready, v_stat(L, name))
                dve.reciprocal(rinv[:, :], root[:, :]).then_inc(rinv_ready, 1)

            def boundary(L, n, b, post, pre, gain):
                invert(L, post)
                dve.wait_ge(bc_full, v_stat(L, post))
                dve.wait_ge(f_out, v_f(L, n, DT - 1))
                for i in range(DT + 2):
                    if i < DT:
                        if i >= 2:
                            dve.wait_ge(h_ready, L * 4 * DT + n * DT + i - 1)
                        dve.tensor_tensor(ga[:, i % 2, :], f[:, i, :], bc, ALU.mult).then_inc(step_t, 1)
                    if i >= 2:
                        m = i - 2
                        dve.wait_ge(xhi_ready, v_x(L, b, m))
                        dve.scalar_tensor_tensor(x_lo[:, m, :], h[:, m, :], cur[:, COL[gain] + m:COL[gain] + m + 1],
                                                 x_hi[:, m, :].bitcast(F32), ALU.mult, ALU.subtract).then_inc(x_ready, 1)
                        add_square(L, pre, m, m % 2)
                if n < 3:
                    invert(L, pre)
                    dve.wait_ge(rb_ready, L * 4 + n + 2)

            def move(out, bank):
                dve.tensor_tensor(out, ps[:, bank, 0:T], rb[:, :], ALU.mult).then_inc(moved, 1)

            def up_step(L, ph, which, nxt, pair, prev_pair, banks):
                for j in range(4):
                    split(L, nxt, pair, j)
                    g = j // 2
                    dve.wait_ge(halves_done, v_half(L, ph, prev_pair, j) + 4)
                    if j % 2 == 0:
                        dve.wait_ge(mid_ready, L * 2 * FT + which * FT + 2 * prev_pair + g + 1)
                    move((ga, gb)[j % 2][:, g, :], banks[j])

            def down_step(L, nxt, pair, prev_pair, name, peel=False):
                for j in range(4):
                    if j >= 2:
                        add_square(L, name, 2 * prev_pair + j % 2, j % 2)
                    split(L, nxt, pair, j)

            def ffn(L, up, dn, after, which, name):
                up_step(L, up, which, up, 1, 0, FIRST_BANKS)
                with dve.Fori(2, PAIRS[up]) as i:
                    up_step(L, up, which, up, i, i - 1, range(4))
                up_step(L, up, which, dn, 0, PAIRS[up] - 1, range(4))
                down_step(L, dn, 1, 0, name)
                with dve.Fori(2, PAIRS[dn]) as i:
                    down_step(L, dn, i, i - 1, name)
                down_step(L, after, 0, PAIRS[dn] - 1, name)

            def gate_step(L, ph, group, pair, nxt, sname, m0, banks=range(4), taps=(), short=False):
                for j in range(4):
                    split(L, *nxt, j)
                    dve.wait_ge(halves_done, v_half(L, ph, pair, j) + 4)
                    dve.wait_ge(sig, v_sig(L, sname, m0 + j - 2))
                    move(ga[:, j % 2, :], banks[j])
                    if short:
                        short_gate(L, j)
                    if j < len(taps):
                        long_taps(L, taps[j])

            todo = iter(TAPS)

            def long_taps(L, n):
                for _ in range(n):
                    k, t = next(todo)
                    c = COL["cf_conv"] + k * WT + t
                    if k == 0:
                        dve.wait_ge(glu_ready, L * WT + t + 1)
                    for i in range(2):
                        src, dst = part(i, cbuf, CH, t, k), tok(i, cc[:, t, :])
                        if k == 0:
                            b = COL["cf_conv_b"] + t
                            dve.tensor_scalar(dst, src, cur[:, c:c + 1], cur[:, b:b + 1], ALU.mult, ALU.add).then_inc(tap, 1)
                        else:
                            dve.wait_ge(tap, L * NTAP + 2 * TAP_AT[k - 1, t] + i + 1)
                            dve.scalar_tensor_tensor(dst, src, cur[:, c:c + 1], dst, ALU.mult, ALU.add).then_inc(tap, 1)

            NC3 = (2 * SK + 1) * WT

            def short_conv(L, t):
                dve.wait_ge(cv_ready, L * WT + t + 1)
                for k in range(SK):
                    c = COL["sc_conv"] + k * WT + t
                    for i in range(2):
                        src, dst = part(i, sbuf, SH, t, k), tok(i, f[:, t, :])
                        if k == 0:
                            dve.tensor_scalar(dst, src, cur[:, c:c + 1], None, ALU.mult).then_inc(c3, 1)
                        else:
                            dve.wait_ge(c3, L * NC3 + 2 * SK * t + 2 * (k - 1) + i + 1)
                            dve.scalar_tensor_tensor(dst, src, cur[:, c:c + 1], dst, ALU.mult, ALU.add).then_inc(c3, 1)

            def short_gate(L, t):
                dve.wait_ge(c3, L * NC3 + 2 * SK * (t + 1))
                dve.wait_ge(moved, v_moved(L, "bgate", t))
                dve.tensor_tensor(f[:, t, :], f[:, t, :], bg[:, t, :], ALU.mult).then_inc(c3, 1)

            dve.memset(ssq[:, T:TPAD], 0.0).then_inc(w_lo, 4)
            dve.memset(ones[:, :], 1.0).then_inc(moved, 4)
            dve.memset(meanw[:, :], 1.0 / W).then_inc(const_ready, 1)
            dve.memset(eps[:, 0:1], EPS).then_inc(const_ready, 1)
            dve.memset(eps[:, 1:2], 4 * EPS).then_inc(const_ready, 1)
            for m in range(DT):
                if m == 0:
                    dve.wait_ge(loaded, 32)
                if m == DT // 2:
                    dve.wait_ge(loaded_rest, 16)
                dve.wait_ge(xhi_ready, m + 1)
                dve.scalar_tensor_tensor(x_lo[:, m, :], h[:, m, :], pars[:, FIRST_G + m:FIRST_G + m + 1],
                                         x_hi[:, m, :].bitcast(F32), ALU.mult, ALU.subtract).then_inc(x_ready, 1)
                add_square(0, None, m, m % 2)
            for j in range(4):
                split(0, "f1_up", 0, j)
            with dve.Fori(0, DEPTH) as L:
                dve.wait_ge(x_ready, L * NX + DT)
                dve.tensor_copy(cur[:, :], pars[:, bass.ds(L * NCOL, NCOL)]).then_inc(par_ready, 1)
                invert(L, None)
                dve.wait_ge(rb_ready, L * 4 + 1)
                dve.wait_ge(pw_hi_ready, L * 2 + 2)
                dve.tensor_tensor(p_lo[:, :], p_raw, p_hi[:, :].bitcast(F32), ALU.subtract).then_inc(pw_split, 1)
                dve.tensor_tensor(pw_lo[:, :], pw_raw, pw_hi[:, :].bitcast(F32), ALU.subtract).then_inc(pw_split, 1)
                dve.wait_ge(par_ready, L + 1)
                ffn(L, "f1_up", "f1_dn", "glu", 0, "post1")
                boundary(L, 0, "b1", "post1", "pre1", "g_mix_pre")
                for n, (ph, pair, nxt) in enumerate([("glu", 0, ("glu", 1)), ("glu", 1, ("short", 0)),
                                                     ("short", 0, ("short", 1)), ("short", 1, ("pool", 0))]):
                    for j in range(4):
                        split(L, *nxt, j)
                        dve.wait_ge(halves_done, v_half(L, ph, pair, j) + 4)
                        if j % 2 == 0 and n > 0:
                            dve.wait_ge(glu_ready if n < 3 else cv_ready, L * WT + (2 * n - 2 if n < 3 else 0) + j // 2 + 1)
                        move((ga, gb)[j % 2][:, j // 2, :], FIRST_BANKS[j] if n == 0 else j)
                        if n >= 1:
                            long_taps(L, 3 if n > 1 else (0, 2, 2, 4)[j])
                dve.wait_ge(hist_in, L * 6 + 6)
                for j in range(4):
                    split(L, "bgate", 0, j)
                    dve.wait_ge(halves_done, v_half(L, "pool", 0, j) + 4)
                    dve.tensor_tensor(part(0, abuf, AH, j, AH), prompt(ps[:, j, 0:T]), prompt(rb), ALU.mult)
                    dve.tensor_tensor(part(1, abuf, AH, j, AH), sample(ps[:, j, 0:T]), sample(rb), ALU.mult).then_inc(moved, 1)
                    long_taps(L, 3)
                for j in range(4):
                    split(L, "gate0", 0, j)
                    dve.wait_ge(halves_done, v_half(L, "bgate", 0, j) + 4)
                    move(bg[:, j, :], j)
                    short_conv(L, j)
                    long_taps(L, 1)
                gate_step(L, "gate0", "gate0", 0, ("gate0", 1), "gate0", 0, taps=(2, 2, 2, 2), short=True)
                gate_step(L, "gate0", "gate0", 1, ("out0", 0), "gate0", 4, taps=(3, 3, 3, 3))
                dve.wait_ge(yb_ready, L * WT + WT)
                for j in range(4):
                    split(L, "gate1", 0, j)
                    dve.wait_ge(halves_done, v_half(L, "out0", 0, j) + 4)
                    for m in (2 * j, 2 * j + 1):
                        dve.wait_ge(sig, v_sig(L, "gate0", m))
                        dve.tensor_tensor(f[:, m, :], ps[:, m % 4, 0:T], gate[:, m, :], ALU.mult).then_inc(moved, 1)
                    long_taps(L, 2)
                gate_step(L, "gate1", "gate1", 0, ("gate1", 1), "gate1", 0, taps=(3, 3, 2, 1))
                for g in range(WT):
                    dve.wait_ge(ya_hi, L * WT + g + 1)
                    dve.scalar_tensor_tensor(y0_lo[:, g, :], ps[:, FIRST_BANKS[g], 0:T], cur[:, COL["pool_scale"] + g:COL["pool_scale"] + g + 1],
                                             y0_hi[:, g, :].bitcast(F32), ALU.mult, ALU.subtract).then_inc(moved, 1)
                gate_step(L, "gate1", "gate1b", 1, ("out1", 0), "gate1", 4, taps=(2, 3, 2, 2))

                def add_branch(b, nxt, xlo):
                    for j in range(4):
                        dve.wait_ge(halves_done, v_half(L, f"out{b}", 0, j) + 4)
                        for m in (2 * j, 2 * j + 1):
                            dve.wait_ge(sig, v_sig(L, f"gate{b}", m))
                            n = (b - 1) * DT + m
                            if n >= 2:
                                dve.wait_ge(added, L * 2 * DT + n - 1)
                            dve.tensor_tensor(gb[:, m % 2, :], ps[:, m % 4, 0:T], gate[:, m, :], ALU.mult).then_inc(moved, 1)
                        if xlo and j:
                            x_of_sum(2 * j - 2)
                            x_of_sum(2 * j - 1)
                        split(L, *nxt, j)

                def x_of_sum(m):
                    dve.wait_ge(xhi_ready, v_x(L, "m", m))
                    dve.tensor_tensor(x_lo[:, m, :], f[:, m, :], x_hi[:, m, :].bitcast(F32), ALU.subtract).then_inc(x_ready, 1)

                add_branch(1, ("gate2", 0), False)
                dve.wait_ge(ln_mean, L + 1)
                for t in range(WT):
                    dve.tensor_tensor(cc[:, t, :], cc[:, t, :], bc, ALU.subtract).then_inc(ln_step, 1)
                for j in range(4):
                    if j == 3:
                        invert(L, "ln")
                    split(L, "gate2", 1, j)
                    dve.wait_ge(halves_done, v_half(L, "gate2", 0, j) + 4)
                    dve.wait_ge(sig, v_sig(L, "gate2", j - 2))
                    move(ga[:, j % 2, :], j)
                    if j < 2:
                        add_square(L, "ln", 2 * j, 0)
                        add_square(L, "ln", 2 * j + 1, 1)
                dve.wait_ge(bc_full, v_stat(L, "ln"))
                for t in range(WT):
                    dve.tensor_tensor(cc[:, t, :], cc[:, t, :], bc, ALU.mult).then_inc(ln_step, 1)
                for t in range(WT):
                    dve.wait_ge(ln_sig, L * WT + t + 1)
                    g, b = COL["cf_ln_g"] + t, COL["cf_ln_b"] + t
                    dve.tensor_scalar(cc[:, t, :], cc[:, t, :], cur[:, g:g + 1], cur[:, b:b + 1], ALU.mult, ALU.add).then_inc(ln_step, 1)
                for t in (0, 2):
                    dve.wait_ge(ln_step, L * 3 * WT + 2 * WT + t + 1)
                    dve.tensor_tensor(cc[:, t, :], cc[:, t, :], sg[:, t, :], ALU.mult).then_inc(silu_even, 1)
                for j in range(4):
                    split(L, "out2", 0, j)
                    dve.wait_ge(halves_done, v_half(L, "gate2", 1, j) + 4)
                    dve.wait_ge(sig, v_sig(L, "gate2", 4 + j - 2))
                    move(ga[:, j % 2, :], j)
                    if j == 0:
                        for t in (0, 2):
                            dve.wait_ge(yc_hi, L * WT + t // 2 + 1)
                            dve.tensor_tensor(y1_lo[:, t, :], cc[:, t, :], y1_hi[:, t, :].bitcast(F32), ALU.subtract).then_inc(yc_even, 1)
                add_branch(2, ("wo", 0), True)
                x_of_sum(DT - 2)
                x_of_sum(DT - 1)
                for pair, nxt in ((0, ("wo", 1)), (1, ("f2_up", 0))):
                    for j in range(4):
                        add_square(L, "post2", 4 * pair + j, j % 2)
                        split(L, *nxt, j)
                boundary(L, 1, "b2", "post2", "pre2", "g_f2_pre")
                ffn(L, "f2_up", "f2_dn", "pg", 1, "post3")
                boundary(L, 2, "b3", "post3", "pre3", "g_ple_pre")
                gate_step(L, "pg", "pg", 0, ("pg", 1), "pg", 0, banks=FIRST_BANKS)
                gate_step(L, "pg", "pg", 1, ("pp", 0), "pg", 4)
                for m in range(DT):
                    if m % 2 == 0:
                        dve.wait_ge(halves_done, v_half(L, "pp", 0, m // 2) + 4)
                    dve.wait_ge(sig, v_sig(L, "pg", m))
                    dve.tensor_tensor(gate[:, m, :], ps[:, m % 4, 0:T], gate[:, m, :], ALU.mult).then_inc(moved, 1)
                    if m >= 2:
                        add_square(L, "post4", m - 2, m % 2)
                    if m % 2 == 1 and m > 1:
                        split(L + 1, "f1_up", 0, m // 2 - 1)
                for m in (DT - 2, DT - 1):
                    add_square(L, "post4", m, m % 2)
                split(L + 1, "f1_up", 0, 3)
                boundary(L, 3, "b4", "post4", "pre4", "g_next")
            invert(DEPTH, None)
            dve.wait_ge(rb_ready, DEPTH * 4 + 1)
            for m in range(DT):
                c = COL["g_next"] + m
                dve.scalar_tensor_tensor(f[:, m, :], h[:, m, :], cur[:, c:c + 1], rb[:, :], ALU.mult, ALU.mult).then_inc(y_ready, 1)

        @block.gpsimd
        def _(pool):
            def wait_alone(s, value):
                pool.wait_ge(s, value)
                pool.sem_inc(tick, 1)

            def update_h(L, n):
                for m in range(DT):
                    pool.wait_ge(step_t, L * 4 * DT + n * DT + m + 1)
                    pool.tensor_tensor(h[:, m, :], h[:, m, :], ga[:, m % 2, :], ALU.add).then_inc(h_ready, 1)

            def hidden(L, ph, which, pair):
                for g in range(2):
                    m = 2 * pair + g
                    n = (L * 2 * FT + which * FT + m) * 3
                    pool.wait_ge(moved, v_moved(L, ph, 4 * pair + 2 * g + 1))
                    pool.tensor_tensor(gb[:, g, :], ga[:, g, :], gb[:, g, :], ALU.mult).then_inc(swi, 1)
                    pool.wait_ge(swi, n + 1)
                    pool.wait_ge(sig, v_sig(L, "f1" if which == 0 else "f2", m))
                    pool.tensor_tensor(gb[:, g, :], gb[:, g, :], sg[:, g, :], ALU.mult).then_inc(swi, 1)
                    wait_alone(swi, n + 2)
                    hi, lo = mid_hi[:, bass.ds(m, 1), :], mid_lo[:, bass.ds(m, 1), :]
                    pool.tensor_copy(hi, gb[:, g:g + 1, :]).then_inc(swi, 1)
                    pool.wait_ge(swi, n + 3)
                    pool.tensor_tensor(lo, gb[:, g:g + 1, :], hi.bitcast(F32), ALU.subtract).then_inc(mid_ready, 1)

            NPS = sum(g + 1 + 3 + 1 + 1 for g in range(WT))
            steps = [sum(k + 1 + 5 for k in range(g)) for g in range(WT)]

            tap_of_3 = iter(range(1, CK))

            def add3(L, n=1):
                for _ in range(n):
                    k = next(tap_of_3)
                    pool.wait_ge(prod3, L * (CK - 1) + k)
                    if k == 1:
                        pool.wait_ge(tap, L * NTAP + 2 * TAP_AT[0, 3] + 2)
                    else:
                        pool.wait_ge(tap3, L * (CK - 1) + k - 1)
                    pool.tensor_tensor(cc[:, 3, :], cc[:, 3, :], sg[:, k % RING3, :], ALU.add).then_inc(tap3, 1)

            def pooling(L, g):
                n = L * NPS + steps[g]
                w, wide = 2 << g, padded(AH)
                src, s = abuf[:, g, :], 0
                pool.wait_ge(moved, v_moved(L, "pool", g))
                for k in range(g + 1):
                    a, d = 2 * (1 << k) - 1, 1 << k
                    dst = win[:, k % 2, :]
                    pool.tensor_tensor(dst[:, a:wide], src[:, a:wide], src[:, a - d:wide - d], ALU.add).then_inc(pstep, 1)
                    s += 1
                    if k:
                        add3(L)
                    pool.wait_ge(pstep, n + s)
                    src = dst
                c = COUNTS + g * AH
                pool.tensor_tensor(src[:, AH:AH + w - 1], src[:, AH:AH + w - 1], pars[:, c:c + w - 1], ALU.mult).then_inc(pstep, 1)
                s += 1
                wait_alone(pstep, n + s)
                pool.tensor_scalar(src[:, AH:wide], src[:, AH:wide], 1.0 / w, None, ALU.mult).then_inc(pstep, 1)
                s += 1
                pool.wait_ge(pstep, n + s)
                a = abuf[:, g, :]
                pool.tensor_tensor(prompt(pmf), pad_prompt(src, AH, AH), pad_prompt(a, AH, AH), ALU.subtract).then_inc(pstep, 1)
                pool.tensor_tensor(sample(pmf), pad_sample(src, AH, AH), pad_sample(a, AH, AH), ALU.subtract).then_inc(pstep, 1)
                s += 2
                add3(L)
                wait_alone(pstep, n + s)
                pool.tensor_copy(y1_hi[:, g, :], pmf[:, :]).then_inc(pstep, 1)
                s += 1
                pool.wait_ge(pstep, n + s)
                pool.tensor_tensor(y1_lo[:, g, :], pmf[:, :], y1_hi[:, g, :].bitcast(F32), ALU.subtract).then_inc(pm_ready, 1)
                pool.wait_ge(pm_ready, L * WT + g + 1)

            pool.memset(ident[:, :], 0.0).then_inc(const_ready, 1)
            pool.memset(ga[:, 0, :], 0.0).then_inc(mid_ready, 2)
            pool.memset(ga[:, 1, :], 0.0).then_inc(halves_done, 4)
            pool.memset(gb[:, 1, :], 0.0).then_inc(stored, 16)
            pool.memset(sg[:, 1, :], 0.0).then_inc(f_out, 2)
            pool.memset(sg[:, 0, :], 0.0).then_inc(pw_split, 2)
            pool.wait_ge(const_ready, 4)
            pool.affine_select(out=ident[:, :], in_=ident[:, :], compare_op=ALU.not_equal, fill=1.0, base=0,
                               pattern=[[-1, P]], channel_multiplier=1).then_inc(const_ready, 1)
            pool.wait_ge(const_ready, 5)
            pool.memset(gb[:, 0, :], 0.0).then_inc(const_ready, 1)
            with pool.Fori(0, DEPTH) as L:
                with pool.Fori(0, PAIRS["f1_up"]) as i:
                    hidden(L, "f1_up", 0, i)
                update_h(L, 0)
                wait_alone(side_in, L * 16 + 16)
                at = 0
                for buf, k in ((cbuf, CH), (sbuf, SH), (abuf, AH)):
                    pool.memset(buf[:, :, 0:k], 0.0).then_inc(hist_in, 1)
                    for t in range(WT):
                        cp = pool.tensor_copy(pad_sample(buf[:, t, :], k, 0, k),
                                              hist[:, at:at + NSEQ * k].rearrange("p (s r) -> p s r", r=k))
                        at += NSEQ * k
                    cp.then_inc(hist_in, 1)
                for t in range(WT):
                    pool.wait_ge(sig, v_sig(L, "glu", t))
                    for view in (0, 1):
                        dst = pad_sample(cbuf[:, t, :], CH, CH) if view else pad_prompt(cbuf[:, t, :], CH, CH)
                        pick = sample if view else prompt
                        op = pool.tensor_tensor(dst, pick(ga[:, t % 2, :]), pick(sg[:, t % 2, :]), ALU.mult)
                    op.then_inc(glu_ready, 1)
                for t in range(WT):
                    pool.wait_ge(moved, v_moved(L, "short", 2 * t + 1))
                    for view in (0, 1):
                        dst = pad_sample(sbuf[:, t, :], SH, SH) if view else pad_prompt(sbuf[:, t, :], SH, SH)
                        pick = sample if view else prompt
                        op = pool.tensor_tensor(dst, pick(ga[:, t % 2, :]), pick(gb[:, t % 2, :]), ALU.mult)
                    op.then_inc(cv_ready, 1)
                    add3(L, 2)
                pooling(L, 0)
                pooling(L, 1)
                pooling(L, 2)
                for t in range(WT):
                    wait_alone(c3, L * (2 * SK + 1) * WT + 2 * SK * WT + t + 1)
                    pool.tensor_copy(y0_hi[:, t, :], f[:, t, :]).then_inc(yb_step, 1)
                    pool.wait_ge(yb_step, L * WT + t + 1)
                    pool.tensor_tensor(y0_lo[:, t, :], f[:, t, :], y0_hi[:, t, :].bitcast(F32), ALU.subtract).then_inc(yb_ready, 1)
                    add3(L)
                pooling(L, 3)
                wait_alone(hist_in, L * 6 + 6)
                at = 0
                for buf, k in ((cbuf, CH), (sbuf, SH), (abuf, AH)):
                    n = WT * k
                    pool.tensor_copy(hist[:, at:at + n].rearrange("p (t r) -> p t r", r=k),
                                     buf[:, :, SEQ:SEQ + k]).then_inc(staged, 1)
                    at += n
                    for t in range(WT):
                        cp = pool.tensor_copy(hist[:, at:at + NSEQ * k].rearrange("p (s r) -> p s r", r=k),
                                              pad_sample(buf[:, t, :], k, SLEN, k))
                        at += NSEQ * k
                    cp.then_inc(staged, 1)
                    add3(L, 2)
                add3(L, 2)
                def add_branch(b):
                    for m in range(DT):
                        pool.wait_ge(moved, v_moved(L, f"out{b}", m))
                        if b == 2:
                            pool.wait_ge(added, L * 2 * DT + m + 1)
                        pool.tensor_tensor(f[:, m, :], f[:, m, :], gb[:, m % 2, :], ALU.add).then_inc(added, 1)

                for t in range(1, WT):
                    if t == 1:
                        pool.wait_ge(tap, (L + 1) * NTAP)
                        pool.wait_ge(tap3, (L + 1) * (CK - 1))
                    else:
                        pool.wait_ge(ln_sum, L * (WT - 1) + t - 1)
                    pool.tensor_tensor(pmf[:, :], cc[:, 0, :] if t == 1 else pmf[:, :], cc[:, t, :], ALU.add).then_inc(ln_sum, 1)
                add_branch(1)
                for t in (1, 3):
                    pool.wait_ge(ln_step, L * 3 * WT + 2 * WT + t + 1)
                    pool.tensor_tensor(cc[:, t, :], cc[:, t, :], sg[:, t, :], ALU.mult).then_inc(silu_odd, 1)
                for t in (1, 3):
                    pool.wait_ge(yc_hi, L * WT + 2 + t // 2 + 1)
                    pool.tensor_tensor(y1_lo[:, t, :], cc[:, t, :], y1_hi[:, t, :].bitcast(F32), ALU.subtract).then_inc(yc_odd, 1)
                add_branch(2)
                update_h(L, 1)
                with pool.Fori(0, PAIRS["f2_up"]) as i:
                    hidden(L, "f2_up", 1, i)
                update_h(L, 2)
                update_h(L, 3)


def _tiles(w, rows, cols):
    w = w.reshape(*w.shape[:-2], rows, P, cols, P)
    return w.swapaxes(-3, -2)


def _slots(halves):
    import numpy as np
    d, n, t = halves.shape[:3]
    a = halves.reshape(d, n // 2, 2, t, P, P).transpose(0, 1, 4, 2, 3, 5)
    return np.ascontiguousarray(a.reshape(d * (n // 2), P, 2 * t * P))


def _layout(i):
    import numpy as np
    i = {k: np.asarray(v) for k, v in i.items()}
    st = {}
    for n in ("1", "2"):
        g = _tiles(i[f"w_f{n}_gate"], DT, FT).swapaxes(1, 2)
        u = _tiles(i[f"w_f{n}_up"], DT, FT).swapaxes(1, 2)
        st[f"f{n}_up"] = _slots(np.stack([g, u], 2).reshape(DEPTH, 2 * FT, DT, P, P))
        d = _tiles(i[f"w_f{n}_down"], FT, DT).swapaxes(1, 2)
        d = d.reshape(DEPTH, DT // 2, 2, 2, FT // 2, P, P).swapaxes(2, 3)
        st[f"f{n}_dn"] = _slots(d.reshape(DEPTH, 2 * DT, FT // 2, P, P))
    z = _tiles(i["w_in"], DT, 6 * WT + 3 * DT).swapaxes(1, 2)
    blk = lambda n: z[:, n * WT:(n + 1) * WT]
    pairs = lambda a, b: np.stack([a, b], 2).reshape(DEPTH, 2 * WT, DT, P, P)
    gate = lambda n: z[:, 6 * WT + n * DT:6 * WT + (n + 1) * DT]
    st["glu"], st["short"] = _slots(pairs(blk(4), blk(5))), _slots(pairs(blk(1), blk(3)))
    st["pool"], st["bgate"] = _slots(blk(0)), _slots(blk(2))
    for n, (b, w) in enumerate(((1, "w_sc_out"), (0, "w_pool_out"), (2, "w_cf_out"))):
        st[f"gate{n}"] = _slots(gate(b))
        o = _tiles(i[w], WT, DT)
        o = o.reshape(DEPTH, WT, 4, 2, P, P).transpose(0, 2, 1, 3, 4, 5)
        st[f"out{n}"] = _slots(o.reshape(DEPTH, 4, 2 * WT, P, P))
    st["wo"] = _slots(_tiles(i["w_o"], DT, DT).swapaxes(1, 2))
    st["pg"] = _slots(_tiles(i["w_ple_gate"], DT, DT).swapaxes(1, 2))
    o = _tiles(i["w_ple_proj"], PT, DT).reshape(DEPTH, PT, 4, 2, P, P).transpose(0, 2, 1, 3, 4, 5)
    st["pp"] = _slots(o.reshape(DEPTH, 4, 2 * PT, P, P))

    def cols(a):
        return a.reshape(-1, P).T

    nxt = np.concatenate([i["g_f1_pre"][1:], i["g_final"][None]])
    blocks = []
    for l in range(DEPTH):
        src = dict({n: i[n][l] for n, _ in _COLS if n != "g_next"}, g_next=nxt[l])
        blocks += [cols(src[n]) for n, _ in _COLS]
    blocks.append(cols(i["g_f1_pre"][0]))
    table = np.zeros((WT, AH), np.float32)
    for g in range(WT):
        for t in range((2 << g) - 1):
            table[g, t] = (2 << g) / (t + 1)
    blocks.append(np.broadcast_to(table.reshape(1, -1), (P, WT * AH)))
    par = np.concatenate(blocks, 1)

    def feature_major(prompt, sample, k):
        a = np.concatenate([prompt.reshape(SEQ, -1), sample.reshape(NSEQ * SLEN, -1)])
        return a.T.reshape(k, P, T).transpose(1, 0, 2).reshape(P, k * T)

    x = feature_major(i["x_prompt"], i["x_sample"], DT)
    p = np.stack([feature_major(i["p_prompt"][l], i["p_sample"][l], PT) for l in range(DEPTH)])
    side = []
    for n in ("state_cconv", "state_sconv", "state_pool"):
        s = i[n]
        s = s.reshape(DEPTH, NSEQ, s.shape[2], WT, P).transpose(0, 4, 3, 1, 2)
        side.append(s.reshape(DEPTH, P, -1))
    side = np.concatenate(side, 2)
    pw = i["pool_w"].transpose(0, 2, 1, 3).reshape(DEPTH, P, WT * P)
    arrays = dict(x=x, par=par, side=side, early=np.concatenate([p, pw], 2), **{f"w_{k}": v for k, v in st.items()})
    return {f"in_{k}": np.ascontiguousarray(v) for k, v in arrays.items()}


def kernel(**inputs):
    import numpy as np
    import concourse.bacc as bacc
    from concourse.bass_utils import run_bass_kernel_spmd as run

    arrays = _layout(inputs)
    nc = bacc.Bacc("TRN2", target_bir_lowering=False, num_devices=1)
    a = {n: nc.dram_tensor(n, v.shape, F32, kind="ExternalInput").ap() for n, v in arrays.items()}
    y = nc.dram_tensor("out_y", (P, DT * T), F32, kind="ExternalOutput").ap()
    states = nc.dram_tensor("out_states", (DEPTH, P, sum(STATES)), F32, kind="ExternalOutput").ap()
    trunk(nc, a["in_x"], a["in_par"], a["in_side"], a["in_early"],
          {n: a[f"in_w_{n}"] for n, _, _ in PHASES}, y, states)
    r = run(nc, [arrays], core_ids=[0]).results[0]

    yt = r["out_y"].reshape(P, DT, T).transpose(2, 1, 0).reshape(T, D)
    got = [yt[:SEQ].reshape(1, SEQ, D), yt[SEQ:].reshape(NSEQ, SLEN, D)]
    s, at, new = r["out_states"], 0, {}
    for name, k in (("c", CH), ("s", SH), ("a", AH)):
        n = WT * k
        new[name, 0] = s[:, :, at:at + n].reshape(DEPTH, P, WT, k).transpose(0, 3, 2, 1).reshape(DEPTH, 1, k, W)
        at += n
        n = WT * NSEQ * k
        new[name, 1] = s[:, :, at:at + n].reshape(DEPTH, P, WT, NSEQ, k).transpose(0, 3, 4, 2, 1).reshape(DEPTH, NSEQ, k, W)
        at += n
    got += [new[n, i] for i in range(2) for n in "asc"]
    return tuple(np.ascontiguousarray(g) for g in got)
```

```python
from contextlib import ExitStack

import concourse.bass as bass
from concourse import mybir

F32 = mybir.dt.float32
F32R = mybir.dt.float32r
ALU = mybir.AluOpType
ACT = mybir.ActivationFunctionType

P = 128
DEPTH = 2
D = 1024
DFF = 2816
W = 512
PLE = 256
SEQ, NSEQ, SLEN = 256, 8, 8
T = SEQ + NSEQ * SLEN
TPAD = 384
DT, FT, WT, PT = D // P, DFF // P, W // P, PLE // P
EPS = 1e-6
CK, SK, WMAX = 31, 3, 16
CH, SH, AH = CK - 1, SK - 1, WMAX - 1


def padded(h):
    return h + SEQ + NSEQ * (h + SLEN)


PHASES = [("f1_up", FT // 2, DT), ("f1_dn", DT // 2, FT // 2),
          ("glu", 2, DT), ("short", 2, DT), ("pool", 1, DT), ("bgate", 1, DT),
          ("gate0", 2, DT), ("out0", 1, 2 * WT), ("gate1", 2, DT), ("out1", 1, 2 * WT),
          ("gate2", 2, DT), ("out2", 1, 2 * WT), ("wo", 2, DT),
          ("f2_up", FT // 2, DT), ("f2_dn", DT // 2, FT // 2),
          ("pg", 2, DT)]
PAIRS = {n: p for n, p, _ in PHASES}
HALF = {n: t * P for n, _, t in PHASES}
PAIR0 = {n: sum(p for _, p, _ in PHASES[:i]) for i, (n, _, _) in enumerate(PHASES)}
NPAIR = sum(PAIRS.values())
NHALF = 4 * NPAIR
HMAX = max(HALF.values())

_MOVED = [("f1_up", 4 * PAIRS["f1_up"]), ("glu", 8), ("short", 8), ("pool", 4), ("bgate", 4),
          ("gate0", 8), ("out0", 8), ("gate1", 6), ("poolw", 4), ("gate1b", 2), ("out1", 8),
          ("gate2", 8), ("out2", 8), ("f2_up", 4 * PAIRS["f2_up"]), ("pg", 8)]
MOVED0 = {n: sum(k for _, k in _MOVED[:i]) for i, (n, _) in enumerate(_MOVED)}
NMOVED = sum(k for _, k in _MOVED)

_SQ = [("post1", DT), ("pre1", DT), ("ln", WT), ("post2", DT), ("pre2", DT),
       ("post3", DT), ("pre3", DT), ("post4", DT), ("pre4", DT)]
SQ0 = {n: sum(k for _, k in _SQ[:i]) for i, (n, _) in enumerate(_SQ)}
NSQ = sum(k for _, k in _SQ)
STAT = {n: i for i, (n, _) in enumerate(_SQ)}
NSTAT = len(_SQ)
X0 = {"b1": 0, "m": DT, "b2": 2 * DT, "b3": 3 * DT, "b4": 4 * DT}
NX = 5 * DT
XH0 = {"b1": 0, "m": DT - 1, "b2": 2 * DT - 1, "b3": 3 * DT - 2, "b4": 4 * DT - 3}
NXH = 5 * DT - 4
SIG0 = {"f1": 0, "glu": FT, "gate0": FT + WT, "gate1": FT + WT + DT, "gate2": FT + WT + 2 * DT,
        "f2": FT + WT + 3 * DT, "pg": 2 * FT + WT + 3 * DT}
NSIG = 2 * FT + WT + 4 * DT

TAPS = [(k, t) for k in range(CK) for t in (0, 1)]
TAPS[12:12] = [(0, 3)]
TAPS += [(k, 2) for k in range(CK)]
TAP_AT = {u: i for i, u in enumerate(TAPS)}
NTAP = 2 * len(TAPS)
RING3 = 4

_COLS = [("g_f1_post", DT), ("g_mix_pre", DT), ("g_mix_post", DT), ("g_f2_pre", DT), ("g_f2_post", DT),
         ("g_ple_pre", DT), ("g_ple_post", DT), ("g_next", DT), ("pool_scale", WT), ("cf_conv_b", WT),
         ("cf_ln_g", WT), ("cf_ln_b", WT), ("sc_conv", SK * WT), ("cf_conv", CK * WT)]
COL = {n: sum(k for _, k in _COLS[:i]) for i, (n, _) in enumerate(_COLS)}
NCOL = sum(k for _, k in _COLS)
FIRST_G = DEPTH * NCOL
COUNTS = FIRST_G + DT
NPAR = COUNTS + WT * AH

HISTORY = [WT * NSEQ * k for k in (CH, SH, AH)]
STATES = [WT * (NSEQ + 1) * k for k in (CH, SH, AH)]


def trunk(nc, x, par, side, early, w_proj, streams, y, states):
    with ExitStack() as ctx:
        def sb(name, cols, dt=F32, where=ctx):
            return where.enter_context(nc.sbuf_tensor(name, [P, *cols], dt))

        def sem(name):
            return ctx.enter_context(nc.semaphore(name))

        raw = sb("raw", [4, HMAX])
        w_hi_sb = sb("w_hi_sb", [4, HMAX], F32R)
        w_lo_sb = sb("w_lo_sb", [4, HMAX], F32R)
        h = sb("h", [DT, T])
        x_hi = sb("x_hi", [DT, T], F32R)
        x_lo = sb("x_lo", [DT, T], F32R)
        f = sb("f", [DT, T])
        ga = sb("ga", [2, T])
        gb = sb("gb", [2, T])
        sg = sb("sg", [RING3, T])
        sq = sb("sq", [2, T])
        ssq = sb("ssq", [TPAD])
        rb = sb("rb", [T])
        pars = sb("pars", [NPAR])
        cur = sb("cur", [NCOL])
        ones = sb("ones", [P])
        meanw = sb("meanw", [P])
        ident = sb("ident", [P])
        eps = sb("eps", [2])
        root = sb("root", [3])
        rinv = sb("rinv", [3])
        hist = sb("hist", [sum(STATES)])
        p_raw, pw_raw = hist[:, 0:PT * T], hist[:, PT * T:PT * T + WT * P]
        p_hi = sb("p_hi", [PT * T], F32R)
        p_lo = sb("p_lo", [PT * T], F32R)
        pw_hi = sb("pw_hi", [WT * P], F32R)
        pw_lo = sb("pw_lo", [WT * P], F32R)
        with ExitStack() as ffn:
            mid_hi = sb("mid_hi", [FT, T], F32R, ffn)
            mid_lo = sb("mid_lo", [FT, T], F32R, ffn)
        cbuf = sb("cbuf", [WT, padded(CH)])
        sbuf = sb("sbuf", [WT, padded(SH)])
        abuf = sb("abuf", [WT, padded(AH)])
        bg = sb("bg", [WT, T])
        cc = sb("cc", [WT, T])
        y0_hi = sb("y0_hi", [WT, T], F32R)
        y0_lo = sb("y0_lo", [WT, T], F32R)
        y1_hi = sb("y1_hi", [WT, T], F32R)
        y1_lo = sb("y1_lo", [WT, T], F32R)
        win = sb("win", [2, padded(AH)])
        pmf = sb("pmf", [T])
        gate = sb("gate", [DT, T])

        ps = ctx.enter_context(nc.psum_tensor("ps", [P, 8, 512], F32))
        STATB = 7
        bc = ps[:, STATB, 64:64 + T]
        FIRST_BANKS = (4, 5, 6, 3)
        PROJ = DT * PT * P
        proj_raw = gate[:, :, :].rearrange("p k t -> p (k t)")[:, 0:PROJ]
        proj_hi = x_hi[:, :, :].rearrange("p k t -> p (k t)")[:, 0:PROJ]
        proj_lo = x_lo[:, :, :].rearrange("p k t -> p (k t)")[:, 0:PROJ]
        PROJ_BANKS = (4, 5, 6, 3, 2, 0, 1, 3)
        PROJ_DVE = 3
        POOLW_BANKS = (4, 5, 6, 0)

        loaded = sem("loaded")
        loaded_rest = sem("loaded_rest")
        raw_in = [sem("raw_in0"), sem("raw_in1")]
        early_in = sem("early_in")
        side_in = sem("side_in")
        const_ready = sem("const_ready")
        w_hi = sem("w_hi")
        w_lo = sem("w_lo")
        halves_done = sem("halves_done")
        moved = sem("moved")
        squared = sem("squared")
        f_out = sem("f_out")
        summed = sem("summed")
        stat_full = sem("stat_full")
        root_ready = sem("root_ready")
        rinv_ready = sem("rinv_ready")
        bc_full = sem("bc_full")
        rb_ready = sem("rb_ready")
        par_ready = sem("par_ready")
        step_t = sem("step_t")
        h_ready = sem("h_ready")
        xhi_ready = sem("xhi_ready")
        x0_hi = sem("x0_hi")
        proj_in = sem("proj_in")
        proj_hi_ready = sem("proj_hi_ready")
        proj_split = sem("proj_split")
        proj_done = sem("proj_done")
        proj_dve = sem("proj_dve")
        proj_act = sem("proj_act")
        ple_out = sem("ple_out")
        x_ready = sem("x_ready")
        sig = sem("sig")
        swi = sem("swi")
        mid_ready = sem("mid_ready")
        glu_ready = sem("glu_ready")
        cv_ready = sem("cv_ready")
        tap = sem("tap")
        prod3 = sem("prod3")
        tap3 = sem("tap3")
        c3 = sem("c3")
        pstep = sem("pstep")
        pm_ready = sem("pm_ready")
        pw_split = sem("pw_split")
        pw_hi_ready = sem("pw_hi_ready")
        poolw_done = sem("poolw_done")
        ya_hi = sem("ya_hi")
        yb_ready = sem("yb_ready")
        yb_step = sem("yb_step")
        silu_even = sem("silu_even")
        silu_odd = sem("silu_odd")
        yc_hi = sem("yc_hi")
        yc_even = sem("yc_even")
        yc_odd = sem("yc_odd")
        added = sem("added")
        ln_sum = sem("ln_sum")
        ln_mean = sem("ln_mean")
        ln_step = sem("ln_step")
        ln_sig = sem("ln_sig")
        ln_y = sem("ln_y")
        hist_in = sem("hist_in")
        staged = sem("staged")
        stored = sem("stored")
        y_ready = sem("y_ready")
        tick = sem("tick")

        block = ctx.enter_context(nc.Block())

        def v_half(L, ph, pair, j):
            return L * NHALF + 4 * (PAIR0[ph] + pair) + j + 1

        def v_moved(L, ph, n):
            return L * NMOVED + MOVED0[ph] + n + 5

        def v_sq(L, name, m):
            return L * NSQ + (m + 1 if name is None else DT + SQ0[name] + m + 1)

        def v_f(L, n, m):
            return (L * 4 + n) * DT + m + 3

        def v_stat(L, name):
            return L * NSTAT + (1 if name is None else STAT[name] + 2)

        def v_x(L, b, m):
            return DT + L * NX + X0[b] + m + 1

        def v_xhi(L, b, m):
            return DT + L * NXH + XH0[b] + m + (1 if b == "m" else 0)

        def x_over_proj(L, m):
            return L * DT + min(DT, 2 * (((m + 1) * T - 1) // (2 * PT * P) + 1))

        def v_sig(L, name, m):
            return L * NSIG + SIG0[name] + m + 1

        def prompt(t):
            return t[:, 0:SEQ]

        def sample(t):
            return t[:, SEQ:T].rearrange("p (s t) -> p s t", t=SLEN)

        def pad_prompt(t, hist_rows, at):
            return t[:, at:at + SEQ]

        def pad_sample(t, hist_rows, at, n=SLEN):
            return t[:, hist_rows + SEQ:].rearrange("p (s w) -> p s w", w=hist_rows + SLEN)[:, :, at:at + n]

        def part(i, buf, hist_rows, tile, at):
            row = buf[:, tile, :]
            return pad_sample(row, hist_rows, at) if i else pad_prompt(row, hist_rows, at)

        def tok(i, row):
            return sample(row) if i else prompt(row)

        STEP = [ga[:, 0, :], ga[:, 1, :], gb[:, 0, :], gb[:, 1, :]]
        CHASE_SQ = [sg[:, i, :] for i in range(RING3)] + [sq[:, i, :] for i in range(2)]

        @block.sync
        def _(sp):
            sp.dma_start(pars[:, :], par).then_inc(loaded, 16)

            def load_x(c):
                k = slice(c * (DT // 2), (c + 1) * (DT // 2))
                sp.dma_start(h[:, k, :], x.rearrange("p (k t) -> p k t", t=T)[:, k, :]).then_inc((loaded, loaded_rest)[c], 16)

            load_x(0)

            def load_pair(L, ph, pair, layer=None):
                src = streams[ph]
                for s in range(2):
                    sp.wait_ge(w_lo, L * NHALF + 4 * (PAIR0[ph] + pair) + 2 * s + 2)
                    row = ((L if layer is None else layer) * PAIRS[ph] + pair) * 2 + s
                    sp.dma_start(raw[:, 2 * s:2 * s + 2, 0:HALF[ph]],
                                 src[bass.ds(row, 1), :, :].rearrange("a p (h n) -> (a p) h n", h=2)
                                 ).then_inc(raw_in[s], 16)

            load_pair(0, "f1_up", 0)
            load_x(1)
            with sp.Fori(0, DEPTH) as L:
                sp.wait_ge(stored, L * 16 + 16)
                sp.sem_inc(tick, 1)
                sp.wait_ge(pw_split, L * 2 + 2)
                sp.dma_start(hist[:, 0:PT * T + WT * P], early[bass.ds(L, 1), :, :].rearrange("a p n -> (a p) n")).then_inc(early_in, 16)
                for ph, n, _ in PHASES:
                    if ph == "f1_dn":
                        sp.wait_ge(pw_split, L * 2 + 4)
                        sp.dma_start(hist[:, 0:sum(HISTORY)],
                                     side[bass.ds(L, 1), :, :].rearrange("a p n -> (a p) n")).then_inc(side_in, 16)
                    if ph == "f2_dn":
                        sp.wait_ge(moved, v_moved(L, "out2", DT - 1))
                        sp.dma_start(proj_raw, w_proj[bass.ds(L, 1), :, :].rearrange("a p n -> (a p) n")).then_inc(proj_in, 16)
                    if n > 2:
                        with sp.Fori(1 if ph == "f1_up" else 0, n) as i:
                            load_pair(L, ph, i)
                    else:
                        for i in range(n):
                            load_pair(L, ph, i)
                load_pair(L + 1, "f1_up", 0, layer=DEPTH - 1)

        @block.tensor
        def _(pe):
            WARM_SUM, WARM_X = 4, 9

            def products(out, w, n, rhs_hi, rhs_lo, start, stop):
                whi, wlo = w_hi_sb[:, w, n:n + P], w_lo_sb[:, w, n:n + P]
                pe.matmul(out, whi, rhs_hi, start=start, stop=False, skip_group_check=True)
                pe.matmul(out, whi, rhs_lo, start=False, stop=False, skip_group_check=True)
                return pe.matmul(out, wlo, rhs_hi, start=False, stop=stop, skip_group_check=True)

            def wait_half(L, ph, pair, j):
                pe.wait_ge(w_lo, v_half(L, ph, pair, j) + 4)

            def pair_of_x(L, ph, pair, moved0, between={}, stat=None, banks_free=False, xl=None):
                for j in range(4):
                    wait_half(L, ph, pair, j)
                    if j < 3 and banks_free:
                        pass
                    else:
                        pe.wait_ge(moved, moved0 + j - 4)
                    for k in range(DT):
                        if xl is not None and j == 0:
                            pe.wait_ge(x_ready, xl + k + 1)
                        mm = products(ps[:, j, 0:T], j, k * P, x_hi[:, k, :], x_lo[:, k, :], k == 0, k == DT - 1)
                    mm.then_inc(halves_done, 1)
                    if j in between:
                        between[j](L, stat)

            def first_pair(L, ph, xl, stat):
                half = DT // 2

                def some(j, ks):
                    for k in ks:
                        mm = products(ps[:, FIRST_BANKS[j], 0:T], j, k * P, x_hi[:, k, :], x_lo[:, k, :], k == 0, k == DT - 1)
                    return mm

                for j in range(3):
                    wait_half(L, ph, 0, j)
                for k in range(half):
                    pe.wait_ge(x_ready, xl + k + 1)
                    for j in range(3):
                        some(j, [k])
                wait_half(L, ph, 0, 3)
                if ph == "pg":
                    pe.wait_ge(proj_act, (L + 1) * (DT - PROJ_DVE))
                some(3, range(half))
                for k in range(half, DT):
                    pe.wait_ge(x_ready, xl + k + 1)
                    for j in range(2):
                        mm = some(j, [k])
                        if k == DT - 1:
                            mm.then_inc(halves_done, 1)
                some(2, range(half, DT)).then_inc(halves_done, 1)
                some(3, [half])
                sums(L, stat)
                some(3, range(half + 1, DT - 1))
                spread(L, stat)
                some(3, [DT - 1]).then_inc(halves_done, 1)

            def keep_warm(n):
                for _ in range(n):
                    pe.matmul(ps[:, FIRST_BANKS[2], 0:P], ident[:, :], ident[:, :], start=True, stop=True)

            def sums(L, name):
                n = WT if name == "ln" else DT
                pe.wait_ge(summed, v_sq(L, name, n - 1))
                for t in range(3):
                    mm = pe.matmul(ps[:, STATB, t:t + 1], ssq[:, t * P:(t + 1) * P], ones[:, 0:1], start=True, stop=True)
                mm.then_inc(stat_full, 1)

            def spread(L, name):
                pe.wait_ge(rinv_ready, v_stat(L, name))
                for t in range(3):
                    n = min(P, T - t * P)
                    mm = pe.matmul(ps[:, STATB, 64 + t * P:64 + t * P + n], rinv[:, t:t + 1].broadcast_to([P, P]),
                                   ident[:, 0:n], start=True, stop=True)
                mm.then_inc(bc_full, 1)

            def down(L, ph, banks_left, which, n):
                with pe.Fori(0, PAIRS[ph]) as i:
                    pe.wait_ge(moved, banks_left)
                    for j in range(4):
                        g, c = j % 2, j // 2
                        wait_half(L, ph, i, j)
                        if c == 0:
                            pe.wait_ge(f_out, v_f(L, n, 2 * i + g - 2))
                        pe.wait_ge(mid_ready, L * 2 * FT + which * FT + 2 + (c + 1) * (FT // 2))
                        for k in range(FT // 2):
                            m = c * (FT // 2) + k
                            mm = products(ps[:, g, 0:T], j, k * P, mid_hi[:, m, :], mid_lo[:, m, :], m == 0, m == FT - 1)
                        mm.then_inc(halves_done, 1)

            def narrow(L, ph, kt, rhs_hi, rhs_lo):
                for j in range(4):
                    wait_half(L, ph, 0, j)
                    for c in range(2):
                        q = 2 * j + c
                        pe.wait_ge(moved, v_moved(L, ph, q) - 4)
                        for k in range(kt):
                            mm = products(ps[:, q % 4, 0:T], j, k * 2 * P + c * P, rhs_hi[:, k, :], rhs_lo[:, k, :],
                                          k == 0, k == kt - 1)
                    mm.then_inc(halves_done, 1)

            pe.wait_ge(const_ready, 6)
            with pe.Fori(0, DEPTH) as L:
                first_pair(L, "f1_up", L * NX, None)
                pair_of_x(L, "f1_up", 1, v_moved(L, "f1_up", 4), banks_free=True)
                with pe.Fori(2, PAIRS["f1_up"]) as i:
                    pair_of_x(L, "f1_up", i, v_moved(L, "f1_up", 4 * i))
                down(L, "f1_dn", v_moved(L, "f1_up", 4 * PAIRS["f1_up"] - 3), 0, 0)
                keep_warm(WARM_SUM)
                sums(L, "post1")
                spread(L, "post1")
                keep_warm(WARM_X)
                first_pair(L, "glu", v_x(L, "b1", -1), "pre1")
                pair_of_x(L, "glu", 1, v_moved(L, "glu", 4), banks_free=True)
                for ph in ("short", "pool", "bgate", "gate0"):
                    for i in range(PAIRS[ph]):
                        pair_of_x(L, ph, i, v_moved(L, ph, 4 * i))
                pe.wait_ge(yb_ready, L * WT + WT)
                narrow(L, "out0", WT, y0_hi, y0_lo)
                pair_of_x(L, "gate1", 0, v_moved(L, "gate1", 0))

                def pool_products(L, _):
                    pe.wait_ge(pw_split, L * 2 + 4)
                    for g in range(WT):
                        pe.wait_ge(pm_ready, L * WT + g + 1)
                        if g == 3:
                            pe.wait_ge(moved, v_moved(L, "gate1", 4))
                        out = ps[:, POOLW_BANKS[g], 0:T]
                        whi, wlo = pw_hi[:, g * P:(g + 1) * P], pw_lo[:, g * P:(g + 1) * P]
                        pe.matmul(out, whi, y1_hi[:, g, :], start=True, stop=False)
                        pe.matmul(out, whi, y1_lo[:, g, :], start=False, stop=False)
                        pe.matmul(out, wlo, y1_hi[:, g, :], start=False, stop=True).then_inc(poolw_done, 1)

                pair_of_x(L, "gate1", 1, v_moved(L, "gate1", 4), {1: pool_products})
                pe.wait_ge(moved, v_moved(L, "poolw", WT - 1))
                narrow(L, "out1", WT, y0_hi, y0_lo)
                pe.wait_ge(ln_sum, L * (WT - 1) + WT - 1)
                pe.matmul(bc, meanw[:, :], pmf[:, :], start=True, stop=True).then_inc(ln_mean, 1)
                pair_of_x(L, "gate2", 0, v_moved(L, "gate2", 0), {2: sums, 3: spread}, "ln")
                pair_of_x(L, "gate2", 1, v_moved(L, "gate2", 4))
                pe.wait_ge(yc_even, L * 2 + 2)
                pe.wait_ge(yc_odd, L * 2 + 2)
                narrow(L, "out2", WT, y1_hi, y1_lo)
                pair_of_x(L, "wo", 0, v_moved(L, "out2", 8), xl=v_x(L, "m", -1))
                for j in range(4):
                    wait_half(L, "wo", 1, j)
                    pe.wait_ge(f_out, v_f(L, 1, j))
                    for k in range(DT):
                        mm = products(ps[:, j, 0:T], j, k * P, x_hi[:, k, :], x_lo[:, k, :], k == 0, k == DT - 1)
                    mm.then_inc(halves_done, 1)
                keep_warm(WARM_SUM)
                sums(L, "post2")
                spread(L, "post2")
                keep_warm(WARM_X)
                first_pair(L, "f2_up", v_x(L, "b2", -1), "pre2")
                pair_of_x(L, "f2_up", 1, v_moved(L, "f2_up", 4), banks_free=True)
                with pe.Fori(2, PAIRS["f2_up"]) as i:
                    pair_of_x(L, "f2_up", i, v_moved(L, "f2_up", 4 * i))
                down(L, "f2_dn", v_moved(L, "f2_up", 4 * PAIRS["f2_up"] - 3), 1, 2)

                def project(q):
                    if q == 5:
                        pe.wait_ge(f_out, v_f(L, 2, DT - 1))
                    if q == DT - 1:
                        pe.wait_ge(proj_act, L * (DT - PROJ_DVE) + 1)
                    for k in range(PT):
                        c = (2 * PT * (q // 2) + 2 * k + q % 2) * P
                        ph, pl = p_hi[:, k * T:(k + 1) * T], p_lo[:, k * T:(k + 1) * T]
                        out = ps[:, PROJ_BANKS[q], 0:T]
                        pe.matmul(out, proj_hi[:, c:c + P], ph, start=k == 0, stop=False)
                        pe.matmul(out, proj_hi[:, c:c + P], pl, start=False, stop=False)
                        mm = pe.matmul(out, proj_lo[:, c:c + P], ph, start=False, stop=k == PT - 1)
                    mm.then_inc(proj_done, 1)

                pe.wait_ge(proj_split, L + 1)
                for q in (0, 1):
                    project(q)
                sums(L, "post3")
                project(2)
                spread(L, "post3")
                for q in range(3, DT):
                    project(q)
                pe.wait_ge(proj_dve, L * PROJ_DVE + PROJ_DVE)
                first_pair(L, "pg", v_x(L, "b3", -1), "pre3")
                pair_of_x(L, "pg", 1, v_moved(L, "pg", 4), banks_free=True)
                keep_warm(2 * WARM_SUM)
                sums(L, "post4")
                spread(L, "post4")
                keep_warm(WARM_X)
            sums(DEPTH, None)
            spread(DEPTH, None)

        @block.scalar
        def _(act):
            def split(L, ph, pair, j):
                if j % 2 == 0:
                    act.wait_ge(raw_in[j // 2], (L * NPAIR + PAIR0[ph] + pair + 1) * 16)
                act.wait_ge(halves_done, v_half(L, ph, pair, j))
                n = HALF[ph]
                act.activation(w_hi_sb[:, j, 0:n], raw[:, j, 0:n], ACT.Copy).then_inc(w_hi, 1)

            def square(src, L, name, m, par):
                act.wait_ge(summed, v_sq(L, name, m - 2))
                act.activation(sq[:, par, :], src, ACT.Square).then_inc(squared, 1)

            def finish_root(L, name):
                act.wait_ge(stat_full, v_stat(L, name))
                twice = 4.0 if name in ("post1", "post3") else 1.0
                width = W if name == "ln" else D
                e = eps[:, 1:2] if twice == 4.0 else eps[:, 0:1]
                act.activation(root[:, :], ps[:, STATB, 0:3], ACT.Sqrt, bias=e, scale=twice / width).then_inc(root_ready, 1)

            def keep_rb(L, name):
                act.wait_ge(bc_full, v_stat(L, name))
                act.activation(rb[:, :], bc, ACT.Copy).then_inc(rb_ready, 1)

            def output(src, L, name, m, par, gain):
                square(src, L, name, m, par)
                act.activation(f[:, bass.ds(m, 1), :] if not isinstance(m, int) else f[:, m, :], src, ACT.Copy,
                               scale=cur[:, bass.ds(COL[gain] + m, 1)] if not isinstance(m, int)
                               else cur[:, COL[gain] + m:COL[gain] + m + 1]).then_inc(f_out, 1)

            def last_output(src, L, name, m, par, gain, nxt):
                square(src, L, name, m, par)
                if name == "post4":
                    act.preload_act_table(ACT.Sqrt)
                else:
                    split(*nxt, 3)
                finish_root(L, name)
                if name == "post4":
                    split(*nxt, 2)
                    split(*nxt, 3)
                act.activation(f[:, m, :], src, ACT.Copy, scale=cur[:, COL[gain] + m:COL[gain] + m + 1]).then_inc(f_out, 1)

            def keep_product(L, q):
                act.wait_ge(proj_done, L * DT + q + 1)
                act.activation(gate[:, q, :], ps[:, PROJ_BANKS[q], 0:T], ACT.Copy).then_inc(proj_act, 1)

            def chase(L, n, pre, gain):
                if n == 2:
                    keep_product(L, 3)
                    keep_product(L, 4)
                for m in range(1, DT + 1):
                    if m < DT:
                        act.wait_ge(h_ready, L * 4 * DT + n * DT + m + 1)
                        if n == 2:
                            act.wait_ge(proj_done, x_over_proj(L, m))
                        act.activation(x_hi[:, m, :], h[:, m, :], ACT.Copy,
                                       scale=cur[:, COL[gain] + m:COL[gain] + m + 1]).then_inc(xhi_ready, 1)
                    else:
                        act.wait_ge(h_ready, L * 4 * DT + n * DT + m)
                    if m > len(CHASE_SQ):
                        act.wait_ge(summed, v_sq(L, pre, m - 1 - len(CHASE_SQ)))
                    act.activation(CHASE_SQ[(m - 1) % len(CHASE_SQ)], h[:, m - 1, :], ACT.Square).then_inc(squared, 1)
                    if n == 2 and m + 4 < DT:
                        keep_product(L, m + 4)

            def keep_norm(L, pre, ph):
                split(L, ph, 1, 0)
                finish_root(L, pre)
                act.preload_act_table(ACT.Sigmoid)
                split(L, ph, 1, 1)
                keep_rb(L, pre)

            def sigmoid(out, src, L, ph, n):
                act.wait_ge(moved, v_moved(L, ph, n))
                act.activation(out, src, ACT.Sigmoid).then_inc(sig, 1)

            def up_step(L, ph, nxt, pair, prev_pair, split_from=0):
                for j in range(4):
                    if j >= split_from:
                        split(L, nxt, pair, j)
                    if j % 2 == 1:
                        sigmoid(sg[:, j // 2, :], ga[:, j // 2, :], L, ph, 4 * prev_pair + j - 1)

            def down_step(L, ph, nxt, pair, prev_pair, name, gain, last=False):
                for j in range(4):
                    if j >= 2:
                        act.wait_ge(halves_done, v_half(L, ph, prev_pair, j) + 4)
                        if j == 3 and last:
                            last_output(ps[:, 1, 0:T], L, name, DT - 1, 1, gain, (L, nxt, pair))
                            break
                        output(ps[:, j % 2, 0:T], L, name, 2 * prev_pair + j % 2, j % 2, gain)
                    split(L, nxt, pair, j)

            def ffn(L, up, dn, after, name, gain):
                up_step(L, up, up, 1, 0, split_from=2)
                if up == "f1_up":
                    act.wait_ge(early_in, L * 16 + 16)
                    act.activation(p_hi[:, :], p_raw, ACT.Copy).then_inc(pw_hi_ready, 1)
                    act.activation(pw_hi[:, :], pw_raw, ACT.Copy).then_inc(pw_hi_ready, 1)
                with act.Fori(2, PAIRS[up]) as i:
                    up_step(L, up, up, i, i - 1)
                up_step(L, up, dn, 0, PAIRS[up] - 1)
                if up == "f2_up":
                    act.wait_ge(proj_in, L * 16 + 16)
                    act.wait_ge(halves_done, v_half(L, up, PAIRS[up] - 1, 3) + 4)
                    act.activation(proj_hi, proj_raw, ACT.Copy).then_inc(proj_hi_ready, 1)
                act.preload_act_table(ACT.Sqrt)
                with act.Fori(1, PAIRS[dn]) as i:
                    down_step(L, dn, dn, i, i - 1, name, gain)
                down_step(L, dn, after, 0, PAIRS[dn] - 1, name, gain, last=True)

            tap_of_3 = iter(range(1, CK))

            def product3(L):
                k = next(tap_of_3, None)
                if k is None:
                    return
                if k == 1:
                    act.wait_ge(hist_in, L * 6 + 2)
                    act.wait_ge(glu_ready, L * WT + WT)
                if k > RING3:
                    act.wait_ge(tap3, L * (CK - 1) + k - RING3)
                c = COL["cf_conv"] + k * WT + 3
                for i in range(2):
                    op = act.activation(tok(i, sg[:, k % RING3, :]), part(i, cbuf, CH, 3, k), ACT.Copy, scale=cur[:, c:c + 1])
                op.then_inc(prod3, 1)

            def gates(L, ph, group, name, m0, nxt, pair):
                for j in range(4):
                    split(L, nxt, pair, j)
                    sigmoid(gate[:, m0 + j, :], ga[:, j % 2, :], L, group, j)
                    product3(L)

            act.wait_ge(const_ready, 6)
            act.preload_act_table(ACT.Sqrt)
            for m in range(DT):
                if m == 0:
                    act.wait_ge(loaded, 32)
                if m == DT // 2:
                    for j in range(4):
                        split(0, "f1_up", 0, j)
                    act.wait_ge(loaded_rest, 16)
                act.activation(x_hi[:, m, :], h[:, m, :], ACT.Copy,
                               scale=pars[:, FIRST_G + m:FIRST_G + m + 1]).then_inc(xhi_ready, 1)
                if m >= 2:
                    act.wait_ge(summed, m - 1)
                act.activation(sq[:, m % 2, :], h[:, m, :], ACT.Square).then_inc(squared, 1)
            with act.Fori(0, DEPTH) as L:
                keep_norm(L, None, "f1_up")
                act.wait_ge(par_ready, L + 1)
                ffn(L, "f1_up", "f1_dn", "glu", "post1", "g_f1_post")
                chase(L, 0, "pre1", "g_mix_pre")
                keep_norm(L, "pre1", "glu")
                for pair in range(2):
                    nxt = [("glu", 1), ("short", 0)][pair]
                    for j in range(4):
                        if pair or j >= 2:
                            split(L, nxt[0], nxt[1], j)
                        if j % 2 == 1:
                            act.wait_ge(moved, v_moved(L, "glu", 4 * pair + j))
                            act.activation(sg[:, j // 2, :], gb[:, j // 2, :], ACT.Sigmoid).then_inc(sig, 1)
                for nxt in (("short", 1), ("pool", 0), ("bgate", 0), ("gate0", 0)):
                    for j in range(4):
                        split(L, *nxt, j)
                        product3(L)
                gates(L, "gate0", "gate0", "gate0", 0, "gate0", 1)
                for j in range(4):
                    split(L, "out0", 0, j)
                    sigmoid(gate[:, 4 + j, :], ga[:, j % 2, :], L, "gate0", 4 + j)
                    product3(L)
                for j in range(4):
                    split(L, "gate1", 0, j)
                    product3(L)
                for j in range(4):
                    split(L, "gate1", 1, j)
                    sigmoid(gate[:, j, :], ga[:, j % 2, :], L, "gate1", j)
                    product3(L)
                for j in range(4):
                    split(L, "out1", 0, j)
                    sigmoid(gate[:, 4 + j, :], ga[:, j % 2, :], L, *(("gate1", 4 + j) if j < 2 else ("gate1b", j - 2)))
                    if j == 1:
                        for g in range(WT):
                            act.wait_ge(poolw_done, L * WT + g + 1)
                            act.activation(y0_hi[:, g, :], ps[:, POOLW_BANKS[g], 0:T], ACT.Copy,
                                           scale=cur[:, COL["pool_scale"] + g:COL["pool_scale"] + g + 1]).then_inc(ya_hi, 1)
                for j in range(4):
                    split(L, "gate2", 0, j)
                for j in range(4):
                    split(L, "gate2", 1, j)
                    if j < 2:
                        for t in (2 * j, 2 * j + 1):
                            act.wait_ge(ln_step, L * 3 * WT + t + 1)
                            square(cc[:, t, :], L, "ln", t, t % 2)
                    sigmoid(gate[:, j, :], ga[:, j % 2, :], L, "gate2", j)
                    if j == 2:
                        act.preload_act_table(ACT.Sqrt)
                        finish_root(L, "ln")
                        act.preload_act_table(ACT.Sigmoid)
                for t in range(WT):
                    act.wait_ge(ln_step, L * 3 * WT + WT + t + 1)
                    act.activation(sg[:, t, :], cc[:, t, :], ACT.Sigmoid,
                                   scale=cur[:, COL["cf_ln_g"] + t:COL["cf_ln_g"] + t + 1],
                                   bias=cur[:, COL["cf_ln_b"] + t:COL["cf_ln_b"] + t + 1]).then_inc(ln_sig, 1)
                for j in range(4):
                    split(L, "out2", 0, j)
                    sigmoid(gate[:, 4 + j, :], ga[:, j % 2, :], L, "gate2", 4 + j)
                    if j < 2:
                        for t in (j, j + 2):
                            act.wait_ge((silu_even, silu_odd)[j], L * 2 + t // 2 + 1)
                            act.activation(y1_hi[:, t, :], cc[:, t, :], ACT.Copy).then_inc(yc_hi, 1)
                for j in range(4):
                    if j < 3:
                        split(L, "wo", 0, j)
                    for m in (2 * j, 2 * j + 1):
                        act.wait_ge(added, L * 2 * DT + DT + m + 1)
                        act.activation(x_hi[:, m, :], f[:, m, :], ACT.Copy).then_inc(xhi_ready, 1)
                act.preload_act_table(ACT.Sqrt)
                split(L, "wo", 0, 3)
                for pair, nxt in ((0, ("wo", 1)), (1, ("f2_up", 0))):
                    for j in range(4):
                        act.wait_ge(halves_done, v_half(L, "wo", pair, j) + 4)
                        if pair == 1 and j == 3:
                            last_output(ps[:, 3, 0:T], L, "post2", DT - 1, 1, "g_mix_post", (L, "f2_up", 0))
                            break
                        output(ps[:, j, 0:T], L, "post2", 4 * pair + j, j % 2, "g_mix_post")
                        split(L, *nxt, j)
                chase(L, 1, "pre2", "g_f2_pre")
                keep_norm(L, "pre2", "f2_up")
                act.wait_ge(staged, L * 6 + 6)
                act.dma_start(states[bass.ds(L, 1), :, :].rearrange("a p n -> (a p) n"), hist[:, :]).then_inc(stored, 16)
                ffn(L, "f2_up", "f2_dn", "pg", "post3", "g_f2_post")
                chase(L, 2, "pre3", "g_ple_pre")
                keep_norm(L, "pre3", "pg")
                for m in range(DT):
                    pair, j = divmod(m, 4)
                    if pair == 0 and j >= 2:
                        split(L, "pg", 1, j)
                    if m >= 4:
                        act.wait_ge(ple_out, L * DT + m - 3)
                    sigmoid(sg[:, m % RING3, :], ga[:, m % 2, :], L, "pg", m)
                    if m:
                        act.wait_ge(ple_out, L * DT + m)
                        output(gate[:, m - 1, :], L, "post4", m - 1, (m - 1) % 2, "g_ple_post")
                    if pair == 1 and j < 2:
                        split(L + 1, "f1_up", 0, j)
                act.wait_ge(ple_out, L * DT + DT)
                last_output(gate[:, DT - 1, :], L, "post4", DT - 1, 1, "g_ple_post", (L + 1, "f1_up", 0))
                chase(L, 3, "pre4", "g_next")
            finish_root(DEPTH, None)
            keep_rb(DEPTH, None)
            for c in range(4):
                act.wait_ge(y_ready, 2 * c + 2)
                act.dma_start(y[:, 2 * c * T:(2 * c + 2) * T],
                              f[:, 2 * c:2 * c + 2, :].rearrange("p k t -> p (k t)")).then_inc(stored, 16)
            act.wait_ge(stored, 16 * (DEPTH + 1 + 4))

        @block.vector
        def _(dve):
            def split(L, ph, pair, j):
                dve.wait_ge(w_hi, v_half(L, ph, pair, j))
                n = HALF[ph]
                dve.tensor_tensor(w_lo_sb[:, j, 0:n], raw[:, j, 0:n], w_hi_sb[:, j, 0:n].bitcast(F32),
                                  ALU.subtract).then_inc(w_lo, 1)

            def add_square(L, name, m, par, src=None):
                dve.wait_ge(squared, v_sq(L, name, m))
                first = isinstance(m, int) and m == 0
                src = sq[:, par, :] if src is None else src
                if first:
                    dve.tensor_copy(ssq[:, 0:T], src).then_inc(summed, 1)
                else:
                    dve.wait_ge(summed, v_sq(L, name, m - 1))
                    dve.tensor_tensor(ssq[:, 0:T], ssq[:, 0:T], src, ALU.add).then_inc(summed, 1)

            def invert(L, name):
                dve.wait_ge(root_ready, v_stat(L, name))
                dve.reciprocal(rinv[:, :], root[:, :]).then_inc(rinv_ready, 1)

            def keep_product(L, q):
                dve.wait_ge(proj_done, L * DT + q + 1)
                dve.tensor_copy(gate[:, q, :], ps[:, PROJ_BANKS[q], 0:T]).then_inc(proj_dve, 1)

            EARLY_ADDS = 5

            def boundary(L, n, b, post, pre, gain, nxt):
                g = COL[gain]

                def step(i):
                    if i >= len(STEP):
                        dve.wait_ge(h_ready, L * 4 * DT + n * DT + i - len(STEP) + 1)
                    if i == DT - 1:
                        dve.wait_ge(f_out, v_f(L, n, i))
                    dve.tensor_tensor(STEP[i % len(STEP)], f[:, i, :], bc, ALU.mult).then_inc(step_t, 1)

                def x_low(m):
                    if m == 0:
                        dve.wait_ge(x0_hi, L * 4 + n + 1)
                    else:
                        dve.wait_ge(xhi_ready, v_xhi(L, b, m))
                    dve.scalar_tensor_tensor(x_lo[:, m, :], h[:, m, :], cur[:, g + m:g + m + 1],
                                             x_hi[:, m, :].bitcast(F32), ALU.mult, ALU.subtract).then_inc(x_ready, 1)

                if n == 2:
                    keep_product(L, 0)
                    keep_product(L, 1)
                invert(L, post)
                if n == 2:
                    keep_product(L, 2)
                dve.wait_ge(bc_full, v_stat(L, post))
                dve.wait_ge(f_out, v_f(L, n, DT - 2))
                step(0)
                dve.wait_ge(step_t, L * 4 * DT + n * DT + 1)
                dve.tensor_tensor(h[:, 0, :], h[:, 0, :], STEP[0], ALU.add).then_inc(h_ready, 1)
                step(1)
                dve.wait_ge(h_ready, L * 4 * DT + n * DT + 1)
                if n == 2:
                    dve.wait_ge(proj_done, x_over_proj(L, 0))
                dve.tensor_scalar(x_hi[:, 0, :], h[:, 0, :], cur[:, g:g + 1], None, ALU.mult).then_inc(x0_hi, 1)
                x_low(0)
                step(2)
                for i in range(2, DT + 1):
                    if i + 1 < DT:
                        step(i + 1)
                    x_low(i - 1)
                    if i == 4:
                        if n == 3:
                            dve.wait_ge(w_lo, v_half(L + 1, "f1_up", 0, 2) + 4)
                        split(*nxt, 3)
                    if 3 <= i < 3 + EARLY_ADDS:
                        add_square(L, pre, i - 3, None, CHASE_SQ[i - 3])
                for m in range(EARLY_ADDS, DT):
                    add_square(L, pre, m, None, CHASE_SQ[m % len(CHASE_SQ)])

            def keep_norm(L, n, pre, ph):
                split(L, ph, 1, 0)
                invert(L, pre)
                split(L, ph, 1, 1)
                dve.wait_ge(rb_ready, L * 4 + n + 1)

            def move(out, bank):
                dve.tensor_tensor(out, ps[:, bank, 0:T], rb[:, :], ALU.mult).then_inc(moved, 1)

            def up_step(L, ph, which, nxt, pair, prev_pair, banks, split_from=0):
                for j in range(4):
                    g = j // 2
                    dve.wait_ge(halves_done, v_half(L, ph, prev_pair, j) + 4)
                    if j % 2 == 0:
                        dve.wait_ge(mid_ready, L * 2 * FT + which * FT + 2 * prev_pair + g + 1)
                    move((ga, gb)[j % 2][:, g, :], banks[j])
                    if j >= split_from:
                        split(L, nxt, pair, j)

            def down_step(L, nxt, pair, prev_pair, name, last=False):
                for j in range(4):
                    if j >= 2:
                        add_square(L, name, 2 * prev_pair + j % 2, j % 2)
                    if j < 3 or not last:
                        split(L, nxt, pair, j)

            def ffn(L, up, dn, after, which, name):
                up_step(L, up, which, up, 1, 0, FIRST_BANKS, split_from=2)
                if up == "f1_up":
                    dve.wait_ge(pw_hi_ready, L * 2 + 2)
                    dve.tensor_tensor(p_lo[:, :], p_raw, p_hi[:, :].bitcast(F32), ALU.subtract).then_inc(pw_split, 1)
                    dve.tensor_tensor(pw_lo[:, :], pw_raw, pw_hi[:, :].bitcast(F32), ALU.subtract).then_inc(pw_split, 1)
                with dve.Fori(2, PAIRS[up]) as i:
                    up_step(L, up, which, up, i, i - 1, range(4))
                up_step(L, up, which, dn, 0, PAIRS[up] - 1, range(4))
                if up == "f2_up":
                    dve.wait_ge(proj_hi_ready, L + 1)
                    dve.tensor_tensor(proj_lo, proj_raw, proj_hi.bitcast(F32), ALU.subtract).then_inc(proj_split, 1)
                down_step(L, dn, 1, 0, name)
                with dve.Fori(2, PAIRS[dn]) as i:
                    down_step(L, dn, i, i - 1, name)
                down_step(L, after, 0, PAIRS[dn] - 1, name, last=True)

            def gate_step(L, ph, group, pair, nxt, sname, m0, banks=range(4), taps=(), short=False):
                for j in range(4):
                    dve.wait_ge(halves_done, v_half(L, ph, pair, j) + 4)
                    dve.wait_ge(sig, v_sig(L, sname, m0 + j - 2))
                    move(ga[:, j % 2, :], banks[j])
                    split(L, *nxt, j)
                    if short:
                        short_gate(L, j)
                    if j < len(taps):
                        long_taps(L, taps[j])

            todo = iter(TAPS)

            def long_taps(L, n):
                for _ in range(n):
                    k, t = next(todo)
                    c = COL["cf_conv"] + k * WT + t
                    if k == 0:
                        dve.wait_ge(glu_ready, L * WT + t + 1)
                    for i in range(2):
                        src, dst = part(i, cbuf, CH, t, k), tok(i, cc[:, t, :])
                        if k == 0:
                            b = COL["cf_conv_b"] + t
                            dve.tensor_scalar(dst, src, cur[:, c:c + 1], cur[:, b:b + 1], ALU.mult, ALU.add).then_inc(tap, 1)
                        else:
                            dve.wait_ge(tap, L * NTAP + 2 * TAP_AT[k - 1, t] + i + 1)
                            dve.scalar_tensor_tensor(dst, src, cur[:, c:c + 1], dst, ALU.mult, ALU.add).then_inc(tap, 1)

            NC3 = (2 * SK + 1) * WT

            def short_conv(L, t):
                dve.wait_ge(cv_ready, L * WT + t + 1)
                for k in range(SK):
                    c = COL["sc_conv"] + k * WT + t
                    for i in range(2):
                        src, dst = part(i, sbuf, SH, t, k), tok(i, f[:, t, :])
                        if k == 0:
                            dve.tensor_scalar(dst, src, cur[:, c:c + 1], None, ALU.mult).then_inc(c3, 1)
                        else:
                            dve.wait_ge(c3, L * NC3 + 2 * SK * t + 2 * (k - 1) + i + 1)
                            dve.scalar_tensor_tensor(dst, src, cur[:, c:c + 1], dst, ALU.mult, ALU.add).then_inc(c3, 1)

            def short_gate(L, t):
                dve.wait_ge(c3, L * NC3 + 2 * SK * (t + 1))
                dve.wait_ge(moved, v_moved(L, "bgate", t))
                dve.tensor_tensor(f[:, t, :], f[:, t, :], bg[:, t, :], ALU.mult).then_inc(c3, 1)

            dve.memset(ssq[:, T:TPAD], 0.0).then_inc(w_lo, 4)
            dve.memset(ones[:, :], 1.0).then_inc(moved, 4)
            dve.memset(meanw[:, :], 1.0 / W).then_inc(const_ready, 1)
            dve.memset(eps[:, 0:1], EPS).then_inc(const_ready, 1)
            dve.memset(eps[:, 1:2], 4 * EPS).then_inc(const_ready, 1)
            for m in range(DT):
                if m == 0:
                    dve.wait_ge(loaded, 32)
                if m == DT // 2:
                    for j in range(4):
                        split(0, "f1_up", 0, j)
                    dve.wait_ge(loaded_rest, 16)
                dve.wait_ge(xhi_ready, m + 1)
                dve.scalar_tensor_tensor(x_lo[:, m, :], h[:, m, :], pars[:, FIRST_G + m:FIRST_G + m + 1],
                                         x_hi[:, m, :].bitcast(F32), ALU.mult, ALU.subtract).then_inc(x_ready, 1)
                add_square(0, None, m, m % 2)
            with dve.Fori(0, DEPTH) as L:
                dve.wait_ge(x_ready, L * NX + DT)
                dve.tensor_copy(cur[:, :], pars[:, bass.ds(L * NCOL, NCOL)]).then_inc(par_ready, 1)
                dve.wait_ge(par_ready, L + 1)
                keep_norm(L, 0, None, "f1_up")
                ffn(L, "f1_up", "f1_dn", "glu", 0, "post1")
                boundary(L, 0, "b1", "post1", "pre1", "g_mix_pre", (L, "glu", 0))
                keep_norm(L, 1, "pre1", "glu")
                for n, (ph, pair, nxt) in enumerate([("glu", 0, ("glu", 1)), ("glu", 1, ("short", 0)),
                                                     ("short", 0, ("short", 1)), ("short", 1, ("pool", 0))]):
                    for j in range(4):
                        dve.wait_ge(halves_done, v_half(L, ph, pair, j) + 4)
                        if j % 2 == 0 and n > 0:
                            dve.wait_ge(glu_ready if n < 3 else cv_ready, L * WT + (2 * n - 2 if n < 3 else 0) + j // 2 + 1)
                        move((ga, gb)[j % 2][:, j // 2, :], FIRST_BANKS[j] if n == 0 else j)
                        if n or j >= 2:
                            split(L, *nxt, j)
                        if n >= 1:
                            long_taps(L, 3 if n > 1 else (1, 3, 3, 3)[j])
                dve.wait_ge(hist_in, L * 6 + 6)
                for j in range(4):
                    dve.wait_ge(halves_done, v_half(L, "pool", 0, j) + 4)
                    dve.tensor_tensor(part(0, abuf, AH, j, AH), prompt(ps[:, j, 0:T]), prompt(rb), ALU.mult)
                    dve.tensor_tensor(part(1, abuf, AH, j, AH), sample(ps[:, j, 0:T]), sample(rb), ALU.mult).then_inc(moved, 1)
                    split(L, "bgate", 0, j)
                    long_taps(L, 3)
                for j in range(4):
                    dve.wait_ge(halves_done, v_half(L, "bgate", 0, j) + 4)
                    move(bg[:, j, :], j)
                    split(L, "gate0", 0, j)
                    short_conv(L, j)
                    long_taps(L, 1)
                gate_step(L, "gate0", "gate0", 0, ("gate0", 1), "gate0", 0, taps=(2, 1, 2, 1), short=True)
                gate_step(L, "gate0", "gate0", 1, ("out0", 0), "gate0", 4, taps=(2, 2, 2, 2))
                dve.wait_ge(yb_ready, L * WT + WT)
                for j in range(4):
                    dve.wait_ge(halves_done, v_half(L, "out0", 0, j) + 4)
                    for m in (2 * j, 2 * j + 1):
                        dve.wait_ge(sig, v_sig(L, "gate0", m))
                        dve.tensor_tensor(f[:, m, :], ps[:, m % 4, 0:T], gate[:, m, :], ALU.mult).then_inc(moved, 1)
                    split(L, "gate1", 0, j)
                    long_taps(L, 2)
                gate_step(L, "gate1", "gate1", 0, ("gate1", 1), "gate1", 0, taps=(3, 3, 2, 1))
                for j in range(4):
                    dve.wait_ge(halves_done, v_half(L, "gate1", 1, j) + 4)
                    dve.wait_ge(sig, v_sig(L, "gate1", 4 + j - 2))
                    move(ga[:, j % 2, :], j)
                    split(L, "out1", 0, j)
                    if j == 1:
                        for g in range(WT):
                            dve.wait_ge(ya_hi, L * WT + g + 1)
                            c = COL["pool_scale"] + g
                            dve.scalar_tensor_tensor(y0_lo[:, g, :], ps[:, POOLW_BANKS[g], 0:T], cur[:, c:c + 1],
                                                     y0_hi[:, g, :].bitcast(F32), ALU.mult, ALU.subtract).then_inc(moved, 1)
                    long_taps(L, (4, 3, 3, 3)[j])

                def add_branch(b, nxt, xlo):
                    for j in range(4):
                        if xlo and j:
                            x_of_sum(2 * j - 2)
                            x_of_sum(2 * j - 1)
                        dve.wait_ge(halves_done, v_half(L, f"out{b}", 0, j) + 4)
                        for m in (2 * j, 2 * j + 1):
                            dve.wait_ge(sig, v_sig(L, f"gate{b}", m))
                            n = (b - 1) * DT + m
                            if n >= 2:
                                dve.wait_ge(added, L * 2 * DT + n - 1)
                            dve.tensor_tensor(gb[:, m % 2, :], ps[:, m % 4, 0:T], gate[:, m, :], ALU.mult).then_inc(moved, 1)
                        if xlo and j == 3:
                            x_of_sum(DT - 2)
                            x_of_sum(DT - 1)
                        split(L, *nxt, j)

                def x_of_sum(m):
                    dve.wait_ge(xhi_ready, v_xhi(L, "m", m))
                    dve.tensor_tensor(x_lo[:, m, :], f[:, m, :], x_hi[:, m, :].bitcast(F32), ALU.subtract).then_inc(x_ready, 1)

                add_branch(1, ("gate2", 0), False)
                dve.wait_ge(ln_mean, L + 1)
                for t in range(WT):
                    dve.tensor_tensor(cc[:, t, :], cc[:, t, :], bc, ALU.subtract).then_inc(ln_step, 1)
                for j in range(4):
                    if j == 3:
                        invert(L, "ln")
                    dve.wait_ge(halves_done, v_half(L, "gate2", 0, j) + 4)
                    dve.wait_ge(sig, v_sig(L, "gate2", j - 2))
                    move(ga[:, j % 2, :], j)
                    split(L, "gate2", 1, j)
                    if j < 2:
                        add_square(L, "ln", 2 * j, 0)
                        add_square(L, "ln", 2 * j + 1, 1)
                dve.wait_ge(bc_full, v_stat(L, "ln"))
                for t in range(WT):
                    dve.tensor_tensor(cc[:, t, :], cc[:, t, :], bc, ALU.mult).then_inc(ln_step, 1)
                for t in range(WT):
                    dve.wait_ge(ln_sig, L * WT + t + 1)
                    g, b = COL["cf_ln_g"] + t, COL["cf_ln_b"] + t
                    dve.tensor_scalar(cc[:, t, :], cc[:, t, :], cur[:, g:g + 1], cur[:, b:b + 1], ALU.mult, ALU.add).then_inc(ln_step, 1)
                for t in (0, 2):
                    dve.wait_ge(ln_step, L * 3 * WT + 2 * WT + t + 1)
                    dve.tensor_tensor(cc[:, t, :], cc[:, t, :], sg[:, t, :], ALU.mult).then_inc(silu_even, 1)
                for j in range(4):
                    dve.wait_ge(halves_done, v_half(L, "gate2", 1, j) + 4)
                    dve.wait_ge(sig, v_sig(L, "gate2", 4 + j - 2))
                    move(ga[:, j % 2, :], j)
                    split(L, "out2", 0, j)
                    if j == 0:
                        for t in (0, 2):
                            dve.wait_ge(yc_hi, L * WT + t // 2 + 1)
                            dve.tensor_tensor(y1_lo[:, t, :], cc[:, t, :], y1_hi[:, t, :].bitcast(F32), ALU.subtract).then_inc(yc_even, 1)
                add_branch(2, ("wo", 0), True)
                for pair, nxt in ((0, ("wo", 1)), (1, ("f2_up", 0))):
                    for j in range(4):
                        add_square(L, "post2", 4 * pair + j, j % 2)
                        if pair == 0 or j < 3:
                            split(L, *nxt, j)
                boundary(L, 1, "b2", "post2", "pre2", "g_f2_pre", (L, "f2_up", 0))
                keep_norm(L, 2, "pre2", "f2_up")
                ffn(L, "f2_up", "f2_dn", "pg", 1, "post3")
                boundary(L, 2, "b3", "post3", "pre3", "g_ple_pre", (L, "pg", 0))
                keep_norm(L, 3, "pre3", "pg")

                def embed(m):
                    dve.wait_ge(sig, v_sig(L, "pg", m))
                    dve.tensor_tensor(gate[:, m, :], gate[:, m, :], sg[:, m % RING3, :], ALU.mult).then_inc(ple_out, 1)

                for m in range(DT):
                    pair, j = divmod(m, 4)
                    dve.wait_ge(halves_done, v_half(L, "pg", pair, j) + 4)
                    if m >= 2:
                        dve.wait_ge(sig, v_sig(L, "pg", m - 2))
                    move(ga[:, m % 2, :], (FIRST_BANKS if pair == 0 else range(4))[j])
                    if m >= 1:
                        embed(m - 1)
                    if m >= 2:
                        add_square(L, "post4", m - 2, m % 2)
                    if pair == 0 and j >= 2:
                        split(L, "pg", 1, j)
                embed(DT - 1)
                for m in (DT - 2, DT - 1):
                    add_square(L, "post4", m, m % 2)
                boundary(L, 3, "b4", "post4", "pre4", "g_next", (L + 1, "f1_up", 0))
            invert(DEPTH, None)
            dve.wait_ge(rb_ready, DEPTH * 4 + 1)
            for m in range(DT):
                c = COL["g_next"] + m
                dve.scalar_tensor_tensor(f[:, m, :], h[:, m, :], cur[:, c:c + 1], rb[:, :], ALU.mult, ALU.mult).then_inc(y_ready, 1)

        @block.gpsimd
        def _(pool):
            def wait_alone(s, value):
                pool.wait_ge(s, value)
                pool.sem_inc(tick, 1)

            def update_h(L, n):
                for m in range(1, DT):
                    pool.wait_ge(step_t, L * 4 * DT + n * DT + m + 1)
                    pool.tensor_tensor(h[:, m, :], h[:, m, :], STEP[m % len(STEP)], ALU.add).then_inc(h_ready, 1)

            def hidden(L, ph, which, pair):
                for g in range(2):
                    m = 2 * pair + g
                    n = (L * 2 * FT + which * FT + m) * 3
                    pool.wait_ge(moved, v_moved(L, ph, 4 * pair + 2 * g + 1))
                    pool.tensor_tensor(gb[:, g, :], ga[:, g, :], gb[:, g, :], ALU.mult).then_inc(swi, 1)
                    pool.wait_ge(swi, n + 1)
                    pool.wait_ge(sig, v_sig(L, "f1" if which == 0 else "f2", m))
                    pool.tensor_tensor(gb[:, g, :], gb[:, g, :], sg[:, g, :], ALU.mult).then_inc(swi, 1)
                    wait_alone(swi, n + 2)
                    hi, lo = mid_hi[:, bass.ds(m, 1), :], mid_lo[:, bass.ds(m, 1), :]
                    pool.tensor_copy(hi, gb[:, g:g + 1, :]).then_inc(swi, 1)
                    pool.wait_ge(swi, n + 3)
                    pool.tensor_tensor(lo, gb[:, g:g + 1, :], hi.bitcast(F32), ALU.subtract).then_inc(mid_ready, 1)

            NPS = sum(g + 1 + 3 + 1 + 1 for g in range(WT))
            steps = [sum(k + 1 + 5 for k in range(g)) for g in range(WT)]

            tap_of_3 = iter(range(1, CK))

            def add3(L, n=1):
                for _ in range(n):
                    k = next(tap_of_3)
                    pool.wait_ge(prod3, L * (CK - 1) + k)
                    if k == 1:
                        pool.wait_ge(tap, L * NTAP + 2 * TAP_AT[0, 3] + 2)
                    else:
                        pool.wait_ge(tap3, L * (CK - 1) + k - 1)
                    pool.tensor_tensor(cc[:, 3, :], cc[:, 3, :], sg[:, k % RING3, :], ALU.add).then_inc(tap3, 1)

            def pooling(L, g):
                n = L * NPS + steps[g]
                w, wide = 2 << g, padded(AH)
                src, s = abuf[:, g, :], 0
                pool.wait_ge(moved, v_moved(L, "pool", g))
                for k in range(g + 1):
                    a, d = 2 * (1 << k) - 1, 1 << k
                    dst = win[:, k % 2, :]
                    pool.tensor_tensor(dst[:, a:wide], src[:, a:wide], src[:, a - d:wide - d], ALU.add).then_inc(pstep, 1)
                    s += 1
                    if k:
                        add3(L)
                    pool.wait_ge(pstep, n + s)
                    src = dst
                c = COUNTS + g * AH
                pool.tensor_tensor(src[:, AH:AH + w - 1], src[:, AH:AH + w - 1], pars[:, c:c + w - 1], ALU.mult).then_inc(pstep, 1)
                s += 1
                wait_alone(pstep, n + s)
                pool.tensor_scalar(src[:, AH:wide], src[:, AH:wide], 1.0 / w, None, ALU.mult).then_inc(pstep, 1)
                s += 1
                pool.wait_ge(pstep, n + s)
                a = abuf[:, g, :]
                pool.tensor_tensor(prompt(pmf), pad_prompt(src, AH, AH), pad_prompt(a, AH, AH), ALU.subtract).then_inc(pstep, 1)
                pool.tensor_tensor(sample(pmf), pad_sample(src, AH, AH), pad_sample(a, AH, AH), ALU.subtract).then_inc(pstep, 1)
                s += 2
                add3(L)
                wait_alone(pstep, n + s)
                pool.tensor_copy(y1_hi[:, g, :], pmf[:, :]).then_inc(pstep, 1)
                s += 1
                pool.wait_ge(pstep, n + s)
                pool.tensor_tensor(y1_lo[:, g, :], pmf[:, :], y1_hi[:, g, :].bitcast(F32), ALU.subtract).then_inc(pm_ready, 1)
                pool.wait_ge(pm_ready, L * WT + g + 1)

            pool.memset(ident[:, :], 0.0).then_inc(const_ready, 1)
            pool.memset(ga[:, 0, :], 0.0).then_inc(mid_ready, 2)
            pool.memset(ga[:, 1, :], 0.0).then_inc(halves_done, 4)
            pool.memset(gb[:, 1, :], 0.0).then_inc(stored, 16)
            pool.memset(sg[:, 1, :], 0.0).then_inc(f_out, 2)
            pool.memset(sg[:, 0, :], 0.0).then_inc(pw_split, 2)
            pool.wait_ge(const_ready, 4)
            pool.affine_select(out=ident[:, :], in_=ident[:, :], compare_op=ALU.not_equal, fill=1.0, base=0,
                               pattern=[[-1, P]], channel_multiplier=1).then_inc(const_ready, 1)
            pool.wait_ge(const_ready, 5)
            pool.memset(gb[:, 0, :], 0.0).then_inc(const_ready, 1)
            with pool.Fori(0, DEPTH) as L:
                with pool.Fori(0, PAIRS["f1_up"]) as i:
                    hidden(L, "f1_up", 0, i)
                update_h(L, 0)
                wait_alone(side_in, L * 16 + 16)
                at = 0
                for buf, k in ((cbuf, CH), (sbuf, SH), (abuf, AH)):
                    pool.memset(buf[:, :, 0:k], 0.0).then_inc(hist_in, 1)
                    for t in range(WT):
                        cp = pool.tensor_copy(pad_sample(buf[:, t, :], k, 0, k),
                                              hist[:, at:at + NSEQ * k].rearrange("p (s r) -> p s r", r=k))
                        at += NSEQ * k
                    cp.then_inc(hist_in, 1)
                for t in range(WT):
                    pool.wait_ge(sig, v_sig(L, "glu", t))
                    for view in (0, 1):
                        dst = pad_sample(cbuf[:, t, :], CH, CH) if view else pad_prompt(cbuf[:, t, :], CH, CH)
                        pick = sample if view else prompt
                        op = pool.tensor_tensor(dst, pick(ga[:, t % 2, :]), pick(sg[:, t % 2, :]), ALU.mult)
                    op.then_inc(glu_ready, 1)
                for t in range(WT):
                    pool.wait_ge(moved, v_moved(L, "short", 2 * t + 1))
                    for view in (0, 1):
                        dst = pad_sample(sbuf[:, t, :], SH, SH) if view else pad_prompt(sbuf[:, t, :], SH, SH)
                        pick = sample if view else prompt
                        op = pool.tensor_tensor(dst, pick(ga[:, t % 2, :]), pick(gb[:, t % 2, :]), ALU.mult)
                    op.then_inc(cv_ready, 1)
                    add3(L, 2)
                pooling(L, 0)
                pooling(L, 1)
                pooling(L, 2)
                for t in range(WT):
                    wait_alone(c3, L * (2 * SK + 1) * WT + 2 * SK * WT + t + 1)
                    pool.tensor_copy(y0_hi[:, t, :], f[:, t, :]).then_inc(yb_step, 1)
                    pool.wait_ge(yb_step, L * WT + t + 1)
                    pool.tensor_tensor(y0_lo[:, t, :], f[:, t, :], y0_hi[:, t, :].bitcast(F32), ALU.subtract).then_inc(yb_ready, 1)
                    add3(L)
                pooling(L, 3)
                wait_alone(hist_in, L * 6 + 6)
                at = 0
                for buf, k in ((cbuf, CH), (sbuf, SH), (abuf, AH)):
                    n = WT * k
                    pool.tensor_copy(hist[:, at:at + n].rearrange("p (t r) -> p t r", r=k),
                                     buf[:, :, SEQ:SEQ + k]).then_inc(staged, 1)
                    at += n
                    for t in range(WT):
                        cp = pool.tensor_copy(hist[:, at:at + NSEQ * k].rearrange("p (s r) -> p s r", r=k),
                                              pad_sample(buf[:, t, :], k, SLEN, k))
                        at += NSEQ * k
                    cp.then_inc(staged, 1)
                    add3(L, 2)
                add3(L, 2)
                def add_branch(b):
                    for m in range(DT):
                        pool.wait_ge(moved, v_moved(L, f"out{b}", m))
                        if b == 2:
                            pool.wait_ge(added, L * 2 * DT + m + 1)
                        pool.tensor_tensor(f[:, m, :], f[:, m, :], gb[:, m % 2, :], ALU.add).then_inc(added, 1)

                for t in range(1, WT):
                    if t == 1:
                        pool.wait_ge(tap, (L + 1) * NTAP)
                        pool.wait_ge(tap3, (L + 1) * (CK - 1))
                    else:
                        pool.wait_ge(ln_sum, L * (WT - 1) + t - 1)
                    pool.tensor_tensor(pmf[:, :], cc[:, 0, :] if t == 1 else pmf[:, :], cc[:, t, :], ALU.add).then_inc(ln_sum, 1)
                add_branch(1)
                for t in (1, 3):
                    pool.wait_ge(ln_step, L * 3 * WT + 2 * WT + t + 1)
                    pool.tensor_tensor(cc[:, t, :], cc[:, t, :], sg[:, t, :], ALU.mult).then_inc(silu_odd, 1)
                for t in (1, 3):
                    pool.wait_ge(yc_hi, L * WT + 2 + t // 2 + 1)
                    pool.tensor_tensor(y1_lo[:, t, :], cc[:, t, :], y1_hi[:, t, :].bitcast(F32), ALU.subtract).then_inc(yc_odd, 1)
                add_branch(2)
                update_h(L, 1)
                with pool.Fori(0, PAIRS["f2_up"]) as i:
                    hidden(L, "f2_up", 1, i)
                update_h(L, 2)
                wait_alone(w_lo, v_half(L, "pg", 1, 3) + 4)
                for j in range(3):
                    pool.wait_ge(w_hi, v_half(L + 1, "f1_up", 0, j))
                    n = HALF["f1_up"]
                    pool.tensor_tensor(w_lo_sb[:, j, 0:n], raw[:, j, 0:n], w_hi_sb[:, j, 0:n].bitcast(F32),
                                       ALU.subtract).then_inc(w_lo, 1)
                update_h(L, 3)


def _tiles(w, rows, cols):
    w = w.reshape(*w.shape[:-2], rows, P, cols, P)
    return w.swapaxes(-3, -2)


def _slots(halves):
    import numpy as np
    d, n, t = halves.shape[:3]
    a = halves.reshape(d, n // 2, 2, t, P, P).transpose(0, 1, 4, 2, 3, 5)
    return np.ascontiguousarray(a.reshape(d * (n // 2), P, 2 * t * P))


def _layout(i):
    import numpy as np
    i = {k: np.asarray(v) for k, v in i.items()}
    st = {}
    for n in ("1", "2"):
        g = _tiles(i[f"w_f{n}_gate"], DT, FT).swapaxes(1, 2)
        u = _tiles(i[f"w_f{n}_up"], DT, FT).swapaxes(1, 2)
        st[f"f{n}_up"] = _slots(np.stack([g, u], 2).reshape(DEPTH, 2 * FT, DT, P, P))
        d = _tiles(i[f"w_f{n}_down"], FT, DT).swapaxes(1, 2)
        d = d.reshape(DEPTH, DT // 2, 2, 2, FT // 2, P, P).swapaxes(2, 3)
        st[f"f{n}_dn"] = _slots(d.reshape(DEPTH, 2 * DT, FT // 2, P, P))
    z = _tiles(i["w_in"], DT, 6 * WT + 3 * DT).swapaxes(1, 2)
    blk = lambda n: z[:, n * WT:(n + 1) * WT]
    pairs = lambda a, b: np.stack([a, b], 2).reshape(DEPTH, 2 * WT, DT, P, P)
    gate = lambda n: z[:, 6 * WT + n * DT:6 * WT + (n + 1) * DT]
    st["glu"], st["short"] = _slots(pairs(blk(4), blk(5))), _slots(pairs(blk(1), blk(3)))
    st["pool"], st["bgate"] = _slots(blk(0)), _slots(blk(2))
    for n, (b, w) in enumerate(((1, "w_sc_out"), (0, "w_pool_out"), (2, "w_cf_out"))):
        st[f"gate{n}"] = _slots(gate(b))
        o = _tiles(i[w], WT, DT)
        o = o.reshape(DEPTH, WT, 4, 2, P, P).transpose(0, 2, 1, 3, 4, 5)
        st[f"out{n}"] = _slots(o.reshape(DEPTH, 4, 2 * WT, P, P))
    st["wo"] = _slots(_tiles(i["w_o"], DT, DT).swapaxes(1, 2))
    st["pg"] = _slots(_tiles(i["w_ple_gate"], DT, DT).swapaxes(1, 2))
    o = _tiles(i["w_ple_proj"], PT, DT).reshape(DEPTH, PT, 4, 2, P, P).transpose(0, 2, 1, 3, 4, 5)
    proj = o.reshape(DEPTH, 4, 2 * PT, P, P).transpose(0, 3, 1, 2, 4).reshape(DEPTH, P, -1)

    def cols(a):
        return a.reshape(-1, P).T

    nxt = np.concatenate([i["g_f1_pre"][1:], i["g_final"][None]])
    blocks = []
    for l in range(DEPTH):
        src = dict({n: i[n][l] for n, _ in _COLS if n != "g_next"}, g_next=nxt[l])
        blocks += [cols(src[n]) for n, _ in _COLS]
    blocks.append(cols(i["g_f1_pre"][0]))
    table = np.zeros((WT, AH), np.float32)
    for g in range(WT):
        for t in range((2 << g) - 1):
            table[g, t] = (2 << g) / (t + 1)
    blocks.append(np.broadcast_to(table.reshape(1, -1), (P, WT * AH)))
    par = np.concatenate(blocks, 1)

    def feature_major(prompt, sample, k):
        a = np.concatenate([prompt.reshape(SEQ, -1), sample.reshape(NSEQ * SLEN, -1)])
        return a.T.reshape(k, P, T).transpose(1, 0, 2).reshape(P, k * T)

    x = feature_major(i["x_prompt"], i["x_sample"], DT)
    p = np.stack([feature_major(i["p_prompt"][l], i["p_sample"][l], PT) for l in range(DEPTH)])
    side = []
    for n in ("state_cconv", "state_sconv", "state_pool"):
        s = i[n]
        s = s.reshape(DEPTH, NSEQ, s.shape[2], WT, P).transpose(0, 4, 3, 1, 2)
        side.append(s.reshape(DEPTH, P, -1))
    side = np.concatenate(side, 2)
    pw = i["pool_w"].transpose(0, 2, 1, 3).reshape(DEPTH, P, WT * P)
    arrays = dict(x=x, par=par, side=side, early=np.concatenate([p, pw], 2), proj=proj, **{f"w_{k}": v for k, v in st.items()})
    return {f"in_{k}": np.ascontiguousarray(v) for k, v in arrays.items()}


def kernel(**inputs):
    import numpy as np
    import concourse.bacc as bacc
    from concourse.bass_utils import run_bass_kernel_spmd as run

    arrays = _layout(inputs)
    nc = bacc.Bacc("TRN2", target_bir_lowering=False, num_devices=1)
    a = {n: nc.dram_tensor(n, v.shape, F32, kind="ExternalInput").ap() for n, v in arrays.items()}
    y = nc.dram_tensor("out_y", (P, DT * T), F32, kind="ExternalOutput").ap()
    states = nc.dram_tensor("out_states", (DEPTH, P, sum(STATES)), F32, kind="ExternalOutput").ap()
    trunk(nc, a["in_x"], a["in_par"], a["in_side"], a["in_early"], a["in_proj"],
          {n: a[f"in_w_{n}"] for n, _, _ in PHASES}, y, states)
    r = run(nc, [arrays], core_ids=[0]).results[0]

    yt = r["out_y"].reshape(P, DT, T).transpose(2, 1, 0).reshape(T, D)
    got = [yt[:SEQ].reshape(1, SEQ, D), yt[SEQ:].reshape(NSEQ, SLEN, D)]
    s, at, new = r["out_states"], 0, {}
    for name, k in (("c", CH), ("s", SH), ("a", AH)):
        n = WT * k
        new[name, 0] = s[:, :, at:at + n].reshape(DEPTH, P, WT, k).transpose(0, 3, 2, 1).reshape(DEPTH, 1, k, W)
        at += n
        n = WT * NSEQ * k
        new[name, 1] = s[:, :, at:at + n].reshape(DEPTH, P, WT, NSEQ, k).transpose(0, 3, 4, 2, 1).reshape(DEPTH, NSEQ, k, W)
        at += n
    got += [new[n, i] for i in range(2) for n in "asc"]
    return tuple(np.ascontiguousarray(g) for g in got)
```
